# Optimizing a Trainium2 kernel written in Bass

```python
import math
import jax
import jax.numpy as jnp
from jax import lax
import numpy as np

D_MODEL = 1024
BATCH = 1
SEQ = 128
DEPTH = 1
DEC_BATCH = 1
DEC_SEQ = 512
PAST_LEN = 128

F32 = jnp.float32
GRID_W = 64
D_MIX = 512
A_HEADS = 8
A_HD = 64
A_LORA_W = 64
A_LORA_A = 64
A_LORA_G = 128
B_HEADS = 8
B_HD = 64
WIN_R = 8
WIN_C = 16
C_GROUP = 16
C_GROUPS = D_MIX // C_GROUP
C_STATE = 64
N_EXPERTS = 64
TOP_K = 8
N_GROUPS = 8
TOPK_GROUPS = 4
D_EXPERT = 128
D_SHARED = 128
ROUTED_SCALE = 2.5
LN_EPS = 1e-5
GN_EPS = 64e-5
NEG = -1e30
Q_BLOCK = 128
DN_ALPHA = (2 * DEPTH) ** 0.25
DN_BETA = (8 * DEPTH) ** -0.25
A_COLS = 3 * D_MIX + 2 * A_LORA_W + 2 * A_LORA_A + A_LORA_G
IN_COLS = A_COLS + 3 * D_MIX + D_MIX + 3 * D_MODEL

kernel_name = 'hybrid_rwkv7_natten_s5_moe_diffusion_step'

def split_cols(z, sizes):
    return jnp.split(z, [int(i) for i in np.cumsum(sizes)[:-1]], axis=-1)

def layer_norm(x, g, b):
    xf = x.astype(F32)
    mu = jnp.mean(xf, axis=-1, keepdims=True)
    var = jnp.mean(jnp.square(xf - mu), axis=-1, keepdims=True)
    return ((xf - mu) * lax.rsqrt(var + LN_EPS) * g + b).astype(x.dtype)

def modulation(cond, w_ada, b_ada):
    m = jax.nn.silu(cond) @ w_ada + b_ada
    return jnp.split(m[:, None, :], 6, axis=-1)

def token_shift_mix(z, mu):
    zp = jnp.pad(z, ((0, 0), (1, 1), (0, 0)))
    return z + mu * (0.5 * (zp[:, :-2] + zp[:, 2:]) - z)

def mixer_inputs(h, p):
    z = h @ p['w_in']
    za, zq, zk, zv, zu, zg = split_cols(z, [A_COLS, D_MIX, D_MIX, D_MIX, D_MIX, 3 * D_MODEL])
    return token_shift_mix(za, p['rwkv_mu']), zq, zk, zv, zu, zg

def rwkv_prep(za, p):
    bsz, t = za.shape[:2]
    r, k, v, lw, la, lg = split_cols(za.astype(F32), [D_MIX, D_MIX, D_MIX, 2 * A_LORA_W, 2 * A_LORA_A, A_LORA_G])
    lw = lw.reshape(bsz, t, 2, A_LORA_W)
    la = la.reshape(bsz, t, 2, A_LORA_A)
    w = p['rwkv_w0'] + jnp.einsum('btnr,nrc->btnc', jnp.tanh(lw), p['rwkv_w2'])
    decay = jnp.exp(-jnp.exp(-jax.nn.softplus(-w) - 0.5))
    a = jax.nn.sigmoid(p['rwkv_a0'] + jnp.einsum('btnr,nrc->btnc', la, p['rwkv_a2']))
    g = jax.nn.sigmoid(lg) @ p['rwkv_g2']
    kk = (k * p['rwkv_kk']).reshape(bsz, t, A_HEADS, A_HD)
    kk = kk / jnp.maximum(jnp.linalg.norm(kk, axis=-1, keepdims=True), 1e-12)
    k_dir = k[:, :, None, :] * (1.0 + (a - 1.0) * p['rwkv_ka'])

    def to_heads(y):
        return y.reshape(y.shape[:-1] + (A_HEADS, A_HD))
    return (to_heads(r), to_heads(decay), to_heads(k_dir), to_heads(v),
            kk, kk[:, :, None] * to_heads(a), g)

def rwkv_scan(r, w, k, v, kk, b, s0, reverse):
    def step(s, inp):
        r_t, w_t, k_t, v_t, kk_t, b_t = inp
        sa = jnp.einsum('bhvk,bhk->bhv', s, kk_t)
        s = s * w_t[:, :, None, :] - sa[..., None] * b_t[:, :, None, :] + v_t[..., None] * k_t[:, :, None, :]
        return s, jnp.einsum('bhvk,bhk->bhv', s, r_t)
    xs = tuple(jnp.moveaxis(y, 1, 0) for y in (r, w, k, v, kk, b))
    s_fin, y = lax.scan(step, s0, xs, reverse=reverse)
    return jnp.moveaxis(y, 0, 1), s_fin

def rwkv_branch(za, p, s0):
    bsz, t = za.shape[:2]
    r, decay, k_dir, v, kk, b_dir, g = rwkv_prep(za, p)
    s0 = s0.astype(F32)
    y_f, s_f = rwkv_scan(r, decay[:, :, 0], k_dir[:, :, 0], v, kk, b_dir[:, :, 0], s0[:, 0], False)
    y_b, s_b = rwkv_scan(r, decay[:, :, 1], k_dir[:, :, 1], v, kk, b_dir[:, :, 1], s0[:, 1], True)
    y = jnp.stack([y_f, y_b], axis=2)
    mu = jnp.mean(y, axis=-1, keepdims=True)
    var = jnp.mean(jnp.square(y - mu), axis=-1, keepdims=True)
    gn = (y - mu) * lax.rsqrt(var + GN_EPS) * p['rwkv_gn_g'].reshape(A_HEADS, A_HD) + p['rwkv_gn_b'].reshape(A_HEADS, A_HD)
    bonus = jnp.sum(r[:, :, None] * k_dir * p['rwkv_rk'].reshape(A_HEADS, A_HD), axis=-1, keepdims=True) * v[:, :, None]
    out = jnp.sum(gn + bonus, axis=2).reshape(bsz, t, D_MIX) * g
    return out, jnp.stack([s_f, s_b], axis=1)

def linear_scan(a, b):
    a_seq = jnp.broadcast_to(a, b.shape)

    def combine(e1, e2):
        return e1[0] * e2[0], e2[0] * e1[1] + e2[1]
    return lax.associative_scan(combine, (a_seq, b), axis=1)[1]

def s5_branch(u, p, x0):
    bsz, t = u.shape[:2]
    a = lax.complex(p['s5_a_re'].astype(F32), p['s5_a_im'].astype(F32))
    dt = jnp.exp(p['s5_log_dt'].astype(F32))[..., None]
    a_bar = jnp.exp(dt * a)
    b_mat = lax.complex(p['s5_b_re'].astype(F32), p['s5_b_im'].astype(F32))
    b_bar = ((a_bar - 1.0) / a)[..., None] * b_mat
    c_mat = lax.complex(p['s5_c_re'].astype(F32), p['s5_c_im'].astype(F32))
    uf = u.astype(F32)
    ug = uf.reshape(bsz, t, C_GROUPS, C_GROUP).astype(jnp.complex64)
    bu = jnp.einsum('btgh,ngph->nbtgp', ug, b_bar)
    bu_f = bu[0].at[:, 0].add(a_bar[0] * x0[:, 0])
    bu_b = bu[1].at[:, -1].add(a_bar[1] * x0[:, 1])
    x_f = linear_scan(a_bar[0], bu_f)
    x_b = jnp.flip(linear_scan(a_bar[1], jnp.flip(bu_b, axis=1)), axis=1)
    y = jnp.einsum('btgp,ghp->btgh', x_f + x_b, c_mat).real.reshape(bsz, t, D_MIX) + p['s5_d'] * uf
    y = jax.nn.gelu(y)
    y = y * jax.nn.sigmoid(y @ p['s5_w_glu'] + p['s5_b_glu'])
    return y, jnp.stack([x_f[:, -1], x_b[:, 0]], axis=1)

def attn_heads(z):
    bsz, t = z.shape[:2]
    return z.reshape(bsz, t, B_HEADS, B_HD).transpose(0, 2, 1, 3)

def merge_heads(y):
    bsz, nh, t, hd = y.shape
    return y.transpose(0, 2, 1, 3).reshape(bsz, t, nh * hd)

def context_attention(q, k, v):
    bsz, nh, n, hd = q.shape
    qb = q.reshape(bsz, nh, n // Q_BLOCK, Q_BLOCK, hd).transpose(2, 0, 1, 3, 4)

    def block(qi):
        s = jnp.einsum('bhqd,bhkd->bhqk', qi, k).astype(F32) * hd ** -0.5
        return jnp.einsum('bhqk,bhkd->bhqd', jax.nn.softmax(s, axis=-1).astype(v.dtype), v)
    out = lax.map(block, qb)
    return out.transpose(1, 2, 0, 3, 4).reshape(bsz, nh, n, hd)

def na_latent(zq, zk, zv, k_ctx, v_ctx, rpb):
    bsz, t = zq.shape[:2]
    rows = t // GRID_W
    wr = min(WIN_R, rows)

    def to_grid(y):
        return y.reshape(bsz, rows, GRID_W, B_HEADS, B_HD).transpose(0, 3, 1, 2, 4)
    qg, kg, vg = to_grid(zq), to_grid(zk), to_grid(zv)
    cq = np.arange(GRID_W)[:, None]
    ck = np.arange(GRID_W)[None, :]
    cs = np.clip(cq - WIN_C // 2, 0, GRID_W - WIN_C)
    col_bias = np.where((ck >= cs) & (ck < cs + WIN_C), 0.0, NEG).astype(np.float32)
    col_idx = np.clip(ck - cq + WIN_C - 1, 0, 2 * WIN_C - 2)
    rpb_col = rpb.astype(F32)[:, :, col_idx]
    scale = B_HD ** -0.5
    n_loc = wr * GRID_W

    def row_block(r):
        rs = jnp.clip(r - wr // 2, 0, rows - wr)
        kb = lax.dynamic_slice_in_dim(kg, rs, wr, axis=2)
        vb = lax.dynamic_slice_in_dim(vg, rs, wr, axis=2)
        qr = lax.dynamic_index_in_dim(qg, r, axis=2, keepdims=False)
        row_idx = rs + jnp.arange(wr) - r + WIN_R - 1
        bias = jnp.take(rpb_col, row_idx, axis=1).transpose(0, 2, 1, 3) + col_bias[:, None, :]
        s_loc = jnp.einsum('bhqd,bhjkd->bhqjk', qr, kb).astype(F32) * scale + bias
        s_ctx = jnp.einsum('bhqd,bhld->bhql', qr, k_ctx).astype(F32) * scale
        prob = jax.nn.softmax(jnp.concatenate([s_loc.reshape(bsz, B_HEADS, GRID_W, n_loc), s_ctx], axis=-1), axis=-1)
        p_loc = prob[..., :n_loc].reshape(bsz, B_HEADS, GRID_W, wr, GRID_W).astype(vb.dtype)
        p_ctx = prob[..., n_loc:].astype(v_ctx.dtype)
        return (jnp.einsum('bhqjk,bhjkd->bhqd', p_loc, vb)
                + jnp.einsum('bhql,bhld->bhqd', p_ctx, v_ctx))
    out = lax.map(row_block, jnp.arange(rows))
    return out.transpose(1, 0, 3, 2, 4).reshape(bsz, t, B_HEADS * B_HD)

def merge_branches(y_a, y_b, y_c, zg, p):
    y = jnp.stack([y_a, y_b, y_c], axis=2)
    gates = jax.nn.sigmoid(zg.astype(F32)).reshape(zg.shape[:2] + (3, D_MODEL))
    merged = jnp.sum(jnp.einsum('btnc,ncd->btnd', y, p['w_branch']) * gates, axis=2)
    return merged @ p['w_out']

def moe_ffn(h, p):
    shape = h.shape
    x = h.reshape(-1, D_MODEL)
    n = x.shape[0]
    scores = jax.nn.sigmoid((x @ p['router_w']).astype(F32))
    sel = scores + p['router_bias'].astype(F32)
    grp_score = jnp.sum(lax.top_k(sel.reshape(n, N_GROUPS, N_EXPERTS // N_GROUPS), 2)[0], axis=-1)
    _, gidx = lax.top_k(grp_score, TOPK_GROUPS)
    gmask = jnp.sum(jax.nn.one_hot(gidx, N_GROUPS, dtype=F32), axis=1)
    sel = jnp.where(jnp.repeat(gmask, N_EXPERTS // N_GROUPS, axis=1) > 0, sel, NEG)
    _, eidx = lax.top_k(sel, TOP_K)
    w = jnp.take_along_axis(scores, eidx, axis=1)
    w = ROUTED_SCALE * w / jnp.sum(w, axis=-1, keepdims=True)
    gates = jnp.sum(jax.nn.one_hot(eidx, N_EXPERTS, dtype=F32) * w[..., None], axis=1)
    hg = jnp.einsum('nd,edf->nef', x, p['exp_w_gate'])
    hu = jnp.einsum('nd,edf->nef', x, p['exp_w_up'])
    y = jnp.einsum('nef,efd->nd', jax.nn.silu(hg) * hu * gates[..., None].astype(hg.dtype), p['exp_w_down'])
    y_sh = (jax.nn.silu(x @ p['sh_w_gate']) * (x @ p['sh_w_up'])) @ p['sh_w_down']
    return (y + y_sh).reshape(shape)

def context_layer(x, mod, p):
    shift1, scale1, gate1, shift2, scale2, gate2 = mod
    bsz = x.shape[0]
    h = x * (1.0 + scale1) + shift1
    za, zq, zk, zv, zu, zg = mixer_inputs(h, p)
    y_a, s_rwkv = rwkv_branch(za, p, jnp.zeros((bsz, 2, A_HEADS, A_HD, A_HD), F32))
    k_h, v_h = attn_heads(zk), attn_heads(zv)
    y_b = merge_heads(context_attention(attn_heads(zq), k_h, v_h))
    y_c, s_s5 = s5_branch(zu, p, jnp.zeros((bsz, 2, C_GROUPS, C_STATE), jnp.complex64))
    x = layer_norm(DN_ALPHA * x + gate1 * merge_branches(y_a, y_b, y_c, zg, p), p['ln1_g'], p['ln1_b'])
    h = x * (1.0 + scale2) + shift2
    x = layer_norm(DN_ALPHA * x + gate2 * moe_ffn(h, p), p['ln2_g'], p['ln2_b'])
    return x, k_h, v_h, s_rwkv, s_s5

def latent_layer(x, mod, p, k_ctx, v_ctx, s_rwkv, s5_x0):
    shift1, scale1, gate1, shift2, scale2, gate2 = mod
    h = x * (1.0 + scale1) + shift1
    za, zq, zk, zv, zu, zg = mixer_inputs(h, p)
    y_a, _ = rwkv_branch(za, p, s_rwkv)
    y_b = na_latent(zq, zk, zv, k_ctx, v_ctx, p['na_rpb'])
    y_c, _ = s5_branch(zu, p, s5_x0)
    x = layer_norm(DN_ALPHA * x + gate1 * merge_branches(y_a, y_b, y_c, zg, p), p['ln1_g'], p['ln1_b'])
    h = x * (1.0 + scale2) + shift2
    x = layer_norm(DN_ALPHA * x + gate2 * moe_ffn(h, p), p['ln2_g'], p['ln2_b'])
    return x

def setup_inputs(seed: int = 0) -> dict:
    key = jax.random.key(seed)
    ks = iter(jax.random.split(key, 64))

    def nrm(shape, scale):
        return scale * jax.random.normal(next(ks), shape, F32)

    def unif(shape, lo, hi):
        return jax.random.uniform(next(ks), shape, F32, lo, hi)
    L = DEPTH
    col_scale = np.ones((IN_COLS,), np.float32)
    col_scale[2 * D_MIX:3 * D_MIX] = DN_BETA
    col_scale[A_COLS + 2 * D_MIX:A_COLS + 3 * D_MIX] = DN_BETA
    a_im0 = np.pi * np.arange(C_STATE, dtype=np.float32)
    return {
        'x_prompt': nrm((BATCH, SEQ, D_MODEL), 1.0),
        'x_sample': nrm((DEC_BATCH, DEC_SEQ, D_MODEL), 1.0),
        'c': nrm((DEC_BATCH, D_MODEL), 1.0),
        'cache_na_k': nrm((DEC_BATCH, DEPTH, B_HEADS, PAST_LEN, B_HD), 1.0),
        'cache_na_v': nrm((DEC_BATCH, DEPTH, B_HEADS, PAST_LEN, B_HD), 1.0),
        'state_rwkv': nrm((DEC_BATCH, DEPTH, 2, A_HEADS, A_HD, A_HD), 0.5),
        'state_s5_re': nrm((DEC_BATCH, DEPTH, 2, C_GROUPS, C_STATE), 0.5),
        'state_s5_im': nrm((DEC_BATCH, DEPTH, 2, C_GROUPS, C_STATE), 0.5),
        'c_ctx': nrm((D_MODEL,), 1.0),
        'w_ada': nrm((L, D_MODEL, 6 * D_MODEL), D_MODEL ** -0.5),
        'b_ada': nrm((L, 6 * D_MODEL), 0.1),
        'w_in': nrm((L, D_MODEL, IN_COLS), D_MODEL ** -0.5) * col_scale,
        'rwkv_mu': unif((L, A_COLS), 0.0, 1.0),
        'rwkv_w0': unif((L, 2, D_MIX), -5.0, 1.0),
        'rwkv_w2': nrm((L, 2, A_LORA_W, D_MIX), 0.1 * A_LORA_W ** -0.5),
        'rwkv_a0': nrm((L, 2, D_MIX), 0.5),
        'rwkv_a2': nrm((L, 2, A_LORA_A, D_MIX), A_LORA_A ** -0.5),
        'rwkv_g2': nrm((L, A_LORA_G, D_MIX), A_LORA_G ** -0.5),
        'rwkv_kk': 0.85 + nrm((L, D_MIX), 0.05),
        'rwkv_ka': 1.0 + nrm((L, D_MIX), 0.05),
        'rwkv_rk': nrm((L, D_MIX), 0.1),
        'rwkv_gn_g': 1.0 + nrm((L, D_MIX), 0.05),
        'rwkv_gn_b': nrm((L, D_MIX), 0.02),
        'na_rpb': nrm((L, B_HEADS, 2 * WIN_R - 1, 2 * WIN_C - 1), 0.1),
        's5_a_re': -0.5 + nrm((L, 2, C_GROUPS, C_STATE), 0.01),
        's5_a_im': a_im0 + nrm((L, 2, C_GROUPS, C_STATE), 0.01),
        's5_log_dt': unif((L, 2, C_GROUPS), math.log(1e-3), math.log(1e-1)),
        's5_b_re': nrm((L, C_GROUPS, C_STATE, C_GROUP), (2 * C_GROUP) ** -0.5),
        's5_b_im': nrm((L, C_GROUPS, C_STATE, C_GROUP), (2 * C_GROUP) ** -0.5),
        's5_c_re': nrm((L, C_GROUPS, C_GROUP, C_STATE), (2 * C_STATE) ** -0.5),
        's5_c_im': nrm((L, C_GROUPS, C_GROUP, C_STATE), (2 * C_STATE) ** -0.5),
        's5_d': nrm((L, D_MIX), 1.0),
        's5_w_glu': nrm((L, D_MIX, D_MIX), D_MIX ** -0.5),
        's5_b_glu': nrm((L, D_MIX), 0.02),
        'w_branch': nrm((L, 3, D_MIX, D_MODEL), D_MIX ** -0.5),
        'w_out': nrm((L, D_MODEL, D_MODEL), DN_BETA * D_MODEL ** -0.5),
        'ln1_g': 1.0 + nrm((L, D_MODEL), 0.05),
        'ln1_b': nrm((L, D_MODEL), 0.02),
        'router_w': nrm((L, D_MODEL, N_EXPERTS), D_MODEL ** -0.5),
        'router_bias': nrm((L, N_EXPERTS), 0.01),
        'exp_w_gate': nrm((L, N_EXPERTS, D_MODEL, D_EXPERT), D_MODEL ** -0.5),
        'exp_w_up': nrm((L, N_EXPERTS, D_MODEL, D_EXPERT), D_MODEL ** -0.5),
        'exp_w_down': nrm((L, N_EXPERTS, D_EXPERT, D_MODEL), DN_BETA * D_EXPERT ** -0.5),
        'sh_w_gate': nrm((L, D_MODEL, D_SHARED), D_MODEL ** -0.5),
        'sh_w_up': nrm((L, D_MODEL, D_SHARED), D_MODEL ** -0.5),
        'sh_w_down': nrm((L, D_SHARED, D_MODEL), DN_BETA * D_SHARED ** -0.5),
        'ln2_g': 1.0 + nrm((L, D_MODEL), 0.05),
        'ln2_b': nrm((L, D_MODEL), 0.02),
    }

def reference(x_prompt, x_sample, c, cache_na_k, cache_na_v, state_rwkv, state_s5_re, state_s5_im,
              c_ctx, w_ada, b_ada, w_in, rwkv_mu, rwkv_w0, rwkv_w2, rwkv_a0, rwkv_a2, rwkv_g2,
              rwkv_kk, rwkv_ka, rwkv_rk, rwkv_gn_g, rwkv_gn_b, na_rpb, s5_a_re, s5_a_im, s5_log_dt,
              s5_b_re, s5_b_im, s5_c_re, s5_c_im, s5_d, s5_w_glu, s5_b_glu, w_branch, w_out,
              ln1_g, ln1_b, router_w, router_bias, exp_w_gate, exp_w_up, exp_w_down,
              sh_w_gate, sh_w_up, sh_w_down, ln2_g, ln2_b):
    stacked = {
        'w_ada': w_ada, 'b_ada': b_ada, 'w_in': w_in, 'rwkv_mu': rwkv_mu, 'rwkv_w0': rwkv_w0,
        'rwkv_w2': rwkv_w2, 'rwkv_a0': rwkv_a0, 'rwkv_a2': rwkv_a2, 'rwkv_g2': rwkv_g2,
        'rwkv_kk': rwkv_kk, 'rwkv_ka': rwkv_ka, 'rwkv_rk': rwkv_rk, 'rwkv_gn_g': rwkv_gn_g,
        'rwkv_gn_b': rwkv_gn_b, 'na_rpb': na_rpb, 's5_a_re': s5_a_re, 's5_a_im': s5_a_im,
        's5_log_dt': s5_log_dt, 's5_b_re': s5_b_re, 's5_b_im': s5_b_im, 's5_c_re': s5_c_re,
        's5_c_im': s5_c_im, 's5_d': s5_d, 's5_w_glu': s5_w_glu, 's5_b_glu': s5_b_glu,
        'w_branch': w_branch, 'w_out': w_out, 'ln1_g': ln1_g, 'ln1_b': ln1_b,
        'router_w': router_w, 'router_bias': router_bias, 'exp_w_gate': exp_w_gate,
        'exp_w_up': exp_w_up, 'exp_w_down': exp_w_down, 'sh_w_gate': sh_w_gate,
        'sh_w_up': sh_w_up, 'sh_w_down': sh_w_down, 'ln2_g': ln2_g, 'ln2_b': ln2_b,
    }
    xp, xs = x_prompt, x_sample
    new_k, new_v, new_rwkv, new_s5 = [], [], [], []
    for l in range(DEPTH):
        p = {name: arr[l] for name, arr in stacked.items()}
        xp, k_h, v_h, s_rwkv, s_s5 = context_layer(xp, modulation(c_ctx[None, :], p['w_ada'], p['b_ada']), p)
        new_k.append(k_h)
        new_v.append(v_h)
        new_rwkv.append(s_rwkv)
        new_s5.append(s_s5)
        s5_x0 = lax.complex(state_s5_re[:, l].astype(F32), state_s5_im[:, l].astype(F32))
        xs = latent_layer(xs, modulation(c, p['w_ada'], p['b_ada']), p,
                          cache_na_k[:, l], cache_na_v[:, l], state_rwkv[:, l], s5_x0)
    s5_all = jnp.stack(new_s5, axis=1)
    return (xp, xs, jnp.stack(new_k, axis=1), jnp.stack(new_v, axis=1), jnp.stack(new_rwkv, axis=1),
            s5_all.real, s5_all.imag)


_drawn_inputs = setup_inputs


def setup_inputs(seed=0):
    import zlib

    import numpy as np

    out = dict(_drawn_inputs(seed))
    spreads = {}
    factors = {'rwkv_w2': 3.028,
     'rwkv_gn_b': 4.059,
     'na_rpb': 6.26,
     's5_a_re': 4.362,
     's5_b_glu': 5.644,
     'ln2_b': 2.906}
    for name, (base, spread) in spreads.items():
        noise = np.random.default_rng([zlib.crc32(name.encode()), seed]).standard_normal(out[name].shape)
        drawn = base * np.exp(spread * noise) if base else spread * noise
        out[name] = jnp.asarray(drawn.astype(out[name].dtype))
    for name, factor in factors.items():
        out[name] = (out[name] * factor).astype(out[name].dtype)
    return out
```

```python
from contextlib import ExitStack

import concourse.bass as bass
from concourse import mybir
from concourse.alu_op_type import AluOpType as ALU

F32 = mybir.dt.float32
I32 = mybir.dt.int32
U32 = mybir.dt.uint32
ACT = mybir.ActivationFunctionType
AX = mybir.AxisListType
ds = bass.ds

P = 128
D = 1024
KT = D // P
TS, TP = 512, 128
N = TS + TP
NT = N // P
MIX = 512
MT = MIX // P
HEADS, HD = 8, 64
ACOLS = 3 * MIX + 2 * 64 + 2 * 64 + 128
RT = ACOLS // P
QCOL, KCOL, VCOL, UCOL, GCOL = ACOLS, ACOLS + MIX, ACOLS + 2 * MIX, ACOLS + 3 * MIX, ACOLS + 4 * MIX
GRID_W, WIN_C, WIN_R = 64, 16, 8
GRID_H = TS // GRID_W
NDR, NDC = 2 * WIN_R - 1, 2 * WIN_C - 1
NEG = -1e30
ALPHA = 2.0 ** 0.25
LN_EPS, GN_EPS = 1e-5, 64e-5
E_N, E_F, TOPK = 64, 128, 8
EGROUPS, TOPG = 8, 4
ROUTED_SCALE = 2.5
ZS, ZP = 1, 515
ZW = 644
DECAY_C = 0.6065306597126334
PCOLS = {"c": (0, 8), "c_ctx": (8, 8), "rwkv_mu": (16, 15), "rwkv_w0": (31, 8), "rwkv_a0": (39, 8), "rwkv_kk": (47, 4),
         "rwkv_ka": (51, 4), "rwkv_rk": (55, 4), "s5_d": (59, 4), "s5_b_glu": (63, 4)}
NPCOL = 67
SHIFT1, SCALE1, GATE1, SHIFT2, SCALE2, GATE2 = range(6)


class Chain:

    def __init__(self, eng, sem, base=0):
        self.eng, self.sem, self.base, self.n = eng, sem, base, 0

    def __call__(self, ins):
        self.n += 1
        ins.then_inc(self.sem, 1)
        self.eng.wait_ge(self.sem, self.base + self.n)


class Mem:
    pass


def sems(nc, m, names):
    new = [nc.alloc_semaphore(name) for name in names.split()]
    m.phase_sems += new
    return new


def clear_sems(nc, m):
    nc.clear_and_free_semaphores(m.phase_sems)
    m.phase_sems = []
    nc.all_engine_barrier()


def ada_block(nc, m, j, slot, land, used, n):
    nc.tensor.wait_ge(land, n)
    for k in range(KT):
        last = nc.tensor.matmul(m.ps_mod[0:2, slot, :], m.c_silu[:, k, :], m.w_ada_sb[:, slot, k, :],
                                start=(k == 0), stop=(k == KT - 1))
    last.then_inc(m.s_mod_mm, 1)


def setup_phase(nc, m, a):
    with ExitStack() as ctx:
        x_sb = m.z[:].rearrange("p t c -> p (t c)")[:, 0:NT * D].rearrange("p (t d) -> p t d", t=NT)
        prow = ctx.enter_context(nc.sbuf_tensor("prow", [NPCOL, P], F32))
        ps_mod = ctx.enter_context(nc.psum_tensor("ps_mod0", [P, 2, 512], F32))
        ps_x = ctx.enter_context(nc.psum_tensor("ps_x", [P, 2, 512], F32))
        ps_xp = ctx.enter_context(nc.psum_tensor("ps_xp", [P, 2, 512], F32))
        ps_mt = ctx.enter_context(nc.psum_tensor("ps_mt", [P, 512], F32))
        m.ps_mod = ps_mod
        (m.s_x, m.s_c, m.s_b_ada, m.s_wa0, m.s_wa1, m.s_mod_mm, m.s_mod_sb, m.s_ident, m.s_silu, m.s_xt_mm,
         m.s_xt_sb, m.s_modt_mm, m.s_dve_a, m.s_h_spill, m.s_ht, m.s_pcol, m.s_pcol_mm) = sems(
            nc, m, "s_x s_c s_b_ada s_wa0 s_wa1 s_mod_mm s_mod_sb s_ident s_silu s_xt_mm s_xt_sb s_modt_mm s_dve_a s_h_spill "
            "s_ht s_pcol s_pcol_mm")
        w_ada = a["w_ada"].rearrange("(k p) n -> p k n", p=P)
        land = [m.s_wa0, m.s_wa1]
        with nc.Block() as block:

            @block.sync
            def _(sp):
                for j in range(4):
                    if j >= 2:
                        sp.wait_ge(m.s_mod_mm, j - 1)
                    sp.dma_start(m.w_ada_sb[:, j % 2], w_ada[:, :, ts512(j)]).then_inc(land[j % 2], 16)
                for t in range(2):
                    sp.dma_start(m.w_in_sb[:, t], a["w_in_t"][:, :, t * P:(t + 1) * P]).then_inc(m.s_win[t], 16)
                sp.wait_ge(m.s_ht, 8 * 2)
                sp.dma_start(m.h1_dram.rearrange("k p n -> p k n"), m.hT[:]).then_inc(m.s_h_spill, 16)
                sp.wait_ge(m.s_h_spill, 16)

            @block.scalar
            def _(act):
                for name, (c0, n) in PCOLS.items():
                    v = a[name]
                    v = v.rearrange("o n -> (o n)") if len(v.shape) == 2 else v
                    act.dma_start(prow[c0:c0 + n, :], v.rearrange("(k p) -> k p", p=P)).then_inc(m.s_c, 16)
                for t in range(NT - 1):
                    act.dma_start(x_sb[:, t], a["x_sample"][t * P:(t + 1) * P, :]).then_inc(m.s_x, 16)
                act.dma_start(x_sb[:, NT - 1], a["x_prompt"]).then_inc(m.s_x, 16)
                act.dma_start(m.mods[0:1], a["b_ada"].unsqueeze(0)).then_inc(m.s_b_ada, 16)
                act.dma_start(m.mods[1:2], a["b_ada"].unsqueeze(0)).then_inc(m.s_b_ada, 16)
                for t in range(2, 4):
                    act.dma_start(m.w_in_sb[:, t], a["w_in_t"][:, :, t * P:(t + 1) * P]).then_inc(m.s_win[t], 16)
                act.wait_ge(m.s_pcol, 1)
                nc.scalar.activation(m.c_silu[:], m.pcol[:, 0:2 * KT].rearrange("p (c k) -> p k c", c=2), ACT.Silu).then_inc(m.s_silu, 1)
                for k in range(KT):
                    act.wait_ge(m.s_xt_mm, k + 1)
                    nc.scalar.activation(m.hT[:, k, 0:TS], ps_x[:, k % 2, :], ACT.Identity)
                    nc.scalar.activation(m.hT[:, k, TS:N], ps_xp[:, k % 2, 0:TP],
                                         ACT.Identity).then_inc(m.s_xt_sb, 1)

            @block.gpsimd
            def _(pool):
                nc.gpsimd.memset(m.ident[:], 0.0).then_inc(m.s_ident, 1)
                pool.wait_ge(m.s_ident, 1)
                nc.gpsimd.affine_select(out=m.ident[:], in_=m.ident[:], compare_op=ALU.not_equal, fill=1.0, base=0,
                                        pattern=[[-1, P]], channel_multiplier=1).then_inc(m.s_ident, 1)

            @block.tensor
            def _(pe):
                pe.wait_ge(m.s_ident, 2)
                pe.wait_ge(m.s_c, 16 * len(PCOLS))
                nc.tensor.transpose(ps_mt[:, 128:128 + NPCOL], prow[:, :], m.ident[0:NPCOL, 0:NPCOL]).then_inc(m.s_pcol_mm, 1)
                pe.wait_ge(m.s_x, 16 * NT)
                for k in range(KT):
                    if k >= 2:
                        pe.wait_ge(m.s_xt_sb, k - 1)
                    for t in range(NT - 1):
                        nc.tensor.transpose(ps_x[:, k % 2, t * P:(t + 1) * P], x_sb[:, t, k * P:(k + 1) * P], m.ident[:])
                    nc.tensor.transpose(ps_xp[:, k % 2, 0:TP], x_sb[:, NT - 1, k * P:(k + 1) * P],
                                        m.ident[:]).then_inc(m.s_xt_mm, 1)
                pe.wait_ge(m.s_silu, 1)
                for j in range(4):
                    if j >= 2:
                        pe.wait_ge(m.s_mod_sb, j - 1)
                    ada_block(nc, m, j, j % 2, land[j % 2], m.s_mod_mm, 16 * (j // 2 + 1))
                pe.wait_ge(m.s_mod_sb, 4)
                for v in range(2):
                    for k in range(KT):
                        c0 = v * D + k * P
                        last = nc.tensor.transpose(ps_mt[:, (v * KT + k) * 2:(v * KT + k) * 2 + 2],
                                                   m.mods[0:2, c0:c0 + P], m.ident[0:2, 0:2])
                last.then_inc(m.s_modt_mm, 1)

            @block.vector
            def _(dve):
                dve.wait_ge(m.s_pcol_mm, 1)
                nc.vector.tensor_copy(m.pcol[:], ps_mt[:, 128:128 + NPCOL]).then_inc(m.s_pcol, 1)
                dve.wait_ge(m.s_b_ada, 32)
                for j in range(4):
                    dve.wait_ge(m.s_mod_mm, j + 1)
                    nc.vector.tensor_tensor(m.mods[0:2, ts512(j)], m.ps_mod[0:2, j % 2, :],
                                            m.mods[0:2, ts512(j)], ALU.add).then_inc(m.s_mod_sb, 1)
                link = Chain(dve, m.s_dve_a)
                dve.wait_ge(m.s_modt_mm, 1)
                pm = ps_mt[:, 0:4 * KT].rearrange("p (v k c) -> p v k c", v=2, c=2)
                nc.vector.tensor_copy(m.modT[:, 0], pm[:, 0])
                link(nc.vector.tensor_scalar_add(m.modT[:, 1], pm[:, 1], 1.0))
                for k in range(KT):
                    dve.wait_ge(m.s_xt_sb, k + 1)
                    for c, sl in ((0, slice(0, TS)), (1, slice(TS, N))):
                        nc.vector.tensor_scalar(m.hT[:, k, sl], m.hT[:, k, sl], m.modT[:, 1, k, c:c + 1],
                                                m.modT[:, 0, k, c:c + 1], ALU.mult, ALU.add).then_inc(m.s_ht, 1)


def ts512(j):
    return ds(j * 512, 512)


Z_TILES = RT + 3 * MT


def z_col(t):
    return t * P if t < RT + 2 * MT else t * P + MIX


def inproj_phase(nc, m, a):
    with ExitStack() as ctx:
        wv_sb = ctx.enter_context(nc.sbuf_tensor("wv_sb", [P, KT, MIX], F32))
        ps_s = ctx.enter_context(nc.psum_tensor("ps_s", [P, 2, 512], F32))
        ps_p = ctx.enter_context(nc.psum_tensor("ps_p", [P, 2, 512], F32))
        ps_v = ctx.enter_context(nc.psum_tensor("ps_v", [P, 1, 512], F32))
        ps_mod = ctx.enter_context(nc.psum_tensor("ps_mod1", [P, 2, 512], F32))
        ps_mt = ctx.enter_context(nc.psum_tensor("ps_mt2", [P, 64], F32))
        kp_sb = m.yb[:, 0, 0:MIX]
        m.ps_mod = ps_mod
        (m.s_z_mm, m.s_z_act, m.s_z_dve, m.s_wv, m.s_v_mm, m.s_v_sb, m.s_wb0, m.s_wb1, m.s_mod_mm2, m.s_mod_sb2,
         m.s_kp_mm, m.s_kp_sb, m.s_out_kv, m.s_mt2, m.s_modT2, m.s_spill_mod) = sems(
            nc, m, "s_z_mm s_z_act s_z_dve s_wv s_v_mm s_v_sb s_wb0 s_wb1 s_mod_mm2 s_mod_sb2 s_kp_mm s_kp_sb s_out_kv s_mt2 "
            "s_modT2 s_spill_mod")
        w_ada = a["w_ada"].rearrange("(k p) n -> p k n", p=P)
        land = [m.s_wb0, m.s_wb1]
        m.s_mod_mm = m.s_mod_mm2
        NB = 6

        def z_tile(t):
            return m.zr[:, t, :] if t < RT else m.z[:, t - RT, :]

        with nc.Block() as block:

            def load(eng, t, r, n):
                return eng.dma_start(m.w_in_sb[:, r], a["w_in_t"][:, :, ds(t * P, P)])

            @block.sync
            def _(sp):
                for t in range(0, 23 - 4):
                    sp.wait_ge(m.s_z_mm, t + 1)
                    sp.dma_start(m.w_in_sb[:, t % 4], a["w_in_t"][:, :, (t + 4) * P:(t + 5) * P]).then_inc(m.s_win[t % 4], 16)
                for t in range(19, 23):
                    sp.wait_ge(m.s_z_mm, t + 1)
                    c0 = z_col(t + 4)
                    sp.dma_start(m.w_in_sb[:, t % 4], a["w_in_t"][:, :, c0:c0 + P]).then_inc(m.s_win[t % 4], 16)

            @block.gpsimd
            def _(pool):
                pool.dma_start(wv_sb[:], a["w_in_t"][:, :, VCOL:VCOL + MIX]).then_inc(m.s_wv, 16)
                for j in range(4, 12):
                    if j >= 6:
                        pool.wait_ge(m.s_mod_mm2, j - 5)
                    pool.dma_start(m.w_ada_sb[:, j % 2], w_ada[:, :, ts512(j)]).then_inc(land[j % 2], 16)
                pool.wait_ge(m.s_kp_sb, 1)
                pool.dma_start(a["new_k"].rearrange("h t d -> t h d"),
                               kp_sb.rearrange("p (h d) -> p h d", h=HEADS)).then_inc(m.s_out_kv, 16)
                pool.wait_ge(m.s_v_sb, NT)
                pool.dma_start(a["new_v"].rearrange("h t d -> t h d"),
                               m.zv[:, NT - 1].rearrange("p (h d) -> p h d", h=HEADS)).then_inc(m.s_out_kv, 16)
                pool.wait_ge(m.s_mod_sb2, 8)
                pool.dma_start(m.mods_dram, m.mods[0:2]).then_inc(m.s_spill_mod, 16)
                pool.wait_ge(m.s_out_kv, 32)
                pool.wait_ge(m.s_spill_mod, 16)

            @block.tensor
            def _(pe):
                def tile(t, i):
                    r, b = t % 4, t % 2
                    pe.wait_ge(m.s_win[r], 16 * (t // 4 + 1))
                    if t >= 2:
                        pe.wait_ge(m.s_z_act, t - 1)
                        pe.wait_ge(m.s_z_dve, t - 1)
                    for k in range(KT):
                        nc.tensor.matmul(ps_s[:, b, :], m.w_in_sb[:, r, k, :], m.hT[:, k, 0:TS],
                                         start=(k == 0), stop=(k == KT - 1))
                    for k in range(KT):
                        last = nc.tensor.matmul(ps_p[:, b, 0:TP], m.w_in_sb[:, r, k, :], m.hT[:, k, TS:N],
                                                start=(k == 0), stop=(k == KT - 1))
                    last.then_inc(m.s_z_mm, 1)

                for t in range(Z_TILES):
                    tile(t, 0)
                pe.wait_ge(m.s_wv, 16)
                for t in range(NT):
                    if t >= 1:
                        pe.wait_ge(m.s_v_sb, t)
                    for k in range(KT):
                        last = nc.tensor.matmul(ps_v[:, 0, :], m.hT[:, k, t * P:(t + 1) * P], wv_sb[:, k, :],
                                                start=(k == 0), stop=(k == KT - 1))
                    last.then_inc(m.s_v_mm, 1)
                pe.wait_ge(m.s_z_dve, Z_TILES)
                for q in range(MT):
                    last = nc.tensor.transpose(ps_p[:, 0, q * P:(q + 1) * P], z_tile(RT + MT + q)[:, ZP:ZP + TP], m.ident[:])
                last.then_inc(m.s_kp_mm, 1)
                for j in range(4, 12):
                    if j >= 6:
                        pe.wait_ge(m.s_mod_sb2, j - 5)
                    ada_block(nc, m, j, j % 2, land[j % 2], None, 16 * (j // 2 - 1))
                pe.wait_ge(m.s_mod_sb2, 8)
                for v in range(2):
                    for k in range(KT):
                        c0 = (SHIFT2 + v) * D + k * P
                        last = nc.tensor.transpose(ps_mt[:, (v * KT + k) * 2:(v * KT + k) * 2 + 2],
                                                   m.mods[0:2, c0:c0 + P], m.ident[0:2, 0:2])
                last.then_inc(m.s_mt2, 1)

            @block.scalar
            def _(act):
                for t in range(Z_TILES):
                    act.wait_ge(m.s_z_mm, t + 1)
                    nc.scalar.activation(z_tile(t)[:, ZS:ZS + TS], ps_s[:, t % 2, :], ACT.Identity).then_inc(m.s_z_act, 1)
                for t in range(NT):
                    act.wait_ge(m.s_v_mm, t + 1)
                    nc.scalar.activation(m.zv[:, t], ps_v[:, 0, :], ACT.Identity).then_inc(m.s_v_sb, 1)
                act.wait_ge(m.s_kp_mm, 1)
                nc.scalar.activation(kp_sb, ps_p[:, 0, :], ACT.Identity).then_inc(m.s_kp_sb, 1)

            @block.vector
            def _(dve):
                for c0, c1 in ((0, ZS), (ZS + TS, ZP), (ZP + TP, ZW)):
                    nc.vector.memset(m.zr[:, 0:RT, c0:c1], 0.0)
                for t in range(Z_TILES):
                    dve.wait_ge(m.s_z_mm, t + 1)
                    nc.vector.tensor_copy(z_tile(t)[:, ZP:ZP + TP], ps_p[:, t % 2, 0:TP]).then_inc(m.s_z_dve, 1)
                for j in range(4, 12):
                    dve.wait_ge(m.s_mod_mm2, j - 3)
                    nc.vector.tensor_tensor(m.mods[0:2, ts512(j)], m.ps_mod[0:2, j % 2, :],
                                            m.mods[0:2, ts512(j)], ALU.add).then_inc(m.s_mod_sb2, 1)
                dve.wait_ge(m.s_mt2, 1)
                pm = ps_mt[:, 0:4 * KT].rearrange("p (v k c) -> p v k c", v=2, c=2)
                nc.vector.tensor_copy(m.modT[:, 2], pm[:, 0])
                nc.vector.tensor_scalar_add(m.modT[:, 3], pm[:, 1], 1.0).then_inc(m.s_modT2, 1)


def wait(eng, sem, v):
    if not isinstance(v, int) or v > 0:
        eng.wait_ge(sem, v)


ZQ, ZK, ZU = 0, MT, 2 * MT
NSLOT = NDR + 1


def attention_phase(nc, m, a):
    QT = TS // P
    SCALE = HD ** -0.5
    with ExitStack() as ctx:
        def sb(name, shape):
            return ctx.enter_context(nc.sbuf_tensor(name, shape, F32))

        def pb(name, shape):
            return ctx.enter_context(nc.psum_tensor(name, shape, F32))
        ck_sb = sb("ck_sb", [P, HEADS, HD])
        cv_sb = sb("cv_sb", [P, HEADS, HD])
        ckT = sb("ckT", [P, MT, P])
        rpb_in = sb("rpb_in", [HEADS * NDR, NDC])
        rpb_row = sb("rpb_row", [HEADS * NDR, 127])
        bias = sb("bias_tab", [P, HEADS, NSLOT, GRID_W])
        rev = sb("bias_rev", [GRID_W, HEADS, NDR, GRID_W])
        q_sb = sb("q_sb", [P, MT, P])
        s_sb = sb("s_sb", [P, 2, TS + P])
        p_sb = sb("p_sb", [P, 2, TS + P])
        pT_sb = sb("pT_sb", [P, 2, TS + P])
        nmax = sb("nmax", [P, 2])
        rsum = sb("rsum", [P, 2])
        rinv = sb("rinv", [P, 2])
        yb_sb = sb("yb_sb", [P, MIX])
        ps_s = pb("ps_as", [P, 2, TS])
        ps_c = pb("ps_ac", [P, 2, TS])[:, :, 0:P]
        ps_t5 = pb("ps_at5", [P, P])
        ps_t = pb("ps_at", [P, TS])
        ps_o = pb("ps_ao", [P, HD])
        ps_y = pb("ps_ay", [P, MT, P])
        rpb_dram = nc.dram_tensor("rpb_dram", [HEADS * NDR, 127], F32)
        (m.s_rpb, m.s_rpb0, m.s_rpbw, m.s_tab, m.s_tab_lo, m.s_tab_hi, m.s_ck, m.s_cv, m.s_ck_mm, m.s_ckT, m.s_q,
         m.s_sc, m.s_st, m.s_ex, m.s_tr, m.s_trA, m.s_trD, m.s_pv, m.s_o, m.s_rc, m.s_yt, m.s_yz, m.s_dve_b,
         m.s_pool_b) = sems(
            nc, m, "s_rpb s_rpb0 s_rpbw s_tab s_tab_lo s_tab_hi s_ck s_cv s_ck_mm s_ckT s_q s_sc s_st s_ex s_tr s_trA s_trD "
            "s_pv s_o s_rc s_yt s_yz s_dve_b s_pool_b")
        with nc.Block() as block:

            @block.sync
            def _(sp):
                sp.dma_start(ck_sb[:], a["cache_na_k"].rearrange("h t d -> t h d")).then_inc(m.s_ck, 16)
                sp.dma_start(rpb_in[:], a["na_rpb"]).then_inc(m.s_rpb, 16)
                sp.wait_ge(m.s_rpb0, 2)
                sp.dma_start(rpb_dram.ap(), rpb_row[:]).then_inc(m.s_rpbw, 16)
                sp.wait_ge(m.s_rpbw, 16)
                for h in range(HEADS):
                    src = bass.AP(rpb_dram, h * NDR * 127, [[1, GRID_W], [127, NDR], [1, GRID_W]])
                    sp.dma_start(rev[:, h], src).then_inc(m.s_tab, 16)
                sp.wait_ge(m.s_tab_lo, 1)
                sp.dma_start(bias[GRID_W:P, :, 1:NSLOT, :], bias[0:GRID_W, :, 0:NDR, :]).then_inc(m.s_tab_hi, 16)

            @block.gpsimd
            def _(pool):
                nc.gpsimd.memset(rpb_row[:], 0.0).then_inc(m.s_rpb0, 1)
                pool.wait_ge(m.s_rpb0, 1)
                pool.wait_ge(m.s_rpb, 16)
                nc.gpsimd.tensor_copy(rpb_row[:, 48:48 + NDC], rpb_in[:, ::-1]).then_inc(m.s_rpb0, 1)
                pool.dma_start(cv_sb[:], a["cache_na_v"].rearrange("h t d -> t h d")).then_inc(m.s_cv, 16)
                nc.gpsimd.tensor_copy(m.yc[:, :, 0:TS], m.z[:, ZU:ZU + MT, ZS:ZS + TS])
                nc.gpsimd.tensor_copy(m.yc[:, :, TS:N], m.z[:, ZU:ZU + MT, ZP:ZP + TP])
                pool.wait_ge(m.s_tab, 16 * HEADS)
                flat = rev[:].rearrange("p h r c -> p (h r) c")
                lo = flat[:, :, WIN_C:GRID_W]
                nc.gpsimd.affine_select(out=lo, in_=lo, compare_op=ALU.is_ge, fill=NEG, base=WIN_C // 2 + GRID_W - WIN_C - 1,
                                        pattern=[[0, HEADS * NDR], [-1, GRID_W - WIN_C]],
                                        channel_multiplier=-1).then_inc(m.s_pool_b, 1)
                pool.wait_ge(m.s_pool_b, 1)
                hi = flat[:, :, 0:GRID_W - WIN_C]
                nc.gpsimd.affine_select(out=hi, in_=hi, compare_op=ALU.is_ge, fill=NEG, base=WIN_C // 2 - GRID_W,
                                        pattern=[[0, HEADS * NDR], [1, GRID_W - WIN_C]],
                                        channel_multiplier=1).then_inc(m.s_pool_b, 1)

            def q_tile(i):
                return ZP if isinstance(i, int) and i == QT else ZS + i * P

            @block.tensor
            def _(pe):
                pe.wait_ge(m.s_ck, 16)
                for q in range(MT):
                    last = nc.tensor.transpose(ps_y[:, q, :], ck_sb[:, 2 * q:2 * q + 2, :].rearrange("p a d -> p (a d)"), m.ident[:])
                last.then_inc(m.s_ck_mm, 1)

                def scores(i, h):
                    n, b, hb, t = i * HEADS + h, h % 2, (h % 2) * HD, h // 2
                    wait(pe, m.s_st, n - 1)
                    q = q_sb[hb:hb + HD, t, :]
                    if not (isinstance(i, int) and i == QT):
                        nc.tensor.matmul(ps_s[:, b, :], q, m.z[hb:hb + HD, ZK + t, ZS:ZS + TS], start=True, stop=True)
                        nc.tensor.matmul(ps_c[:, b, :], q, ckT[hb:hb + HD, t, :], start=True, stop=True).then_inc(m.s_sc, 1)
                    else:
                        nc.tensor.matmul(ps_c[:, b, :], q, m.z[hb:hb + HD, ZK + t, ZP:ZP + TP],
                                         start=True, stop=True).then_inc(m.s_sc, 1)

                def turn(i, h):
                    n, b = i * HEADS + h, h % 2
                    pe.wait_ge(m.s_ex, n + 1)
                    wait(pe, m.s_trA, n)
                    wait(pe, m.s_trD, n)
                    if not (isinstance(i, int) and i == QT):
                        for k in range(4):
                            nc.tensor.transpose(ps_t[:, k * P:(k + 1) * P], p_sb[:, b, k * P:(k + 1) * P], m.ident[:])
                    nc.tensor.transpose(ps_t5[:], p_sb[:, b, TS:TS + P], m.ident[:]).then_inc(m.s_tr, 1)

                def pv(i, h):
                    n, b = i * HEADS + h, h % 2
                    pe.wait_ge(m.s_trA, n + 1)
                    pe.wait_ge(m.s_trD, n + 1)
                    wait(pe, m.s_o, n)
                    if not (isinstance(i, int) and i == QT):
                        for k in range(4):
                            nc.tensor.matmul(ps_o[:], pT_sb[:, b, k * P:(k + 1) * P], m.zv[:, k, h * HD:(h + 1) * HD],
                                             start=(k == 0), stop=False)
                        nc.tensor.matmul(ps_o[:], pT_sb[:, b, TS:TS + P], cv_sb[:, h, :],
                                         start=False, stop=True).then_inc(m.s_pv, 1)
                    else:
                        nc.tensor.matmul(ps_o[:], pT_sb[:, b, TS:TS + P], m.zv[:, QT, h * HD:(h + 1) * HD],
                                         start=True, stop=True).then_inc(m.s_pv, 1)

                def step(i):
                    pe.wait_ge(m.s_q, i + 1)
                    scores(i, 0)
                    scores(i, 1)
                    for h in range(HEADS):
                        turn(i, h)
                        if h + 2 < HEADS:
                            scores(i, h + 2)
                        if h:
                            pv(i, h - 1)
                    pv(i, HEADS - 1)
                    pe.wait_ge(m.s_o, HEADS * i + HEADS)
                    wait(pe, m.s_yz, i)
                    for t in range(MT):
                        last = nc.tensor.transpose(ps_y[:, t, :], yb_sb[:, t * P:(t + 1) * P], m.ident[:])
                    last.then_inc(m.s_yt, 1)
                pe.wait_ge(m.s_ckT, 1)
                pe.wait_ge(m.s_cv, 16)
                step(0)
                with pe.Fori(1, QT) as i:
                    step(i)
                step(QT)

            @block.vector
            def _(dve):
                link = Chain(dve, m.s_dve_b)
                dve.wait_ge(m.s_ck_mm, 1)
                nc.vector.tensor_copy(ckT[:], ps_y[:]).then_inc(m.s_ckT, 1)
                dve.wait_ge(m.s_pool_b, 2)
                nc.vector.tensor_copy(bias[0:GRID_W, :, 0:NDR, :], rev[:, :, :, ::-1]).then_inc(m.s_tab_lo, 1)

                def stage(i):
                    wait(dve, m.s_sc, HEADS * i)
                    nc.vector.tensor_scalar(q_sb[:], m.z[:, ZQ:ZQ + MT, ds(q_tile(i), P)], 1.0, None, ALU.mult).then_inc(m.s_q, 1)

                def soft(i, h, ctx_only):
                    n, b = i * HEADS + h, h % 2
                    dve.wait_ge(m.s_sc, n + 1)
                    wait(dve, m.s_ex, n - 1)
                    if not ctx_only:
                        tab = bias[:, h, ds(WIN_R - 1 - 2 * i, GRID_H), :]
                        nc.vector.scalar_tensor_tensor(s_sb[:, b, 0:TS], ps_s[:, b, :], SCALE,
                                                       tab.rearrange("p r c -> p (r c)"), ALU.mult, ALU.add)
                    link2(nc.vector.tensor_scalar(s_sb[:, b, TS:TS + P], ps_c[:, b, :], SCALE, None, ALU.mult), n)
                    src = s_sb[:, b, TS:TS + P] if ctx_only else s_sb[:, b, :]
                    nc.vector.tensor_reduce(nmax[:, b:b + 1], src, AX.X, ALU.max, negate=True).then_inc(m.s_st, 1)

                def link2(ins, n):
                    ins.then_inc(m.s_dve_b, 1)
                    dve.wait_ge(m.s_dve_b, n + 1)

                def rest(i, h):
                    n, b = i * HEADS + h, h % 2
                    dve.wait_ge(m.s_ex, n + 1)
                    wait(dve, m.s_o, n - 1)
                    nc.vector.reciprocal(rinv[:, b:b + 1], rsum[:, b:b + 1]).then_inc(m.s_rc, 1)
                    dve.wait_ge(m.s_tr, n + 1)
                    wait(dve, m.s_pv, n - 1)
                    nc.vector.tensor_copy(pT_sb[:, b, TS:TS + P], ps_t5[:]).then_inc(m.s_trD, 1)

                def step(i, ctx_only=False):
                    stage(i)
                    soft(i, 0, ctx_only)
                    for h in range(HEADS):
                        if h + 1 < HEADS:
                            soft(i, h + 1, ctx_only)
                        rest(i, h)
                    dve.wait_ge(m.s_yt, i + 1)
                    nc.vector.tensor_scalar(m.yb[:, :, ds(i * P, P)], ps_y[:], 1.0, None, ALU.mult).then_inc(m.s_yz, 1)
                dve.wait_ge(m.s_tab_hi, 16)
                step(0)
                with dve.Fori(1, QT) as i:
                    step(i)
                step(QT, True)

            @block.scalar
            def _(act):
                def soft(i, h, ctx_only):
                    n, b = i * HEADS + h, h % 2
                    act.wait_ge(m.s_st, n + 1)
                    wait(act, m.s_tr, n - 1)
                    wait(act, m.s_rc, n - 1)
                    sl = slice(TS, TS + P) if ctx_only else slice(0, TS + P)
                    nc.scalar.activation(p_sb[:, b, sl], s_sb[:, b, sl], ACT.Exp, bias=nmax[:, b:b + 1],
                                         accum_out=rsum[:, b:b + 1]).then_inc(m.s_ex, 1)

                def turned(i, h, ctx_only):
                    n, b = i * HEADS + h, h % 2
                    act.wait_ge(m.s_tr, n + 1)
                    wait(act, m.s_pv, n - 1)
                    if ctx_only:
                        act.sem_inc(m.s_trA, 1)
                    else:
                        nc.scalar.activation(pT_sb[:, b, 0:TS], ps_t[:], ACT.Identity).then_inc(m.s_trA, 1)

                def out(i, h):
                    n, b = i * HEADS + h, h % 2
                    act.wait_ge(m.s_pv, n + 1)
                    act.wait_ge(m.s_rc, n + 1)
                    if h == 0:
                        wait(act, m.s_yt, i)
                    nc.scalar.activation(yb_sb[:, h * HD:(h + 1) * HD], ps_o[:], ACT.Identity,
                                         scale=rinv[:, b:b + 1]).then_inc(m.s_o, 1)

                def step(i, ctx_only=False):
                    soft(i, 0, ctx_only)
                    for h in range(HEADS):
                        if h + 1 < HEADS:
                            soft(i, h + 1, ctx_only)
                        turned(i, h, ctx_only)
                        if h:
                            out(i, h - 1)
                    out(i, HEADS - 1)
                step(0)
                with act.Fori(1, QT) as i:
                    step(i)
                step(QT, True)


G_N, G_CH, G_ST = 32, 16, 64
GP = G_N // 2
CH = 8
NCS, NCP = TS // CH, TP // CH
NC = NCS + NCP
TWO_PI_HI, TWO_PI_LO = 6.28125, 0.0019353071795864769
ROUND = 12582912.0


def s5_phase(nc, m, a):
    with ExitStack() as whole, ExitStack() as ctx:
        def outer(name, shape):
            return whole.enter_context(nc.sbuf_tensor(name, shape, F32))

        def sb(name, shape):
            return ctx.enter_context(nc.sbuf_tensor(name, shape, F32))
        sel = outer("s5_sel", [P, CH, 240])
        atT = outer("s5_atT", [P, 2, 2, GP, P])
        tt_sb = outer("s5_tt", [P, G_N, P])
        vt = outer("s5_vt", [P, 2, 2, GP, CH, G_CH])
        pc = outer("s5_pc", [P, 4, 2, GP])
        a8 = outer("s5_a8", [P, 2, 2, 2, GP])
        rows = sb("s5_rows", [P, P])
        crow = sb("s5_crow", [P, 2, 2, P])
        dt_row = sb("s5_dt_row", [P, 2, GP, 2])
        dt = sb("s5_dt", [P, 2, GP])
        w = sb("s5_w", [P, 16, 2, GP])
        pw = sb("s5_pw", [P, 2, CH, 2, 2, GP])
        pt = sb("s5_pt", [P, 2, 4, 2, 2, GP])
        b_sb = sb("s5_b", [P, 2, GP, G_CH])
        bb = sb("s5_bb", [P, 2, 2, GP, G_CH])
        c_sb = sb("s5_c", [P, 2, GP, G_CH])
        at = sb("s5_at", [P, 2, 2, GP, CH, G_CH])
        tmp = sb("s5_tmp", [P, GP, 2, G_CH])
        (m.s_p5, m.s_p5b, m.s_p5_mm, m.s_p5c, m.s_c5_mm, m.s_d5, m.s_sin5, m.s_w5, m.s_sel5, m.s_msk5, m.s_pool5,
         m.s_at_mm, m.s_at_sb, m.s_t_mm, m.s_t_sb, m.s_u_mm, m.s_u_sb, m.s_zz_mm, m.s_zz_sb, m.s_x5, m.s_y5_mm,
         m.s_y5_sb, m.s_f5_mm, m.s_f5_sb, m.s_ge5, m.s_glu_mm, m.s_glu_sb, m.s_glu_w, m.s_out5, m.s_fin_mm,
         m.s_fin_sb, m.s_dve5, m.s_tab5, m.s_du5, m.s_sp5, m.s_yc5) = sems(
            nc, m, "s_p5 s_p5b s_p5_mm s_p5c s_c5_mm s_d5 s_sin5 s_w5 s_sel5 s_msk5 s_pool5 s_at_mm s_at_sb s_t_mm s_t_sb "
            "s_u_mm s_u_sb s_zz_mm s_zz_sb s_x5 s_y5_mm s_y5_sb s_f5_mm s_f5_sb s_ge5 s_glu_mm s_glu_sb s_glu_w s_out5 "
            "s_fin_mm s_fin_sb s_dve5 s_tab5 s_du5 s_sp5 s_yc5")
        ps_a = ctx.enter_context(nc.psum_tensor("ps_5a", [P, 2, 512], F32))
        with nc.Block() as block:

            @block.sync
            def _(sp):
                for n, name in enumerate(("s5_a_re", "s5_a_im", "state_s5_re", "state_s5_im")):
                    sp.dma_start(rows[32 * n:32 * n + 32, :],
                                 a[name].rearrange("d (j e) p -> (d j) (e p)", e=2)).then_inc(m.s_p5, 16)
                for c, name in enumerate(("s5_c_re", "s5_c_im")):
                    for j in range(GP):
                        sp.dma_start(crow[(j % 8) * G_CH:(j % 8 + 1) * G_CH, c, j // 8, :].rearrange("h (e p) -> h e p", e=2),
                                     a[name][2 * j:2 * j + 2].rearrange("e h p -> h e p")).then_inc(m.s_p5c, 16)

            @block.gpsimd
            def _(pool):
                pool.dma_start(dt_row[:], bass.AP(a["s5_log_dt"].tensor, 0, [[0, P], [1, 2 * G_N]])
                               .rearrange("p (d j e) -> p d j e", d=2, e=2)).then_inc(m.s_d5, 16)
                for c, name in enumerate(("s5_b_re", "s5_b_im")):
                    for e in range(2):
                        pool.dma_start(b_sb[e * G_ST:(e + 1) * G_ST, c],
                                       a[name].rearrange("(j e) p h -> e p j h", e=2)[e]).then_inc(m.s_p5b, 16)
                nc.gpsimd.memset(sel[:], 0.0).then_inc(m.s_pool5, 1)
                pool.wait_ge(m.s_pool5, 1)
                nc.gpsimd.affine_select(out=sel[:], in_=sel[:], compare_op=ALU.not_equal, fill=1.0, base=112,
                                        pattern=[[-16, CH], [-1, 240]], channel_multiplier=1).then_inc(m.s_pool5, 1)
                pool.wait_ge(m.s_pool5, 2)
                nc.gpsimd.affine_select(out=sel[:], in_=sel[:], compare_op=ALU.is_ge, fill=0.0, base=0,
                                        pattern=[[-16, CH], [0, 240]], channel_multiplier=1).then_inc(m.s_pool5, 1)
                pool.wait_ge(m.s_pool5, 3)
                nc.gpsimd.affine_select(out=sel[:], in_=sel[:], compare_op=ALU.is_ge, fill=0.0, base=15,
                                        pattern=[[16, CH], [0, 240]], channel_multiplier=-1).then_inc(m.s_sel5, 1)

            @block.tensor
            def _(pe):
                pe.wait_ge(m.s_p5, 64)
                nc.tensor.transpose(ps_a[:, 0, 0:P], rows[:], m.ident[:]).then_inc(m.s_p5_mm, 1)
                pe.wait_ge(m.s_p5c, 16 * 32)
                for c in range(2):
                    for jt in range(2):
                        last = nc.tensor.transpose(ps_a[:, 1, (c * 2 + jt) * P:(c * 2 + jt + 1) * P], crow[:, c, jt, :], m.ident[:])
                last.then_inc(m.s_c5_mm, 1)

            @block.scalar
            def _(act):
                act.wait_ge(m.s_d5, 16)
                for e in range(2):
                    last = nc.scalar.activation(dt[e * G_ST:(e + 1) * G_ST], dt_row[e * G_ST:(e + 1) * G_ST, :, :, e], ACT.Exp)
                last.then_inc(m.s_w5, 1)
                act.wait_ge(m.s_sin5, 1)
                nc.scalar.activation(w[:, 4], w[:, 0], ACT.Exp)
                nc.scalar.activation(w[:, 5], w[:, 0], ACT.Exp, scale=-1.0)
                nc.scalar.activation(w[:, 6], w[:, 2], ACT.Sin)
                nc.scalar.activation(w[:, 7], w[:, 3], ACT.Sin).then_inc(m.s_w5, 1)

            @block.vector
            def _(dve):
                V = nc.vector
                link = Chain(dve, m.s_dve5)
                dve.wait_ge(m.s_p5_mm, 1)
                link(V.tensor_copy(pc[:], ps_a[:, 0, 0:P].rearrange("p (n d j) -> p n d j", n=4, d=2)))
                dve.wait_ge(m.s_w5, 1)
                V.tensor_tensor(w[:, 0], dt[:], pc[:, 0], ALU.mult)
                link(V.tensor_tensor(w[:, 1], dt[:], pc[:, 1], ALU.mult))
                link(V.tensor_scalar(w[:, 8], w[:, 1], 0.15915494309189535, ROUND, ALU.mult, ALU.add))
                link(V.tensor_scalar(w[:, 8], w[:, 8], ROUND, None, ALU.subtract))
                link(V.scalar_tensor_tensor(w[:, 2], w[:, 8], -TWO_PI_HI, w[:, 1], ALU.mult, ALU.add))
                link(V.scalar_tensor_tensor(w[:, 2], w[:, 8], -TWO_PI_LO, w[:, 2], ALU.mult, ALU.add))
                link(V.tensor_scalar(w[:, 2], w[:, 2], 3.1415925, -3.1415925, ALU.min, ALU.max))
                link(V.scalar_tensor_tensor(w[:, 3], w[:, 2], -1.0, w[:, 2], ALU.mult, ALU.max))
                V.tensor_scalar(w[:, 3], w[:, 3], -1.0, 1.5707963267948966, ALU.mult, ALU.add).then_inc(m.s_sin5, 1)
                dve.wait_ge(m.s_w5, 2)
                V.tensor_tensor(pw[:, 0, 0, 0], w[:, 4], w[:, 7], ALU.mult)
                V.tensor_tensor(pw[:, 1, 0, 0], w[:, 4], w[:, 6], ALU.mult)
                V.tensor_tensor(pw[:, 0, 0, 1], w[:, 5], w[:, 7], ALU.mult)
                link(V.scalar_tensor_tensor(pw[:, 1, 0, 1], w[:, 5], -1.0, w[:, 6], ALU.mult, ALU.mult))

                def power(lo, n, by):
                    for i in range(n):
                        fr, fi, xr, xi = pw[:, 0, by - 1], pw[:, 1, by - 1], pw[:, 0, i], pw[:, 1, i]
                        V.tensor_tensor(pt[:, 0, i], fi, xi, ALU.mult)
                        V.tensor_tensor(pt[:, 1, i], fi, xr, ALU.mult)
                        V.tensor_tensor(pw[:, 0, lo + i], fr, xr, ALU.mult)
                        last = V.tensor_tensor(pw[:, 1, lo + i], fr, xi, ALU.mult)
                    link(last)
                    V.tensor_tensor(pw[:, 0, lo:lo + n], pw[:, 0, lo:lo + n], pt[:, 0, 0:n], ALU.subtract)
                    link(V.tensor_tensor(pw[:, 1, lo:lo + n], pw[:, 1, lo:lo + n], pt[:, 1, 0:n], ALU.add))
                power(1, 1, 1)
                power(2, 2, 2)
                power(4, 4, 4)
                V.tensor_copy(a8[:, 0, :, 0], pw[:, 0, CH - 1, 0])
                V.tensor_copy(a8[:, 0, :, 1], pw[:, 0, CH - 1, 0])
                V.tensor_scalar(a8[:, 1, :, 0], pw[:, 1, CH - 1, 0], -1.0, None, ALU.mult)
                V.tensor_copy(a8[:, 1, :, 1], pw[:, 1, CH - 1, 0])
                V.tensor_scalar(w[:, 8], pw[:, 0, 0, 0], -1.0, None, ALU.add)
                V.tensor_tensor(w[:, 9], pc[:, 0], pc[:, 0], ALU.mult)
                link(V.tensor_tensor(w[:, 10], pc[:, 1], pc[:, 1], ALU.mult))
                link(V.tensor_tensor(w[:, 9], w[:, 9], w[:, 10], ALU.add))
                link(V.reciprocal(w[:, 9], w[:, 9]))
                V.tensor_tensor(w[:, 10], w[:, 8], pc[:, 0], ALU.mult)
                V.tensor_tensor(w[:, 11], pw[:, 1, 0, 0], pc[:, 1], ALU.mult)
                V.tensor_tensor(w[:, 12], pw[:, 1, 0, 0], pc[:, 0], ALU.mult)
                link(V.tensor_tensor(w[:, 13], w[:, 8], pc[:, 1], ALU.mult))
                V.tensor_tensor(w[:, 10], w[:, 10], w[:, 11], ALU.add)
                link(V.tensor_tensor(w[:, 12], w[:, 12], w[:, 13], ALU.subtract))
                V.tensor_tensor(w[:, 10], w[:, 10], w[:, 9], ALU.mult)
                link(V.tensor_tensor(w[:, 12], w[:, 12], w[:, 9], ALU.mult))
                dve.wait_ge(m.s_c5_mm, 1)
                link(V.tensor_copy(c_sb[:], ps_a[:, 1, :].rearrange("p (c j h) -> p c j h", c=2, h=G_CH)))
                dve.wait_ge(m.s_p5b, 64)

                def cmul(out_re, out_im, xr, xi, yr, yi, t, negate_im=False):
                    V.tensor_tensor(out_re, xr, yr, ALU.mult)
                    link(V.tensor_tensor(t, xi, yi, ALU.mult))
                    link(V.tensor_tensor(out_re, out_re, t, ALU.subtract))
                    V.tensor_tensor(out_im, xr, yi, ALU.mult)
                    link(V.tensor_tensor(t, xi, yr, ALU.mult))
                    if negate_im:
                        link(V.scalar_tensor_tensor(out_im, out_im, -1.0, t, ALU.mult, ALU.subtract))
                    else:
                        link(V.tensor_tensor(out_im, out_im, t, ALU.add))

                for d in range(2):
                    g = [w[:, r, d].unsqueeze(2).to_broadcast([P, GP, G_CH]) for r in (10, 12)]
                    cmul(bb[:, 0, d], bb[:, 1, d], b_sb[:, 0], b_sb[:, 1], g[0], g[1], tmp[:, :, 0])
                for d in range(2):
                    for t in range(CH):
                        e = t if d == 0 else CH - 1 - t
                        up = [pw[:, c, e, 0, d].unsqueeze(2).to_broadcast([P, GP, G_CH]) for c in range(2)]
                        dn = [pw[:, c, e, 1, d].unsqueeze(2).to_broadcast([P, GP, G_CH]) for c in range(2)]
                        cmul(vt[:, 0, d, :, t], vt[:, 1, d, :, t], c_sb[:, 0], c_sb[:, 1], up[0], up[1], tmp[:, :, 0], True)
                        cmul(at[:, 0, d, :, t], at[:, 1, d, :, t], bb[:, 0, d], bb[:, 1, d], dn[0], dn[1], tmp[:, :, 1])
        s5_local(nc, m, ctx, atT, tt_sb, vt, at)
        ctx.close()
        s5_scan(nc, m, a, pc, vt, atT, tt_sb, sel, a8)


def s5_local(nc, m, ctx, atT, tt_sb, vt, at):
    ps_t = ctx.enter_context(nc.psum_tensor("ps_5t", [P, 4, 4, P], F32))
    msk = ctx.enter_context(nc.sbuf_tensor("s5_msk", [P, 2, CH, G_CH], F32))
    tm2 = ctx.enter_context(nc.sbuf_tensor("s5_tm2", [P, 4, P], F32))
    with nc.Block() as block:

        @block.gpsimd
        def _(pool):
            nc.gpsimd.memset(msk[:], 1.0).then_inc(m.s_pool5, 1)
            pool.wait_ge(m.s_pool5, 4)
            nc.gpsimd.affine_select(out=msk[:, 0], in_=msk[:, 0], compare_op=ALU.is_ge, fill=0.0, base=15,
                                    pattern=[[16, CH], [0, G_CH]], channel_multiplier=-1)
            nc.gpsimd.affine_select(out=msk[:, 1], in_=msk[:, 1], compare_op=ALU.is_ge, fill=0.0, base=0,
                                    pattern=[[-16, CH], [0, G_CH]], channel_multiplier=1).then_inc(m.s_msk5, 1)

        @block.tensor
        def _(pe):
            for n in range(16):
                c, d, j4 = n // 8, n // 4 % 2, n % 4
                if n >= 4:
                    pe.wait_ge(m.s_at_sb, n - 3)
                for j in range(4):
                    last = nc.tensor.transpose(ps_t[:, n % 4, j, :],
                                               at[:, c, d, 4 * j4 + j].rearrange("p t h -> p (t h)"), m.ident[:])
                last.then_inc(m.s_at_mm, 1)
            for j4 in range(4):
                pe.wait_ge(m.s_at_sb, 16)
                if j4:
                    pe.wait_ge(m.s_t_sb, 2 * j4)
                for d in range(2):
                    for e in range(2):
                        pr = slice(e * G_ST, (e + 1) * G_ST)
                        for j in range(4):
                            jj = 4 * j4 + j
                            for c in range(2):
                                last = nc.tensor.matmul(ps_t[:, 2 * d + e, j, :], at[pr, c, d, jj].rearrange("p t h -> p (t h)"),
                                                        vt[pr, c, d, jj].rearrange("p t h -> p (t h)"),
                                                        start=(c == 0), stop=(c == 1))
                last.then_inc(m.s_t_mm, 1)

        @block.scalar
        def _(act):
            for n in range(16):
                c, d, j4 = n // 8, n // 4 % 2, n % 4
                act.wait_ge(m.s_at_mm, n + 1)
                nc.scalar.activation(atT[:, c, d, 4 * j4:4 * j4 + 4], ps_t[:, n % 4], ACT.Identity).then_inc(m.s_at_sb, 1)

        @block.vector
        def _(dve):
            V = nc.vector
            dve.wait_ge(m.s_msk5, 1)
            mk = [msk[:, d].rearrange("p t h -> p (t h)").unsqueeze(1).to_broadcast([P, 4, P]) for d in range(2)]
            for j4 in range(4):
                dve.wait_ge(m.s_t_mm, j4 + 1)
                for e in range(2):
                    n = 2 * j4 + e
                    o = tt_sb[:, 8 * j4 + e:8 * j4 + 8:2, :]
                    if n:
                        dve.wait_ge(m.s_t_sb, n)
                    V.tensor_tensor(o, ps_t[:, e], mk[0], ALU.mult)
                    V.tensor_tensor(tm2[:], ps_t[:, 2 + e], mk[1], ALU.mult).then_inc(m.s_tab5, 1)
                    dve.wait_ge(m.s_tab5, n + 1)
                    V.tensor_tensor(o, o, tm2[:], ALU.add).then_inc(m.s_t_sb, 1)


def s5_scan(nc, m, a, pc, vt, atT, tt_sb, sel, a8):
    NSL = 2 * NC
    with ExitStack() as ctx:
        def sb(name, shape):
            return ctx.enter_context(nc.sbuf_tensor(name, shape, F32))

        def pb(name, shape):
            return ctx.enter_context(nc.psum_tensor(name, shape, F32))
        ps_u = pb("ps_5u", [P, 2, 4, P])
        ps_z = pb("ps_5z", [P, 4, 4, P])
        u_sb = sb("s5_u", [P, G_N, NC])
        zz = sb("s5_zz", [P, NSL, 2, GP])
        x = sb("s5_x", [P, NSL, 2, GP])
        xw = sb("s5_xw", [P, 3, 2, 2, GP])
        fin = sb("s5_fin", [P, 2, 2, GP])
        finT = sb("s5_finT", [G_ST, P])
        with nc.Block() as block:

            @block.tensor
            def _(pe):
                for n in range(8):
                    if n >= 2:
                        pe.wait_ge(m.s_u_sb, n - 1)
                    for q in range(4):
                        g = 4 * n + q
                        for s in range(CH):
                            last = nc.tensor.matmul(ps_u[:, n % 2, q, 0:NC], sel[:, g % 8, 112 - 16 * s:240 - 16 * s],
                                                    m.yc[:, g // 8, s:N:CH], start=(s == 0), stop=(s == CH - 1))
                    last.then_inc(m.s_u_mm, 1)
                pe.wait_ge(m.s_u_sb, 8)
                for n in range(16):
                    c, d, j4 = n // 8, n // 4 % 2, n % 4
                    if n >= 4:
                        pe.wait_ge(m.s_zz_sb, n - 3)
                    for j in range(4):
                        for e in range(2):
                            last = nc.tensor.matmul(ps_z[e * G_ST:(e + 1) * G_ST, n % 4, j, 0:NC],
                                                    atT[:, c, d, 4 * j4 + j, e * G_ST:(e + 1) * G_ST],
                                                    u_sb[:, 2 * (4 * j4 + j) + e, :], start=True, stop=True)
                    last.then_inc(m.s_zz_mm, 1)

            @block.scalar
            def _(act):
                for n in range(8):
                    act.wait_ge(m.s_u_mm, n + 1)
                    nc.scalar.activation(u_sb[:, 4 * n:4 * n + 4, :], ps_u[:, n % 2, :, 0:NC], ACT.Identity).then_inc(m.s_u_sb, 1)
                for n in range(16):
                    c, d, j4 = n // 8, n // 4 % 2, n % 4
                    act.wait_ge(m.s_zz_mm, n + 1)
                    sl = slice(0, NC) if d == 0 else slice(NSL - 1, NC - 1, -1)
                    nc.scalar.activation(zz[:, sl, c, 4 * j4:4 * j4 + 4], ps_z[:, n % 4, :, 0:NC].rearrange("p j c -> p c j"),
                                         ACT.Identity).then_inc(m.s_zz_sb, 1)

            @block.vector
            def _(dve):
                V = nc.vector

                def two(buf, s0, s1):
                    return buf[:, s0:s1 + 1:s1 - s0]

                V.tensor_copy(two(x, 0, NC + NCP), pc[:, 2:4].rearrange("p c d j -> p d c j"))
                V.memset(x[:, NCS:NCS + 1], 0.0)
                V.memset(x[:, NC:NC + 1], 0.0).then_inc(m.s_x5, 1)
                dve.wait_ge(m.s_x5, 1)
                dve.wait_ge(m.s_zz_sb, 16)

                def step(n, s0, s1, o):
                    V.tensor_tensor(xw[:, 0], two(x, s0, s1), two(zz, s0, s1), ALU.add).then_inc(m.s_x5, 1)
                    dve.wait_ge(m.s_x5, n + 1)
                    V.tensor_tensor(xw[:, 1], xw[:, 0], a8[:, 0], ALU.mult)
                    V.tensor_tensor(xw[:, 2], xw[:, 0, :, ::-1], a8[:, 1], ALU.mult).then_inc(m.s_x5, 1)
                    dve.wait_ge(m.s_x5, n + 2)
                    V.tensor_tensor(o, xw[:, 1], xw[:, 2], ALU.add).then_inc(m.s_x5, 1)
                    dve.wait_ge(m.s_x5, n + 3)
                n = 1
                for k in range(NCP):
                    o = two(x, NCS + k + 1, NC + k + 1) if k + 1 < NCP else fin[:].rearrange("p c d j -> p d c j")
                    step(n, NCS + k, NC + k, o)
                    n += 3
                for k in range(NCS - 1):
                    step(n, k, NC + NCP + k, two(x, k + 1, NC + NCP + k + 1))
                    n += 3
        flat = atT[:].rearrange("p c d j q -> p (c d j q)")
        y_g = flat[:, 0:G_N * NC].rearrange("p (g c) -> p g c", g=G_N)
        y_f = flat[:, G_N * NC:G_N * NC + MT * N].rearrange("p (k n) -> p k n", k=MT)
        glu_w = flat[:, 5120:5120 + MT * MIX].rearrange("p (k n) -> p k n", k=MT)
        ps_y = ps_z[:, 0:2]
        ps_g = ps_z[:, 2:4].rearrange("p b j q -> p b (j q)")
        with nc.Block() as block:

            @block.sync
            def _(sp):
                sp.dma_start(glu_w, a["s5_w_glu"].rearrange("(k p) n -> p k n", p=P)).then_inc(m.s_glu_w, 16)
                sp.dma_start(m.y_dram[1], m.yb[:]).then_inc(m.s_sp5, 16)
                sp.wait_ge(m.s_yc5, MT)
                sp.dma_start(m.y_dram[2], m.yc[:]).then_inc(m.s_sp5, 16)
                sp.wait_ge(m.s_sp5, 32)

            @block.gpsimd
            def _(pool):
                pool.wait_ge(m.s_fin_sb, 1)
                pool.dma_start(a["new_s5_re"].rearrange("d (j e) p -> (d j) (e p)", e=2), finT[0:32, :]).then_inc(m.s_out5, 16)
                pool.dma_start(a["new_s5_im"].rearrange("d (j e) p -> (d j) (e p)", e=2), finT[32:64, :]).then_inc(m.s_out5, 16)
                pool.wait_ge(m.s_out5, 32)

            @block.tensor
            def _(pe):
                for j4 in range(4):
                    for e in range(2):
                        pr = slice(e * G_ST, (e + 1) * G_ST)
                        if j4:
                            pe.wait_ge(m.s_y5_sb, 2 * j4 - 1 + e)
                        for j in range(4):
                            jj = 4 * j4 + j
                            o = ps_y[:, e, j, 0:NC]
                            nc.tensor.matmul(o, tt_sb[:, 2 * jj + e, :], u_sb[:, 2 * jj + e, :], start=True, stop=False)
                            for d in range(2):
                                sl = slice(0, NC) if d == 0 else slice(NSL - 1, NC - 1, -1)
                                for c in range(2):
                                    last = nc.tensor.matmul(o, vt[pr, c, d, jj].rearrange("p t h -> p (t h)"), x[pr, sl, c, jj],
                                                            start=False, stop=(d == 1 and c == 1))
                        last.then_inc(m.s_y5_mm, 1)
                nc.tensor.transpose(ps_g[0:G_ST, 0, 0:P], fin[:].rearrange("p c d j -> p (c d j)"), m.ident[:]).then_inc(m.s_fin_mm, 1)
                pe.wait_ge(m.s_y5_sb, 8)
                for f in range(MT):
                    if f:
                        pe.wait_ge(m.s_f5_sb, 2 * f)
                    for t in range(CH):
                        for g in range(8):
                            last = nc.tensor.matmul(ps_y[:, t // 4, t % 4, 0:NC], sel[:, t, 112 - 16 * g:240 - 16 * g],
                                                    y_g[:, 8 * f + g, :], start=(g == 0), stop=(g == 7))
                    last.then_inc(m.s_f5_mm, 1)
                pe.wait_ge(m.s_glu_w, 16)
                pe.wait_ge(m.s_ge5, MT)
                pe.wait_ge(m.s_fin_sb, 1)
                for f in range(MT):
                    if f:
                        pe.wait_ge(m.s_glu_sb, f)
                    for b, sl in ((0, slice(0, TS)), (1, slice(TS, N))):
                        for k in range(MT):
                            last = nc.tensor.matmul(ps_g[:, b, 0:sl.stop - sl.start], glu_w[:, k, f * P:(f + 1) * P], y_f[:, k, sl],
                                                    start=(k == 0), stop=(k == MT - 1))
                    last.then_inc(m.s_glu_mm, 1)

            @block.vector
            def _(dve):
                V = nc.vector
                for n in range(8):
                    j4, e = n // 2, n % 2
                    dve.wait_ge(m.s_y5_mm, n + 1)
                    V.tensor_copy(y_g[:, 8 * j4 + e:8 * j4 + 8:2, :], ps_y[:, e, :, 0:NC]).then_inc(m.s_y5_sb, 1)
                dve.wait_ge(m.s_fin_mm, 1)
                V.tensor_copy(finT[:], ps_g[0:G_ST, 0, 0:P]).then_inc(m.s_fin_sb, 1)
                for f in range(MT):
                    dve.wait_ge(m.s_f5_mm, f + 1)
                    for b in range(2):
                        o = y_f[:, f].rearrange("p (c t) -> p t c", t=CH)[:, 4 * b:4 * b + 4]
                        u = m.yc[:, f].rearrange("p (c t) -> p t c", t=CH)[:, 4 * b:4 * b + 4]
                        d0 = PCOLS["s5_d"][0] + f
                        V.tensor_scalar(o, u, m.pcol[:, d0:d0 + 1], None, ALU.mult).then_inc(m.s_du5, 1)
                        dve.wait_ge(m.s_du5, 2 * f + b + 1)
                        V.tensor_tensor(o, o, ps_y[:, b, :, 0:NC], ALU.add).then_inc(m.s_f5_sb, 1)
                for f in range(MT):
                    dve.wait_ge(m.s_glu_sb, f + 1)
                    V.tensor_tensor(m.yc[:, f], m.yc[:, f], y_f[:, f], ALU.mult).then_inc(m.s_yc5, 1)

            @block.scalar
            def _(act):
                for f in range(MT):
                    act.wait_ge(m.s_f5_sb, 2 * f + 2)
                    nc.scalar.activation(y_f[:, f], y_f[:, f], ACT.Gelu_apprx_tanh).then_inc(m.s_ge5, 1)
                b0 = PCOLS["s5_b_glu"][0]
                for f in range(MT):
                    act.wait_ge(m.s_glu_mm, f + 1)
                    nc.scalar.activation(m.yc[:, f, 0:TS], ps_g[:, 0, :], ACT.Sigmoid, bias=m.pcol[:, b0 + f:b0 + f + 1])
                    nc.scalar.activation(m.yc[:, f, TS:N], ps_g[:, 1, 0:TP], ACT.Sigmoid,
                                         bias=m.pcol[:, b0 + f:b0 + f + 1]).then_inc(m.s_glu_sb, 1)


R_T, K_T, V_T, LW_T, LA_T, LG_T = 0, MT, 2 * MT, 3 * MT, 3 * MT + 1, 3 * MT + 2
LEVELS = 7


def rwkv_phase(nc, m, a):
    with ExitStack() as ctx:
        def sb(name, shape):
            return ctx.enter_context(nc.sbuf_tensor(name, shape, F32))
        m.vt = sb("vt", [P, NT, MIX])
        m.sig, m.kd, m.bd = (sb(x, [P, 2, MT, N]) for x in ("sig", "kd", "bd"))
        m.lev = sb("lev", [P, 2, LEVELS, P])
        m.smask, m.imask = sb("smask", [P, 2, P]), sb("imask", [P, 2, P])
        m.st, m.rkh = sb("st", [P, 2, MT, HD]), sb("rkh", [P, MT, 2])
        m.bon, m.neghalf = sb("bon", [P, NT, HEADS]), sb("neghalf", [P, HEADS])
        m.kkn = m.zr[:, V_T:V_T + MT, 0:N]
        m.yo = m.zr[:, K_T:K_T + MT, :].rearrange("p t c -> p (t c)")[:, 0:NT * MIX].rearrange("p (t c) -> p t c", t=NT)
        rwkv_prepare(nc, m, a)
        rwkv_chunks(nc, m, a)
        rwkv_finish(nc, m, a)


def rwkv_prepare(nc, m, a):
    with ExitStack() as ctx:
        def sb(name, shape, dt=F32):
            return ctx.enter_context(nc.sbuf_tensor(name, shape, dt))
        w2 = sb("rw_w2", [P, MIX])
        a2 = sb("rw_a2", [P, MIX])
        s_in = sb("rw_sin", [HD, 2, HEADS, HD])
        mu2 = sb("rw_mu2", [P, 2, RT])
        ka1 = sb("rw_ka1", [P, MT])
        nb = sb("rw_nb", [P, 2, ZW - 2])
        zs = sb("rw_zs", [P, 2, ZW - 2])
        blk = sb("rw_blk", [P, P])
        tx = sb("rw_tx", [P, P], I32)
        ty = sb("rw_ty", [P, P], I32)
        kk = sb("rw_kk", [P, MT, N])
        sq = sb("rw_sq", [P, 2, N])
        rn = sb("rw_rn", [P, 2, N])
        ps_s = ctx.enter_context(nc.psum_tensor("ps_rs", [P, 2, 512], F32))
        ps_p = ctx.enter_context(nc.psum_tensor("ps_rp", [P, 2, 512], F32))
        ps_v = ctx.enter_context(nc.psum_tensor("ps_rv", [P, 2, 512], F32))
        ps_n = ctx.enter_context(nc.psum_tensor("ps_rn", [P, 2, 512], F32))
        (m.r_w, m.r_mu, m.r_nb, m.r_zs, m.r_sh, m.r_blk, m.r_pool, m.r_lora, m.r_sg, m.r_sg_mm, m.r_v_mm,
         m.r_v_sb, m.r_kk, m.r_sq, m.r_n_mm, m.r_rt, m.r_kkn, m.r_st, m.r_st_mm, m.r_dve, m.r_sm) = sems(
            nc, m, "r_w r_mu r_nb r_zs r_sh r_blk r_pool r_lora r_sg r_sg_mm r_v_mm r_v_sb r_kk r_sq r_n_mm r_rt r_kkn r_st "
            "r_st_mm r_dve r_sm")
        with nc.Block() as block:

            @block.sync
            def _(sp):
                sp.dma_start(w2[:], a["rwkv_w2"]).then_inc(m.r_w, 16)
                sp.dma_start(a2[:], a["rwkv_a2"]).then_inc(m.r_w, 16)
                sp.dma_start(s_in[:], a["state_rwkv"].rearrange("d h v k -> v d h k")).then_inc(m.r_st, 16)

            @block.gpsimd
            def _(pool):
                link = Chain(pool, m.r_pool)
                for t in range(RT):
                    if t >= 2:
                        pool.wait_ge(m.r_sh, t - 1)
                    nc.gpsimd.tensor_tensor(nb[:, t % 2], m.zr[:, t, 0:ZW - 2], m.zr[:, t, 2:ZW], ALU.add).then_inc(m.r_nb, 1)
                nc.gpsimd.iota(tx[:], pattern=[[0, P]], base=0, channel_multiplier=1)
                nc.gpsimd.iota(ty[:], pattern=[[1, P]], base=0, channel_multiplier=0)
                nc.gpsimd.memset(m.smask[:], 1.0)
                nc.gpsimd.memset(m.imask[:], 1.0)
                nc.gpsimd.memset(m.neghalf[:], -0.5)
                link(nc.gpsimd.memset(blk[:], 1.0))
                for buf, base in ((m.smask, -1), (m.imask, 0)):
                    nc.gpsimd.affine_select(out=buf[:, 0], in_=buf[:, 0], compare_op=ALU.is_ge, fill=0.0, base=base,
                                            pattern=[[-1, P]], channel_multiplier=1)
                    nc.gpsimd.affine_select(out=buf[:, 1], in_=buf[:, 1], compare_op=ALU.is_ge, fill=0.0, base=base,
                                            pattern=[[1, P]], channel_multiplier=-1)
                link(nc.gpsimd.affine_select(out=blk[:, 0:HD], in_=blk[:, 0:HD], compare_op=ALU.is_ge, fill=0.0, base=HD - 1,
                                             pattern=[[0, HD]], channel_multiplier=-1))
                nc.gpsimd.affine_select(out=blk[:, HD:P], in_=blk[:, HD:P], compare_op=ALU.is_ge, fill=0.0, base=-HD,
                                        pattern=[[0, HD]], channel_multiplier=1).then_inc(m.r_blk, 1)

            @block.vector
            def _(dve):
                V = nc.vector
                link = Chain(dve, m.r_dve)
                mu0 = PCOLS["rwkv_mu"][0]
                V.tensor_scalar(mu2[:, 0], m.pcol[:, mu0:mu0 + RT], -1.0, 1.0, ALU.mult, ALU.add)
                V.tensor_scalar(mu2[:, 1], m.pcol[:, mu0:mu0 + RT], 0.5, None, ALU.mult).then_inc(m.r_mu, 1)
                dve.wait_ge(m.r_mu, 1)
                ka0, kk0, rk0 = (PCOLS[x][0] for x in ("rwkv_ka", "rwkv_kk", "rwkv_rk"))
                V.tensor_scalar(ka1[:], m.pcol[:, ka0:ka0 + MT], -1.0, 1.0, ALU.mult, ALU.add)
                link(V.memset(m.rkh[:], 0.0))
                for e in range(2):
                    V.tensor_copy(m.rkh[e * HD:(e + 1) * HD, :, e], m.pcol[e * HD:(e + 1) * HD, rk0:rk0 + MT])
                for t in range(RT):
                    dve.wait_ge(m.r_nb, t + 1)
                    dve.wait_ge(m.r_zs, t + 1)
                    V.scalar_tensor_tensor(m.zr[:, t, 0:TS], nb[:, t % 2, 0:TS], mu2[:, 1, t:t + 1], zs[:, t % 2, 0:TS],
                                           ALU.mult, ALU.add)
                    V.scalar_tensor_tensor(m.zr[:, t, TS:N], nb[:, t % 2, ZP - 1:ZP - 1 + TP], mu2[:, 1, t:t + 1],
                                           zs[:, t % 2, ZP - 1:ZP - 1 + TP], ALU.mult, ALU.add).then_inc(m.r_sh, 1)
                dve.wait_ge(m.r_sh, RT)
                for f in range(MT):
                    V.tensor_scalar(kk[:, f], m.zr[:, K_T + f, 0:N], m.pcol[:, kk0 + f:kk0 + f + 1], None,
                                    ALU.mult).then_inc(m.r_kk, 1)
                dve.wait_ge(m.r_blk, 1)
                link(V.tensor_tensor(tx[:], tx[:], ty[:], ALU.bitwise_xor))
                for j in range(LEVELS):
                    link(V.tensor_single_scalar(ty[:], tx[:], j, ALU.logical_shift_right))
                    link(V.tensor_scalar(m.lev[:, 0, j], ty[:], 1.0, -1.0 if j == 0 else 1.0, ALU.is_equal, ALU.mult))
                    V.tensor_tensor(m.lev[:, 1, j], m.lev[:, 0, j], m.smask[:, 1], ALU.mult)
                    link(V.tensor_tensor(m.lev[:, 0, j], m.lev[:, 0, j], m.smask[:, 0], ALU.mult))
                dve.wait_ge(m.r_st_mm, 1)
                V.tensor_copy(m.st[:], ps_v[:, 0, :].rearrange("p (d q v) -> p d q v", d=2, q=MT)).then_inc(m.r_sm, 1)
                for f in range(MT):
                    dve.wait_ge(m.r_rt, f + 1)
                    link(V.tensor_scalar_max(rn[:, f % 2], rn[:, f % 2], 1e-12))
                    link(V.reciprocal(rn[:, f % 2], rn[:, f % 2]))
                    if f == 0:
                        dve.wait_ge(m.r_v_sb, NT)
                    V.tensor_tensor(m.kkn[:, f], kk[:, f], rn[:, f % 2], ALU.mult).then_inc(m.r_kkn, 1)
                dve.wait_ge(m.r_sg, 16)
                dve.wait_ge(m.r_kkn, MT)
                for d in range(2):
                    for f in range(MT):
                        V.tensor_tensor(m.bd[:, d, f], m.kkn[:, f], m.kd[:, d, f], ALU.mult)
                        link(V.tensor_scalar(m.kd[:, d, f], m.kd[:, d, f], m.pcol[:, ka0 + f:ka0 + f + 1], ka1[:, f:f + 1],
                                             ALU.mult, ALU.add))
                        last = V.tensor_tensor(m.kd[:, d, f], m.kd[:, d, f], m.zr[:, K_T + f, 0:N], ALU.mult)
                link(last)
                V.memset(m.bon[:], 0.0)
                link(V.memset(m.yo[:], 0.0))

            @block.scalar
            def _(act):
                A = nc.scalar.activation
                act.wait_ge(m.r_mu, 1)
                for t in range(RT):
                    if t >= 2:
                        act.wait_ge(m.r_sh, t - 1)
                    A(zs[:, t % 2], m.zr[:, t, 1:ZW - 1], ACT.Identity, scale=mu2[:, 0, t:t + 1]).then_inc(m.r_zs, 1)
                act.wait_ge(m.r_sh, RT)
                A(m.zr[:, LW_T, 0:N], m.zr[:, LW_T, 0:N], ACT.Tanh).then_inc(m.r_lora, 1)
                A(m.zr[:, LG_T, 0:N], m.zr[:, LG_T, 0:N], ACT.Sigmoid).then_inc(m.r_lora, 1)
                n = 0
                for kind, out, b0 in ((0, m.sig, PCOLS["rwkv_w0"][0]), (1, m.kd, PCOLS["rwkv_a0"][0])):
                    for f in range(MT):
                        for d in range(2):
                            act.wait_ge(m.r_sg_mm, n + 1)
                            b = m.pcol[:, b0 + d * MT + f:b0 + d * MT + f + 1]
                            A(out[:, d, f, 0:TS], ps_s[:, d, :], ACT.Sigmoid, bias=b)
                            A(out[:, d, f, TS:N], ps_p[:, d, 0:TP], ACT.Sigmoid, bias=b).then_inc(m.r_sg, 1)
                            n += 1
                act.wait_ge(m.r_sm, 1)
                for t in range(NT):
                    act.wait_ge(m.r_v_mm, t + 1)
                    A(m.vt[:, t], ps_v[:, t % 2, :], ACT.Identity).then_inc(m.r_v_sb, 1)
                for f in range(MT):
                    act.wait_ge(m.r_kk, f + 1)
                    if f >= 2:
                        act.wait_ge(m.r_n_mm, f - 1)
                    A(sq[:, f % 2], kk[:, f], ACT.Square).then_inc(m.r_sq, 1)
                    act.wait_ge(m.r_n_mm, f + 1)
                    if f >= 2:
                        act.wait_ge(m.r_kkn, f - 1)
                    A(rn[:, f % 2, 0:TS], ps_n[:, 0, :], ACT.Sqrt)
                    A(rn[:, f % 2, TS:N], ps_n[:, 1, 0:TP], ACT.Sqrt).then_inc(m.r_rt, 1)

            @block.tensor
            def _(pe):
                pe.wait_ge(m.r_st, 16)
                for d in range(2):
                    for q in range(MT):
                        last = nc.tensor.transpose(ps_v[:, 0, (d * MT + q) * HD:(d * MT + q + 1) * HD],
                                                   s_in[:, d, 2 * q:2 * q + 2].rearrange("v h k -> v (h k)"), m.ident[0:HD, 0:HD])
                last.then_inc(m.r_st_mm, 1)
                pe.wait_ge(m.r_w, 32)
                pe.wait_ge(m.r_lora, 2)
                n = 0
                for kind, w, tile in ((0, w2, LW_T), (1, a2, LA_T)):
                    for f in range(MT):
                        for d in range(2):
                            pr = slice(d * HD, (d + 1) * HD)
                            if n >= 2:
                                pe.wait_ge(m.r_sg, n - 1)
                            nc.tensor.matmul(ps_s[:, d, :], w[pr, f * P:(f + 1) * P], m.zr[pr, tile, 0:TS], start=True, stop=True)
                            nc.tensor.matmul(ps_p[:, d, 0:TP], w[pr, f * P:(f + 1) * P], m.zr[pr, tile, TS:N],
                                             start=True, stop=True).then_inc(m.r_sg_mm, 1)
                            n += 1
                pe.wait_ge(m.r_sm, 1)
                for t in range(NT):
                    if t >= 2:
                        pe.wait_ge(m.r_v_sb, t - 1)
                    for q in range(MT):
                        last = nc.tensor.transpose(ps_v[:, t % 2, q * P:(q + 1) * P], m.zr[:, V_T + q, t * P:(t + 1) * P], m.ident[:])
                    last.then_inc(m.r_v_mm, 1)
                pe.wait_ge(m.r_blk, 1)
                for f in range(MT):
                    pe.wait_ge(m.r_sq, f + 1)
                    if f:
                        pe.wait_ge(m.r_rt, f)
                    nc.tensor.matmul(ps_n[:, 0, :], blk[:], sq[:, f % 2, 0:TS], start=True, stop=True)
                    nc.tensor.matmul(ps_n[:, 1, 0:TP], blk[:], sq[:, f % 2, TS:N], start=True, stop=True).then_inc(m.r_n_mm, 1)


def rwkv_chunks(nc, m, a):
    STEPS = TS // P
    LJ = LEVELS - 1
    with ExitStack() as ctx:
        def sb(name, shape):
            return ctx.enter_context(nc.sbuf_tensor(name, shape, F32))
        rh, ah, kh, bh = (sb(x, [P, 2, MT, P]) for x in ("rc_r", "rc_a", "rc_k", "rc_b"))
        rkd = sb("rc_rkd", [P, MT, P])
        vs = sb("rc_v", [P, 2, MIX])
        cs, dm, dp = (sb(x, [P, MT, P]) for x in ("rc_cs", "rc_dm", "rc_dp"))
        ex = sb("rc_ex", [P, 3, MT, P])
        fs = sb("rc_fs", [P, 2, 2, MT])
        ones = sb("rc_ones", [P, P])
        lo, xi, yi, gg, lj, akt, rkt, rbt = (sb(x, [P, 2, MT, P]) for x in
                                             ("rc_l", "rc_x", "rc_y", "rc_g", "rc_lj", "rc_akt", "rc_rkt", "rc_rbt"))
        ktok, btok = sb("rc_ktok", [P, MIX]), sb("rc_btok", [P, MIX])
        sts = sb("rc_sts", [P, MT, HD])
        rhs, un = sb("rc_rhs", [P, 2, MT, HD]), sb("rc_un", [P, 2, MT, HD])
        ys = sb("rc_ys", [P, HEADS, HD])
        yq = sb("rc_yq", [P, HEADS, HD])
        mv = sb("rc_mv", [P, 4, HEADS])
        scr = sb("rc_scr", [P, 2])
        bank = [ctx.enter_context(nc.psum_tensor(f"ps_c{i}", [P, MT, P], F32)) for i in range(8)]
        (m.c_cs, m.c_d, m.c_ex, m.c_stage, m.c_gr, m.c_L, m.c_gd, m.c_y1, m.c_x1, m.c_lj, m.c_g, m.c_gsb, m.c_yg,
         m.c_xg, m.c_yup, m.c_xup, m.c_kb_mm, m.c_kb, m.c_bo_mm, m.c_bo, m.c_sts, m.c_rh_mm, m.c_rh, m.c_u_mm,
         m.c_un, m.c_y_mm, m.c_y, m.c_s_mm, m.c_s, m.c_mu, m.c_yc, m.c_sq, m.c_var, m.c_gn, m.c_one, m.c_dve,
         m.c_pl, m.c_stz, m.c_gp, m.c_scr) = sems(
            nc, m, "c_cs c_d c_ex c_stage c_gr c_L c_gd c_y1 c_x1 c_lj c_g c_gsb c_yg c_xg c_yup c_xup c_kb_mm c_kb c_bo_mm "
            "c_bo c_sts c_rh_mm c_rh c_u_mm c_un c_y_mm c_y c_s_mm c_s c_mu c_yc c_sq c_var c_gn c_one c_dve c_pl "
            "c_stz c_gp c_scr")

        def tok(i, d):
            if d == 0 or (isinstance(i, int) and i == STEPS):
                return i * P
            return (i * -P) + (STEPS - 1) * P

        def chunk(i, d):
            if d == 0 or (isinstance(i, int) and i == STEPS):
                return i
            return (i * -1) + (STEPS - 1)

        def unit(i, d):
            return i * 2 + d

        def bc4(x):
            return x.unsqueeze(1).to_broadcast([P, MT, P])

        def run(eng, body):
            body(0, 0, (0, 1))
            body(0, 1, (1, 0))
            with eng.Fori(1, STEPS) as i:
                body(i, 0, (i, 1))
                body(i, 1, (i + 1, 0))
            body(STEPS, 0, (STEPS, 1))
            body(STEPS, 1, None)

        with nc.Block() as block:

            @block.tensor
            def _(pe):
                mm = nc.tensor.matmul

                def body(i, d, nxt):
                    n = unit(i, d)
                    pe.wait_ge(m.c_stage, n + 1)
                    wait(pe, m.c_y, n * 2)
                    for e in range(2):
                        pr = slice(e * HD, (e + 1) * HD)
                        for k, (l, r) in enumerate(((ah, bh), (bh, ah), (kh, ah), (kh, rh), (bh, rh))):
                            if e:
                                if k == 0:
                                    pe.wait_ge(m.c_L, n * 2 + 1)
                                else:
                                    pe.wait_ge(m.c_gd, n * 8 + k)
                            for q in range(MT):
                                last = mm(bank[k][:, q, :], l[pr, d, q, :], r[pr, d, q, :], start=True, stop=True)
                            last.then_inc(m.c_gr, 1)
                    wait(pe, m.c_s, n)
                    for q in range(MT):
                        last = nc.tensor.transpose(bank[6][:, q, :], kh[:, d, q, :], m.ident[:])
                    last.then_inc(m.c_kb_mm, 1)
                    wait(pe, m.c_bo, n)
                    for q in range(MT):
                        last = nc.tensor.transpose(bank[7][:, q, :], bh[:, d, q, :], m.ident[:])
                    last.then_inc(m.c_kb_mm, 1)
                    pe.wait_ge(m.c_kb, n * 2 + 2)
                    for q in range(MT):
                        last = mm(bank[7][:, 0, 2 * q:2 * q + 2], rkd[:, q, :], m.rkh[:, q, :], start=True, stop=True)
                    last.then_inc(m.c_bo_mm, 1)
                    for j in range(LJ):
                        for g in range(2):
                            c = n * (2 * LJ) + 2 * j + g
                            pe.wait_ge(m.c_lj, c + 1)
                            if j == 0:
                                pe.wait_ge(m.c_y1, n * 2 + g + 1)
                                pe.wait_ge(m.c_x1, n * 2 + g + 1)
                                pe.wait_ge(m.c_gd, n * 8 + 8)
                            else:
                                pe.wait_ge(m.c_yup, c - 1)
                                pe.wait_ge(m.c_xup, n * (2 * LJ - 2) + 2 * j - 2 + g + 1)
                            for q in range(MT):
                                last = mm(bank[g][:, q, :], lj[:, g, q, :], yi[:, g, q, :], start=True, stop=True)
                            last.then_inc(m.c_g, 1)
                        for g in range(2):
                            c = n * (2 * LJ) + 2 * j + g
                            pe.wait_ge(m.c_gsb, c + 1)
                            for q in range(MT):
                                last = mm(bank[2 + g][:, q, :], xi[:, g, q, :], gg[:, g, q, :], start=True, stop=True)
                            last.then_inc(m.c_yg, 1)
                            if j < LJ - 1:
                                for q in range(MT):
                                    last = mm(bank[4 + g][:, q, :], gg[:, g, q, :], xi[:, g, q, :], start=True, stop=True)
                                last.then_inc(m.c_xg, 1)
                    pe.wait_ge(m.c_sts, n + 1)
                    for e in range(2):
                        pr = slice(e * HD, (e + 1) * HD)
                        for q in range(MT):
                            h, o = 2 * q + e, bank[e][:, q, 0:HD]
                            mm(o, ah[pr, d, q, :], sts[pr, q, :], start=True, stop=False)
                            last = mm(o, akt[:, e, q, :], vs[:, d, h * HD:(h + 1) * HD], start=False, stop=True)
                        last.then_inc(m.c_rh_mm, 1)
                    pe.wait_ge(m.c_yup, n * (2 * LJ) + 2 * LJ)
                    for e in range(2):
                        pe.wait_ge(m.c_rh, n * 2 + e + 1)
                        for q in range(MT):
                            last = mm(bank[2 + e][:, q, 0:HD], yi[:, e, q, :], rhs[:, e, q, :], start=True, stop=True)
                        last.then_inc(m.c_u_mm, 1)
                    for e in range(2):
                        pr = slice(e * HD, (e + 1) * HD)
                        pe.wait_ge(m.c_un, n * 2 + e + 1)
                        for q in range(MT):
                            h, o = 2 * q + e, bank[4 + e][:, q, 0:HD]
                            mm(o, rh[pr, d, q, :], sts[pr, q, :], start=True, stop=False)
                            mm(o, rkt[:, e, q, :], vs[:, d, h * HD:(h + 1) * HD], start=False, stop=False)
                            last = mm(o, rbt[:, e, q, :], un[:, e, q, :], start=False, stop=True)
                        last.then_inc(m.c_y_mm, 1)
                    for e in range(2):
                        pr = slice(e * HD, (e + 1) * HD)
                        for q in range(MT):
                            h = 2 * q + e
                            hc = slice(h * HD, (h + 1) * HD)
                            mm(bank[6][pr, q, 0:HD], ktok[:, hc], vs[:, d, hc], start=True, stop=False)
                            last = mm(bank[6][pr, q, 0:HD], btok[:, hc], un[:, e, q, :], start=False, stop=True)
                    last.then_inc(m.c_s_mm, 1)
                run(pe, body)

            @block.vector
            def _(dve):
                V = nc.vector

                def scans(i, d):
                    n = unit(i, d)
                    wait(dve, m.c_stage, n)
                    for q in range(MT):
                        last = V.tensor_tensor_scan(cs[:, q, :], ones[:], m.sig[:, d, q, ds(tok(i, d), P)], 0.0, ALU.mult, ALU.add)
                    last.then_inc(m.c_cs, 1)
                    dve.wait_ge(m.c_cs, n * 2 + 1)
                    V.tensor_tensor(dm[:], cs[:], cs[:, :, P // 2 - 1:P // 2].to_broadcast([P, MT, P]), ALU.subtract).then_inc(m.c_cs, 1)
                    dve.wait_ge(m.c_cs, n * 2 + 2)
                    V.tensor_tensor(dp[:], dm[:], m.sig[:, d, :, ds(tok(i, d), P)], ALU.subtract).then_inc(m.c_d, 1)

                def body(i, d, nxt):
                    n = unit(i, d)
                    if isinstance(i, int) and i == STEPS:
                        V.memset(m.st[:, d], 0.0).then_inc(m.c_stz, 1)
                        dve.wait_ge(m.c_stz, d + 1)
                    for e in range(2):
                        for k, out in ((1, yi), (2, akt), (3, rkt), (4, rbt)):
                            mk = m.lev[:, 1 - d, 0] if k == 1 else m.smask[:, 1 - d] if k == 2 else m.imask[:, 1 - d]
                            dve.wait_ge(m.c_gr, n * 10 + 5 * e + k + 1)
                            V.tensor_tensor(out[:, e], bank[k][:], bc4(mk), ALU.mult).then_inc(m.c_gd, 1)
                        dve.wait_ge(m.c_gd, n * 8 + 4 * e + 1)
                        V.tensor_tensor(yi[:, e], yi[:, e], bc4(m.ident[:]), ALU.add).then_inc(m.c_y1, 1)
                    dve.wait_ge(m.c_bo_mm, n + 1)
                    V.tensor_tensor(m.bon[:, ds(chunk(i, d), 1), :], m.bon[:, ds(chunk(i, d), 1), :],
                                    bank[7][:, 0:1, 0:HEADS], ALU.add).then_inc(m.c_bo, 1)
                    for j in range(LJ):
                        for g in range(2):
                            c = n * (2 * LJ) + 2 * j + g
                            dve.wait_ge(m.c_yg, c + 1)
                            V.tensor_tensor(yi[:, g], yi[:, g], bank[2 + g][:], ALU.subtract).then_inc(m.c_yup, 1)
                            if j < LJ - 1:
                                dve.wait_ge(m.c_xg, n * (2 * LJ - 2) + 2 * j + g + 1)
                                V.tensor_tensor(xi[:, g], xi[:, g], bank[4 + g][:], ALU.subtract).then_inc(m.c_xup, 1)
                        if j == 0 and nxt:
                            scans(*nxt)
                        if j == 1:
                            wait(dve, m.c_s_mm, n)
                            wait(dve, m.c_dve, n * 3)
                            dve.wait_ge(m.c_ex, n + 1)
                            V.tensor_tensor(sts[:], m.st[:, d], fs[:, d, 0].unsqueeze(2).to_broadcast([P, MT, HD]),
                                            ALU.mult).then_inc(m.c_sts, 1)
                    dve.wait_ge(m.c_s_mm, n + 1)
                    V.tensor_tensor(m.st[:, d], sts[:], bank[6][:, :, 0:HD], ALU.add).then_inc(m.c_s, 1)
                    dve.wait_ge(m.c_s, n + 1)
                    V.tensor_tensor(m.st[:, d], m.st[:, d], fs[:, d, 1].unsqueeze(2).to_broadcast([P, MT, HD]),
                                    ALU.mult).then_inc(m.c_dve, 1)
                    dve.wait_ge(m.c_y, n * 2 + 2)
                    V.tensor_reduce(mv[:, 0], ys[:], AX.X, ALU.add).then_inc(m.c_dve, 1)
                    dve.wait_ge(m.c_dve, n * 3 + 2)
                    V.tensor_scalar(mv[:, 1], mv[:, 0], 1.0 / HD, None, ALU.mult).then_inc(m.c_mu, 1)
                    dve.wait_ge(m.c_sq, n + 1)
                    V.tensor_reduce(mv[:, 2], yq[:], AX.X, ALU.add).then_inc(m.c_dve, 1)
                    dve.wait_ge(m.c_dve, n * 3 + 3)
                    V.tensor_scalar(mv[:, 3], mv[:, 2], 1.0 / HD, GN_EPS, ALU.mult, ALU.add).then_inc(m.c_var, 1)
                V.memset(ones[:], 1.0).then_inc(m.c_one, 1)
                dve.wait_ge(m.c_one, 1)
                scans(0, 0)
                run(dve, body)

            @block.scalar
            def _(act):
                A = nc.scalar.activation

                def exps(i, d):
                    n = unit(i, d)
                    act.wait_ge(m.c_d, n + 1)
                    c = DECAY_C
                    A(ex[:, 0], dm[:] if d == 0 else dp[:], ACT.Exp, scale=-c if d == 0 else c)
                    A(ex[:, 1], dm[:] if d == 0 else dp[:], ACT.Exp, scale=c if d == 0 else -c)
                    A(ex[:, 2], dp[:] if d == 0 else dm[:], ACT.Exp, scale=-c if d == 0 else c)
                    A(fs[:, d, d], cs[:, :, P // 2 - 1], ACT.Exp, scale=-c)
                    A(fs[:, d, 1 - d], dm[:, :, P - 1], ACT.Exp, scale=-c).then_inc(m.c_ex, 1)

                def body(i, d, nxt):
                    n = unit(i, d)
                    for e in range(2):
                        act.wait_ge(m.c_gr, n * 10 + 5 * e + 1)
                        A(lo[:, e], bank[0][:], ACT.Identity).then_inc(m.c_L, 1)
                    for k, out in ((6, ktok), (7, btok)):
                        act.wait_ge(m.c_kb_mm, n * 2 + k - 5)
                        A(out[:], bank[k][:].rearrange("p q c -> p (q c)"), ACT.Identity).then_inc(m.c_kb, 1)
                    for j in range(LJ):
                        for g in range(2):
                            c = n * (2 * LJ) + 2 * j + g
                            act.wait_ge(m.c_g, c + 1)
                            A(gg[:, g], bank[g][:], ACT.Identity).then_inc(m.c_gsb, 1)
                        if j == 2 and nxt:
                            exps(*nxt)
                    for e in range(2):
                        act.wait_ge(m.c_rh_mm, n * 2 + e + 1)
                        A(rhs[:, e], bank[e][:, :, 0:HD], ACT.Identity).then_inc(m.c_rh, 1)
                    for e in range(2):
                        act.wait_ge(m.c_u_mm, n * 2 + e + 1)
                        A(un[:, e], bank[2 + e][:, :, 0:HD], ACT.Identity, scale=-1.0).then_inc(m.c_un, 1)
                    wait(act, m.c_gn, n)
                    for e in range(2):
                        act.wait_ge(m.c_y_mm, n * 2 + e + 1)
                        A(ys[:, e:HEADS:2, :], bank[4 + e][:, :, 0:HD], ACT.Identity).then_inc(m.c_y, 1)
                    act.wait_ge(m.c_yc, n + 1)
                    A(yq[:], ys[:], ACT.Square).then_inc(m.c_sq, 1)
                exps(0, 0)
                run(act, body)

            @block.gpsimd
            def _(pool):
                G = nc.gpsimd

                def absorb():
                    G.tensor_tensor(scr[:, 0:1], scr[:, 1:2], scr[:, 1:2], ALU.add)

                def hats(i, d):
                    n = unit(i, d)
                    t = ds(tok(i, d), P)
                    pool.wait_ge(m.c_ex, n + 1)
                    wait(pool, m.c_s_mm, n - 1)
                    wait(pool, m.c_bo_mm, n)
                    absorb()
                    G.tensor_tensor(rkd[:], m.zr[:, R_T:R_T + MT, t], m.kd[:, d, :, t], ALU.mult)
                    G.tensor_tensor(rh[:, d], m.zr[:, R_T:R_T + MT, t], ex[:, 0], ALU.mult)
                    G.tensor_tensor(ah[:, d], m.kkn[:, :, t], ex[:, 2], ALU.mult)
                    G.tensor_tensor(kh[:, d], m.kd[:, d, :, t], ex[:, 1], ALU.mult)
                    G.tensor_copy(vs[:, d], m.vt[:, ds(chunk(i, d), 1), :].rearrange("p a c -> p (a c)"))
                    G.tensor_tensor(bh[:, d], m.bd[:, d, :, t], ex[:, 1], ALU.mult).then_inc(m.c_stage, 1)

                def body(i, d, nxt):
                    n = unit(i, d)
                    for e in range(2):
                        pool.wait_ge(m.c_L, n * 2 + e + 1)
                        G.tensor_tensor(xi[:, e], lo[:, e], bc4(m.lev[:, d, 0]), ALU.mult).then_inc(m.c_pl, 1)
                        pool.wait_ge(m.c_pl, n * 2 + e + 1)
                        G.tensor_tensor(xi[:, e], xi[:, e], bc4(m.ident[:]), ALU.add).then_inc(m.c_x1, 1)
                    for j in range(LJ):
                        for g in range(2):
                            c = n * (2 * LJ) + 2 * j + g
                            if j:
                                pool.wait_ge(m.c_g, c - 1)
                            G.tensor_tensor(lj[:, g], lo[:, g], bc4(m.lev[:, d, j + 1]), ALU.mult).then_inc(m.c_lj, 1)
                        if j == 4 and nxt:
                            hats(*nxt)
                    pool.wait_ge(m.c_mu, n + 1)
                    G.tensor_tensor(ys[:], ys[:], mv[:, 1].unsqueeze(2).to_broadcast([P, HEADS, HD]), ALU.subtract).then_inc(m.c_yc, 1)
                    pool.wait_ge(m.c_var, n + 1)
                    G.tensor_tensor(mv[:, 3], mv[:, 3], m.neghalf[:], ALU.pow).then_inc(m.c_gp, 1)
                    pool.wait_ge(m.c_gp, n * 2 + 1)
                    G.tensor_tensor(ys[:], ys[:], mv[:, 3].unsqueeze(2).to_broadcast([P, HEADS, HD]), ALU.mult).then_inc(m.c_gp, 1)
                    pool.wait_ge(m.c_gp, n * 2 + 2)
                    wait(pool, m.c_gn, n)
                    absorb()
                    yo = m.yo[:, ds(chunk(i, d), 1), :].rearrange("p a c -> p (a c)")
                    G.tensor_tensor(yo, yo, ys[:].rearrange("p h v -> p (h v)"), ALU.add).then_inc(m.c_gn, 1)
                G.memset(scr[:], 0.0).then_inc(m.c_scr, 1)
                pool.wait_ge(m.c_scr, 1)
                hats(0, 0)
                run(pool, body)


def rwkv_finish(nc, m, a):
    with ExitStack() as ctx:
        def sb(name, shape):
            return ctx.enter_context(nc.sbuf_tensor(name, shape, F32))
        ya = m.sig[:, 0]
        g2 = sb("rf_g2", [P, MIX])
        gg_ = sb("rf_gng", [P, MIX])
        gb = sb("rf_gnb", [P, MIX])
        bv = sb("rf_bv", [P, 2, HEADS, HD])
        so = sb("rf_so", [HD, 2, HEADS, HD])
        ps_g = ctx.enter_context(nc.psum_tensor("ps_fg", [P, 2, 512], F32))
        ps_t = ctx.enter_context(nc.psum_tensor("ps_ft", [P, 2, 512], F32))
        ps_s = ctx.enter_context(nc.psum_tensor("ps_fs", [P, 2, 512], F32))
        (m.f_w, m.f_gn, m.f_g_mm, m.f_bv, m.f_y, m.f_t_mm, m.f_t, m.f_s_mm, m.f_s, m.f_out, m.f_dve, m.f_ya) = sems(
            nc, m, "f_w f_gn f_g_mm f_bv f_y f_t_mm f_t f_s_mm f_s f_out f_dve f_ya")
        with nc.Block() as block:

            @block.sync
            def _(sp):
                sp.dma_start(g2[:], a["rwkv_g2"]).then_inc(m.f_w, 16)
                sp.dma_start(gg_[:], a["rwkv_gn_g"].partition_broadcast(P)).then_inc(m.f_gn, 16)
                sp.dma_start(gb[:], a["rwkv_gn_b"].partition_broadcast(P)).then_inc(m.f_gn, 16)
                sp.wait_ge(m.f_s, 2)
                sp.dma_start(a["new_rwkv"].rearrange("d h v k -> v d h k"), so[:]).then_inc(m.f_out, 16)
                sp.wait_ge(m.f_t, NT)
                sp.dma_start(m.y_dram[0], ya).then_inc(m.f_ya, 16)
                sp.wait_ge(m.f_ya, 16)
                sp.wait_ge(m.f_out, 16)

            @block.tensor
            def _(pe):
                for d in range(2):
                    for q in range(MT):
                        last = nc.tensor.transpose(ps_s[0:HD, d, q * P:(q + 1) * P], m.st[:, d, q, :], m.ident[:])
                    last.then_inc(m.f_s_mm, 1)
                pe.wait_ge(m.f_w, 16)
                for t in range(NT):
                    if t >= 2:
                        pe.wait_ge(m.f_y, t - 1)
                    nc.tensor.matmul(ps_g[:, t % 2, :], m.zr[:, LG_T, t * P:(t + 1) * P], g2[:], start=True, stop=True).then_inc(m.f_g_mm, 1)
                for t in range(NT):
                    pe.wait_ge(m.f_y, t + 1)
                    if t >= 2:
                        pe.wait_ge(m.f_t, t - 1)
                    for q in range(MT):
                        last = nc.tensor.transpose(ps_t[:, t % 2, q * P:(q + 1) * P], m.yo[:, t, q * P:(q + 1) * P], m.ident[:])
                    last.then_inc(m.f_t_mm, 1)

            @block.gpsimd
            def _(pool):
                for t in range(NT):
                    if t >= 2:
                        pool.wait_ge(m.f_y, t - 1)
                    nc.gpsimd.tensor_tensor(bv[:, t % 2], m.vt[:, t].rearrange("p (h v) -> p h v", h=HEADS),
                                            m.bon[:, t].unsqueeze(2).to_broadcast([P, HEADS, HD]), ALU.mult).then_inc(m.f_bv, 1)

            @block.vector
            def _(dve):
                V = nc.vector
                link = Chain(dve, m.f_dve)
                dve.wait_ge(m.f_gn, 32)
                for t in range(NT):
                    y = m.yo[:, t]
                    link(V.tensor_tensor(y, y, gg_[:], ALU.mult))
                    link(V.scalar_tensor_tensor(y, gb[:], 2.0, y, ALU.mult, ALU.add))
                    dve.wait_ge(m.f_bv, t + 1)
                    link(V.tensor_tensor(y, y, bv[:, t % 2].rearrange("p h v -> p (h v)"), ALU.add))
                    dve.wait_ge(m.f_g_mm, t + 1)
                    V.tensor_tensor(y, y, ps_g[:, t % 2, :], ALU.mult).then_inc(m.f_y, 1)

            @block.scalar
            def _(act):
                for d in range(2):
                    act.wait_ge(m.f_s_mm, d + 1)
                    nc.scalar.activation(so[:, d].rearrange("v h k -> v (h k)"), ps_s[0:HD, d, :], ACT.Identity).then_inc(m.f_s, 1)
                for t in range(NT):
                    act.wait_ge(m.f_t_mm, t + 1)
                    nc.scalar.activation(ya[:, :, t * P:(t + 1) * P], ps_t[:, t % 2, :].rearrange("p (q c) -> p q c", q=MT),
                                         ACT.Identity).then_inc(m.f_t, 1)


def merge_phase(nc, m, a):
    FT = D // P
    with ExitStack() as ctx:
        def sb(name, shape):
            return ctx.enter_context(nc.sbuf_tensor(name, shape, F32))
        mT = sb("mg_mT", [P, FT, N])
        with ExitStack() as c2:
            def sb2(name, shape):
                return c2.enter_context(nc.sbuf_tensor(name, shape, F32))
            yT = sb2("mg_y", [P, 3, MT, N])
            hT = sb2("mg_h", [P, KT, N])
            wb = sb2("mg_wb", [P, 2, 3 * MT, P])
            wg = sb2("mg_wg", [P, 2, 3, KT, P])
            gs = sb2("mg_gs", [P, 2, N])
            pr = sb2("mg_pr", [P, 2, N])
            scr = sb2("mg_scr", [P, 2])
            pg_s, pb_s = (c2.enter_context(nc.psum_tensor(x, [P, 2, 512], F32)) for x in ("ps_gs", "ps_bs"))
            pg_p, pb_p = (c2.enter_context(nc.psum_tensor(x, [P, 2, 512], F32)) for x in ("ps_gp", "ps_bp"))
            (m.g_h, m.g_y, m.g_w0, m.g_w1, m.g_g_mm, m.g_b_mm, m.g_gs, m.g_pr, m.g_sum, m.g_scr) = sems(
                nc, m, "g_h g_y g_w0 g_w1 g_g_mm g_b_mm g_gs g_pr g_sum g_scr")
            land = [m.g_w0, m.g_w1]
            w_br = a["w_branch"].rearrange("n (k p) d -> p (n k) d", p=P)
            w_g = a["w_in_t"][:, :, GCOL:GCOL + 3 * D].rearrange("p k (n d) -> p n k d", n=3)

            def run(eng, pair):
                pair(0)
                with eng.Fori(1, FT // 2) as i:
                    pair(i)

            with nc.Block() as block:

                @block.sync
                def _(sp):
                    for k in range(KT):
                        sp.dma_start(hT[:, k], m.h1_dram[k]).then_inc(m.g_h, 16)
                    sp.dma_start(yT[:], m.y_dram.rearrange("n p k c -> p n k c")).then_inc(m.g_y, 16)

                    def pair(i):
                        for e in range(2):
                            wait(sp, m.g_b_mm, i * 6 + 3 * e - 3)
                            f = i * 2 + e
                            for n in range(3):
                                sp.dma_start(wg[:, e, n], w_g[:, n, :, ds(f * P, P)]).then_inc(land[e], 16)
                            sp.dma_start(wb[:, e], w_br[:, :, ds(f * P, P)]).then_inc(land[e], 16)
                    run(sp, pair)

                @block.tensor
                def _(pe):
                    pe.wait_ge(m.g_h, 16 * KT)

                    def pair(i):
                        for e in range(2):
                            pe.wait_ge(land[e], i * 64 + 64)
                            for n in range(3):
                                b = (3 * e + n) % 2
                                t = i * 6 + 3 * e + n
                                wait(pe, m.g_gs, t - 1)
                                for o, sl in ((pg_s[:, b, :], slice(0, TS)), (pg_p[:, b, 0:TP], slice(TS, N))):
                                    for k in range(KT):
                                        last = nc.tensor.matmul(o, wg[:, e, n, k, :], hT[:, k, sl], start=(k == 0), stop=(k == KT - 1))
                                last.then_inc(m.g_g_mm, 1)
                                if isinstance(t, int) and t == 0:
                                    pe.wait_ge(m.g_y, 16)
                                wait(pe, m.g_pr, t - 1)
                                for o, sl in ((pb_s[:, b, :], slice(0, TS)), (pb_p[:, b, 0:TP], slice(TS, N))):
                                    for k in range(MT):
                                        last = nc.tensor.matmul(o, wb[:, e, n * MT + k, :], yT[:, n, k, sl],
                                                                start=(k == 0), stop=(k == MT - 1))
                                last.then_inc(m.g_b_mm, 1)
                    run(pe, pair)

                @block.scalar
                def _(act):
                    def pair(i):
                        for j in range(6):
                            t, b = i * 6 + j, j % 2
                            act.wait_ge(m.g_g_mm, t + 1)
                            wait(act, m.g_pr, t - 1)
                            nc.scalar.activation(gs[:, b, 0:TS], pg_s[:, b, :], ACT.Sigmoid)
                            nc.scalar.activation(gs[:, b, TS:N], pg_p[:, b, 0:TP], ACT.Sigmoid).then_inc(m.g_gs, 1)
                    run(act, pair)

                @block.vector
                def _(dve):
                    def pair(i):
                        for j in range(6):
                            t, b = i * 6 + j, j % 2
                            dve.wait_ge(m.g_b_mm, t + 1)
                            dve.wait_ge(m.g_gs, t + 1)
                            wait(dve, m.g_sum, t - 1)
                            nc.vector.tensor_tensor(pr[:, b, 0:TS], gs[:, b, 0:TS], pb_s[:, b, :], ALU.mult)
                            nc.vector.tensor_tensor(pr[:, b, TS:N], gs[:, b, TS:N], pb_p[:, b, 0:TP],
                                                    ALU.mult).then_inc(m.g_pr, 1)
                    run(dve, pair)

                @block.gpsimd
                def _(pool):
                    def pair(i):
                        for e in range(2):
                            o = mT[:, ds(i * 2 + e, 1), :].rearrange("p a c -> p (a c)")
                            for n in range(3):
                                t, b = i * 6 + 3 * e + n, (3 * e + n) % 2
                                pool.wait_ge(m.g_pr, t + 1)
                                wait(pool, m.g_sum, t)
                                nc.gpsimd.tensor_tensor(scr[:, 0:1], scr[:, 1:2], scr[:, 1:2], ALU.add)
                                if n == 0:
                                    nc.gpsimd.tensor_copy(o, pr[:, b, :]).then_inc(m.g_sum, 1)
                                else:
                                    nc.gpsimd.tensor_tensor(o, o, pr[:, b, :], ALU.add).then_inc(m.g_sum, 1)
                    nc.gpsimd.memset(scr[:], 0.0).then_inc(m.g_scr, 1)
                    pool.wait_ge(m.g_scr, 1)
                    run(pool, pair)

        with ExitStack() as c2:
            def sb3(name, shape):
                return c2.enter_context(nc.sbuf_tensor(name, shape, F32))
            wo = sb3("mg_wo", [P, FT, D])
            g1 = sb3("mg_g1", [P, 2, D])
            lng, lnb = sb3("mg_lng", [P, D]), sb3("mg_lnb", [P, D])
            tp = sb3("mg_tp", [P, 2, D])
            st = sb3("mg_st", [P, NT, 2, 6])
            mv = sb3("mg_mv", [P, NT, 4])
            ps_o = c2.enter_context(nc.psum_tensor("ps_mo", [P, 2, D], F32))
            ps_t = c2.enter_context(nc.psum_tensor("ps_mtr", [P, 2, D], F32))
            (m.o_w, m.o_x, m.o_g, m.o_mm, m.o_dve, m.o_sq, m.o_nrm, m.o_ln, m.o_t_mm, m.o_ht, m.o_tp, m.o_pl, m.o_sqv) = sems(
                nc, m, "o_w o_x o_g o_mm o_dve o_sq o_nrm o_ln o_t_mm o_ht o_tp o_pl o_sqv")
            with nc.Block() as block:

                @block.sync
                def _(sp):
                    sp.dma_start(wo[:], a["w_out"].rearrange("(k p) d -> p k d", p=P)).then_inc(m.o_w, 16)
                    sp.dma_start(m.x1[:, 0:NT - 1], a["x_sample"].rearrange("(t p) d -> p t d", p=P)).then_inc(m.o_x, 16)
                    sp.dma_start(m.x1[:, NT - 1], a["x_prompt"]).then_inc(m.o_x, 16)

                @block.scalar
                def _(act):
                    for c in range(2):
                        act.dma_start(g1[:, c], m.mods_dram[c, GATE1 * D:(GATE1 + 1) * D].partition_broadcast(P)).then_inc(m.o_g, 16)
                    act.dma_start(lng[:], a["ln1_g"].partition_broadcast(P)).then_inc(m.o_g, 16)
                    act.dma_start(lnb[:], a["ln1_b"].partition_broadcast(P)).then_inc(m.o_g, 16)

                    def turned(t):
                        c = t // (NT - 1)
                        act.wait_ge(m.o_t_mm, t + 1)
                        for k in range(KT):
                            last = nc.scalar.activation(m.h2T[:, k, t * P:(t + 1) * P], ps_t[:, t % 2, k * P:(k + 1) * P],
                                                        ACT.Identity, scale=m.modT[:, 3, k, c:c + 1], bias=m.modT[:, 2, k, c:c + 1])
                        last.then_inc(m.o_ht, 1)
                    for t in range(NT):
                        act.wait_ge(m.o_sqv, t + 1)
                        nc.scalar.activation(mv[:, t, 3:4], mv[:, t, 2:3], ACT.Sqrt).then_inc(m.o_sq, 1)
                        if t:
                            turned(t - 1)
                    turned(NT - 1)

                @block.tensor
                def _(pe):
                    pe.wait_ge(m.o_w, 16)

                    def turn(t):
                        pe.wait_ge(m.o_ln, t + 1)
                        if t >= 2:
                            pe.wait_ge(m.o_ht, t - 1)
                        for k in range(KT):
                            last = nc.tensor.transpose(ps_t[:, t % 2, k * P:(k + 1) * P], m.x1[:, t, k * P:(k + 1) * P], m.ident[:])
                        last.then_inc(m.o_t_mm, 1)
                    for t in range(NT):
                        if t >= 2:
                            pe.wait_ge(m.o_tp, t - 1)
                        for h in range(2):
                            for k in range(FT):
                                last = nc.tensor.matmul(ps_o[:, t % 2, ts512(h)], mT[:, k, t * P:(t + 1) * P], wo[:, k, ts512(h)],
                                                        start=(k == 0), stop=(k == FT - 1))
                        last.then_inc(m.o_mm, 1)
                        if t:
                            turn(t - 1)
                    turn(NT - 1)

                @block.vector
                def _(dve):
                    V = nc.vector
                    link = Chain(dve, m.o_dve)
                    dve.wait_ge(m.o_x, 32)
                    dve.wait_ge(m.o_g, 64)
                    for t in range(NT):
                        x, c = m.x1[:, t], t // (NT - 1)
                        dve.wait_ge(m.o_mm, t + 1)
                        V.tensor_tensor(tp[:, t % 2], ps_o[:, t % 2], g1[:, c], ALU.mult).then_inc(m.o_tp, 1)
                        dve.wait_ge(m.o_tp, t + 1)
                        link(V.scalar_tensor_tensor(x, x, ALPHA, tp[:, t % 2], ALU.mult, ALU.add))
                        norm_stats(V, dve, link, m, x, st[:, t], mv[:, t], m.o_sqv, m.o_sq, t)
                        V.tensor_scalar(x, x, mv[:, t, 0:1], mv[:, t, 3:4], ALU.subtract, ALU.mult).then_inc(m.o_nrm, 1)

                @block.gpsimd
                def _(pool):
                    for t in range(NT):
                        x = m.x1[:, t]
                        pool.wait_ge(m.o_nrm, t + 1)
                        nc.gpsimd.tensor_tensor(x, x, lng[:], ALU.mult).then_inc(m.o_pl, 1)
                        pool.wait_ge(m.o_pl, t + 1)
                        nc.gpsimd.tensor_tensor(x, x, lnb[:], ALU.add).then_inc(m.o_ln, 1)


def norm_stats(V, dve, link, m, x, st, mv, sqv, sq, t):
    V.bn_stats(st[:, 0], x[:, 0:512])
    link(V.bn_stats(st[:, 1], x[:, 512:1024]))
    link(V.bn_aggr(mv[:, 0:2], st.rearrange("p s c -> p (s c)")))
    V.tensor_scalar_add(mv[:, 2:3], mv[:, 1:2], LN_EPS).then_inc(sqv, 1)
    dve.wait_ge(sq, t + 1)
    link(V.reciprocal(mv[:, 3:4], mv[:, 3:4]))


def router_phase(nc, m, a):
    GE = E_N // EGROUPS
    with ExitStack() as ctx:
        def sb(name, shape):
            return ctx.enter_context(nc.sbuf_tensor(name, shape, F32))
        rw = sb("ro_w", [P, KT, E_N])
        rb = sb("ro_b", [P, E_N])
        sc, sel, rep = sb("ro_sc", [P, NT, E_N]), sb("ro_sel", [P, NT, E_N]), sb("ro_rep", [P, NT, E_N])
        m8 = sb("ro_m8", [P, NT, EGROUPS, 8])
        top = sb("ro_top", [P, NT, 8])
        grp, rank = sb("ro_grp", [P, NT, EGROUPS]), sb("ro_rank", [P, NT, EGROUPS])
        gt, eq = sb("ro_gt", [P, NT, EGROUPS, EGROUPS]), sb("ro_eq", [P, NT, EGROUPS, EGROUPS])
        low = sb("ro_low", [P, EGROUPS, EGROUPS])
        sm = sb("ro_sum", [P, NT])
        ps = ctx.enter_context(nc.psum_tensor("ps_ro", [P, NT, E_N], F32))
        (m.t_w, m.t_b, m.t_mm, m.t_sc, m.t_low, m.t_dve) = sems(
            nc, m, "t_w t_b t_mm t_sc t_low t_dve")
        with nc.Block() as block:

            @block.sync
            def _(sp):
                sp.dma_start(rw[:], a["router_w"].rearrange("(k p) e -> p k e", p=P)).then_inc(m.t_w, 16)
                sp.dma_start(rb[:], a["router_bias"].partition_broadcast(P)).then_inc(m.t_b, 16)

            @block.gpsimd
            def _(pool):
                nc.gpsimd.memset(low[:], 1.0).then_inc(m.t_low, 1)
                pool.wait_ge(m.t_low, 1)
                nc.gpsimd.affine_select(out=low[:], in_=low[:], compare_op=ALU.is_ge, fill=0.0, base=-1,
                                        pattern=[[1, EGROUPS], [-1, EGROUPS]], channel_multiplier=0).then_inc(m.t_low, 1)

            @block.tensor
            def _(pe):
                pe.wait_ge(m.t_w, 16)
                for t in range(NT):
                    for k in range(KT):
                        last = nc.tensor.matmul(ps[:, t, :], m.h2T[:, k, t * P:(t + 1) * P], rw[:, k, :], start=(k == 0), stop=(k == KT - 1))
                last.then_inc(m.t_mm, 1)

            @block.scalar
            def _(act):
                act.wait_ge(m.t_mm, 1)
                nc.scalar.activation(sc[:], ps[:], ACT.Sigmoid).then_inc(m.t_sc, 1)

            @block.vector
            def _(dve):
                V = nc.vector
                link = Chain(dve, m.t_dve)
                dve.wait_ge(m.t_sc, 1)
                dve.wait_ge(m.t_b, 16)
                link(V.tensor_tensor(sel[:], sc[:], rb[:].unsqueeze(1).to_broadcast([P, NT, E_N]), ALU.add))
                for t in range(NT):
                    for g in range(EGROUPS):
                        last = V.max(m8[:, t, g], sel[:, t, g * GE:(g + 1) * GE])
                link(last)
                link(V.tensor_tensor(grp[:], m8[:, :, :, 0], m8[:, :, :, 1], ALU.add))
                dve.wait_ge(m.t_low, 2)
                for t in range(NT):
                    gj = grp[:, t].unsqueeze(1).to_broadcast([P, EGROUPS, EGROUPS])
                    gi = grp[:, t].unsqueeze(2).to_broadcast([P, EGROUPS, EGROUPS])
                    V.tensor_tensor(gt[:, t], gj, gi, ALU.is_gt)
                    last = V.tensor_tensor(eq[:, t], gj, gi, ALU.is_equal)
                link(last)
                link(V.tensor_tensor(eq[:], eq[:], low[:].unsqueeze(1).to_broadcast([P, NT, EGROUPS, EGROUPS]), ALU.mult))
                link(V.tensor_tensor(gt[:], gt[:], eq[:], ALU.add))
                link(V.tensor_reduce(rank[:], gt[:], AX.X, ALU.add))
                link(V.tensor_scalar(rank[:], rank[:], TOPG - 0.5, None, ALU.is_lt))
                rk = rank[:].unsqueeze(3).to_broadcast([P, NT, EGROUPS, GE])
                s4 = sel[:].rearrange("p t (g e) -> p t g e", g=EGROUPS)
                link(V.tensor_tensor(s4, s4, rk, ALU.mult))
                link(V.tensor_scalar(rank[:], rank[:], -1.0, -NEG, ALU.add, ALU.mult))
                link(V.tensor_tensor(s4, s4, rk, ALU.add))
                for t in range(NT):
                    last = V.max(top[:, t], sel[:, t])
                link(last)
                for t in range(NT):
                    last = V.match_replace(rep[:, t], top[:, t], sel[:, t], 3.0 * NEG)
                link(last)
                link(V.tensor_scalar(rep[:], rep[:], 2.0 * NEG, None, ALU.is_lt))
                link(V.tensor_tensor(rep[:], rep[:], sc[:], ALU.mult))
                link(V.tensor_reduce(sm[:], rep[:], AX.X, ALU.add))
                link(V.reciprocal(sm[:], sm[:]))
                link(V.tensor_scalar(sm[:], sm[:], ROUTED_SCALE, None, ALU.mult))
                link(V.tensor_tensor(m.gates[:], rep[:], sm[:].unsqueeze(2).to_broadcast([P, NT, E_N]), ALU.mult))


def moe_phase(nc, m, a):
    with ExitStack() as ctx:
        def sb(name, shape):
            return ctx.enter_context(nc.sbuf_tensor(name, shape, F32))
        wg, wu = sb("me_wg", [P, 2, KT, E_F]), sb("me_wu", [P, 2, KT, E_F])
        wd = sb("me_wd", [P, 2, D])
        sg = sb("me_sg", [P, 2, N])
        hh = sb("me_hh", [P, 2, N])
        acc = sb("me_acc", [P, NT, D])
        g2 = sb("me_g2", [P, 2, D])
        lng, lnb = sb("me_lng", [P, D]), sb("me_lnb", [P, D])
        st = sb("me_st", [P, NT, 2, 6])
        mv = sb("me_mv", [P, NT, 4])
        pg, pu = (ctx.enter_context(nc.psum_tensor(x, [P, 2, 512], F32)) for x in ("ps_eg", "ps_eu"))
        pd = ctx.enter_context(nc.psum_tensor("ps_ed", [P, 2, D], F32))
        (m.e_wg0, m.e_wg1, m.e_wd0, m.e_wd1, m.e_up, m.e_sg, m.e_hh, m.e_dn, m.e_acc, m.e_g, m.e_dve, m.e_sqv,
         m.e_sq, m.e_nrm, m.e_pl, m.e_ln, m.e_out) = sems(
            nc, m, "e_wg0 e_wg1 e_wd0 e_wd1 e_up e_sg e_hh e_dn e_acc e_g e_dve e_sqv e_sq e_nrm e_pl e_ln e_out")
        lg, ld = [m.e_wg0, m.e_wg1], [m.e_wd0, m.e_wd1]
        gate_w = a["exp_w_gate"].rearrange("e (k p) f -> e p k f", p=P)
        up_w = a["exp_w_up"].rearrange("e (k p) f -> e p k f", p=P)

        def run(eng, item):
            item(0, 0)
            item(1, 1)
            item(2, 0)
            with eng.Fori(1, E_N // 2) as j:
                item(j * 2 + 1, 1)
                item(j * 2 + 2, 0)

        with nc.Block() as block:

            @block.sync
            def _(sp):
                def item(n, b):
                    wait(sp, m.e_up, n - 1)
                    if isinstance(n, int) and n == 0:
                        sp.dma_start(wg[:, b], a["sh_w_gate"].rearrange("(k p) f -> p k f", p=P)).then_inc(lg[b], 16)
                        sp.dma_start(wu[:, b], a["sh_w_up"].rearrange("(k p) f -> p k f", p=P)).then_inc(lg[b], 16)
                    else:
                        sp.dma_start(wg[:, b], gate_w[ds(n - 1, 1)].rearrange("e p k f -> p (e k) f")).then_inc(lg[b], 16)
                        sp.dma_start(wu[:, b], up_w[ds(n - 1, 1)].rearrange("e p k f -> p (e k) f")).then_inc(lg[b], 16)
                run(sp, item)

            @block.gpsimd
            def _(pool):
                def item(n, b):
                    wait(pool, m.e_dn, (n - 1) * NT)
                    if isinstance(n, int) and n == 0:
                        pool.dma_start(wd[:, b], a["sh_w_down"]).then_inc(ld[b], 16)
                    else:
                        pool.dma_start(wd[:, b], a["exp_w_down"][ds(n - 1, 1)].rearrange("e f d -> f (e d)")).then_inc(ld[b], 16)
                run(pool, item)
                for t in range(NT):
                    x = acc[:, t]
                    pool.wait_ge(m.e_nrm, t + 1)
                    nc.gpsimd.tensor_tensor(x, x, lng[:], ALU.mult).then_inc(m.e_pl, 1)
                    pool.wait_ge(m.e_pl, t + 1)
                    nc.gpsimd.tensor_tensor(x, x, lnb[:], ALU.add).then_inc(m.e_ln, 1)
                    pool.wait_ge(m.e_ln, t + 1)
                    o = a["y_prompt"] if t == NT - 1 else a["y_sample"][t * P:(t + 1) * P, :]
                    pool.dma_start(o, x).then_inc(m.e_out, 16)
                pool.wait_ge(m.e_out, 16 * NT)

            @block.tensor
            def _(pe):
                def up(n, b):
                    pe.wait_ge(lg[b], (n - b) * 16 + 32)
                    wait(pe, m.e_sg, n)
                    wait(pe, m.e_hh, n)
                    for ps, w in ((pg, wg), (pu, wu)):
                        for o, sl in ((ps[:, 0, :], slice(0, TS)), (ps[:, 1, 0:TP], slice(TS, N))):
                            for k in range(KT):
                                last = nc.tensor.matmul(o, w[:, b, k, :], m.h2T[:, k, sl], start=(k == 0), stop=(k == KT - 1))
                    last.then_inc(m.e_up, 1)

                def down(n, b):
                    pe.wait_ge(ld[b], (n - b) * 8 + 16)
                    pe.wait_ge(m.e_hh, n + 1)
                    for t in range(NT):
                        s = (b * NT + t) % 2
                        wait(pe, m.e_acc, n * NT + t - 1)
                        for h in range(2):
                            last = nc.tensor.matmul(pd[:, s, ts512(h)], hh[:, b, t * P:(t + 1) * P], wd[:, b, ts512(h)],
                                                    start=True, stop=True)
                        last.then_inc(m.e_dn, 1)
                up(0, 0)
                up(1, 1)
                down(0, 0)
                up(2, 0)
                down(1, 1)
                with pe.Fori(1, E_N // 2) as j:
                    up(j * 2 + 1, 1)
                    down(j * 2, 0)
                    up(j * 2 + 2, 0)
                    down(j * 2 + 1, 1)
                down(E_N, 0)

            @block.scalar
            def _(act):
                for c in range(2):
                    act.dma_start(g2[:, c], m.mods_dram[c, GATE2 * D:(GATE2 + 1) * D].partition_broadcast(P)).then_inc(m.e_g, 16)
                act.dma_start(lng[:], a["ln2_g"].partition_broadcast(P)).then_inc(m.e_g, 16)
                act.dma_start(lnb[:], a["ln2_b"].partition_broadcast(P)).then_inc(m.e_g, 16)

                def item(n, b):
                    act.wait_ge(m.e_up, n + 1)
                    wait(act, m.e_hh, n - 1)
                    nc.scalar.activation(sg[:, b, 0:TS], pg[:, 0, :], ACT.Silu)
                    nc.scalar.activation(sg[:, b, TS:N], pg[:, 1, 0:TP], ACT.Silu).then_inc(m.e_sg, 1)
                run(act, item)
                for t in range(NT):
                    act.wait_ge(m.e_sqv, t + 1)
                    nc.scalar.activation(mv[:, t, 3:4], mv[:, t, 2:3], ACT.Sqrt).then_inc(m.e_sq, 1)

            @block.vector
            def _(dve):
                V = nc.vector

                def mul(n, b):
                    dve.wait_ge(m.e_sg, n + 1)
                    wait(dve, m.e_dn, (n - 1) * NT)
                    V.tensor_tensor(hh[:, b, 0:TS], sg[:, b, 0:TS], pu[:, 0, :], ALU.mult)
                    V.tensor_tensor(hh[:, b, TS:N], sg[:, b, TS:N], pu[:, 1, 0:TP], ALU.mult).then_inc(m.e_hh, 1)

                def add(n, b):
                    for t in range(NT):
                        s = (b * NT + t) % 2
                        dve.wait_ge(m.e_dn, n * NT + t + 1)
                        if isinstance(n, int) and n == 0:
                            V.tensor_copy(acc[:, t], pd[:, s]).then_inc(m.e_acc, 1)
                        else:
                            wait(dve, m.e_acc, (n - 1) * NT + t + 1)
                            V.scalar_tensor_tensor(acc[:, t], pd[:, s], m.gates[:, t, ds(n - 1, 1)], acc[:, t],
                                                   ALU.mult, ALU.add).then_inc(m.e_acc, 1)
                mul(0, 0)
                mul(1, 1)
                add(0, 0)
                mul(2, 0)
                add(1, 1)
                with dve.Fori(1, E_N // 2) as j:
                    mul(j * 2 + 1, 1)
                    add(j * 2, 0)
                    mul(j * 2 + 2, 0)
                    add(j * 2 + 1, 1)
                add(E_N, 0)
                link = Chain(dve, m.e_dve)
                dve.wait_ge(m.e_g, 64)
                dve.wait_ge(m.e_acc, (E_N + 1) * NT)
                for t in range(NT):
                    x, c = acc[:, t], t // (NT - 1)
                    link(V.tensor_tensor(x, x, g2[:, c], ALU.mult))
                    link(V.scalar_tensor_tensor(x, m.x1[:, t], ALPHA, x, ALU.mult, ALU.add))
                    norm_stats(V, dve, link, m, x, st[:, t], mv[:, t], m.e_sqv, m.e_sq, t)
                    V.tensor_scalar(x, x, mv[:, t, 0:1], mv[:, t, 3:4], ALU.subtract, ALU.mult).then_inc(m.e_nrm, 1)


STOP_AFTER = None


def build(nc, a):
    m = Mem()
    a["w_in_t"] = a["w_in"].rearrange("(k p) n -> p k n", p=P)
    m.mods_dram = nc.dram_tensor("mods_dram", [2, 6 * D], F32).ap()
    m.h1_dram = nc.dram_tensor("h1_dram", [KT, P, N], F32).ap()
    m.y_dram = nc.dram_tensor("y_dram", [3, P, MT, N], F32).ap()
    with ExitStack() as ctx:
        m.phase_sems = []
        def sb(stack, name, shape):
            return stack.enter_context(nc.sbuf_tensor(name, shape, F32))

        m.ident = sb(ctx, "ident", [P, P])
        m.pcol = sb(ctx, "pcol", [P, NPCOL])
        m.modT = sb(ctx, "modT", [P, 4, KT, 2])
        m.c_silu = sb(ctx, "c_silu", [P, KT, 2])
        m.s_win = [ctx.enter_context(nc.semaphore(f"s_win{r}")) for r in range(4)]
        with ExitStack() as mixer:
            m.zr = sb(mixer, "zr", [P, RT, ZW])
            with ExitStack() as branches:
                m.yb = sb(branches, "yb", [P, MT, N])
                m.yc = sb(branches, "yc", [P, MT, N])
                with ExitStack() as mid:
                    m.z = sb(mid, "z", [P, 3 * MT, ZW])
                    m.zv = sb(mid, "zv", [P, NT, MIX])
                    with ExitStack() as front:
                        m.hT = sb(front, "hT", [P, KT, N])
                        m.w_ada_sb = sb(front, "w_ada_sb", [P, 2, KT, 512])
                        m.w_in_sb = sb(front, "w_in_sb", [P, 4, KT, P])
                        m.mods = sb(front, "mods", [2, 6 * D])
                        setup_phase(nc, m, a)
                        inproj_phase(nc, m, a)
                    if STOP_AFTER == "inproj":
                        return
                    clear_sems(nc, m)
                    attention_phase(nc, m, a)
                    if STOP_AFTER == "attention":
                        return
                clear_sems(nc, m)
                s5_phase(nc, m, a)
                if STOP_AFTER == "s5":
                    return
            clear_sems(nc, m)
            rwkv_phase(nc, m, a)
            if STOP_AFTER == "rwkv":
                return
        with ExitStack() as tail:
            m.x1 = sb(tail, "x1", [P, NT, D])
            m.h2T = sb(tail, "h2T", [P, KT, N])
            m.gates = sb(tail, "gates", [P, NT, E_N])
            clear_sems(nc, m)
            merge_phase(nc, m, a)
            if STOP_AFTER == "merge":
                return
            clear_sems(nc, m)
            router_phase(nc, m, a)
            if STOP_AFTER == "router":
                return
            clear_sems(nc, m)
            moe_phase(nc, m, a)


_INS = {
    "x_prompt": (TP, D), "x_sample": (TS, D), "c": (1, D), "cache_na_k": (HEADS, 128, HD),
    "cache_na_v": (HEADS, 128, HD), "state_rwkv": (2, HEADS, HD, HD), "state_s5_re": (2, 32, 64),
    "state_s5_im": (2, 32, 64), "c_ctx": (D,), "w_ada": (D, 6 * D), "b_ada": (6 * D,), "w_in": (D, GCOL + 3 * D),
    "rwkv_mu": (ACOLS,), "rwkv_w0": (2, MIX), "rwkv_w2": (128, MIX), "rwkv_a0": (2, MIX), "rwkv_a2": (128, MIX),
    "rwkv_g2": (128, MIX), "rwkv_kk": (MIX,), "rwkv_ka": (MIX,), "rwkv_rk": (MIX,), "rwkv_gn_g": (MIX,),
    "rwkv_gn_b": (MIX,), "na_rpb": (HEADS * NDR, NDC), "s5_a_re": (2, 32, 64), "s5_a_im": (2, 32, 64),
    "s5_log_dt": (2, 32), "s5_b_re": (32, 64, 16), "s5_b_im": (32, 64, 16), "s5_c_re": (32, 16, 64),
    "s5_c_im": (32, 16, 64), "s5_d": (MIX,), "s5_w_glu": (MIX, MIX), "s5_b_glu": (MIX,), "w_branch": (3, MIX, D),
    "w_out": (D, D), "ln1_g": (D,), "ln1_b": (D,), "router_w": (D, E_N), "router_bias": (E_N,),
    "exp_w_gate": (E_N, D, E_F), "exp_w_up": (E_N, D, E_F), "exp_w_down": (E_N, E_F, D), "sh_w_gate": (D, E_F),
    "sh_w_up": (D, E_F), "sh_w_down": (E_F, D), "ln2_g": (D,), "ln2_b": (D,),
}
_OUTS = {"y_prompt": (TP, D), "y_sample": (TS, D), "new_k": (HEADS, TP, HD), "new_v": (HEADS, TP, HD),
         "new_rwkv": (2, HEADS, HD, HD), "new_s5_re": (2, 32, 64), "new_s5_im": (2, 32, 64)}
_RETURNED = {"y_prompt": (1, TP, D), "y_sample": (1, TS, D), "new_k": (1, 1, HEADS, TP, HD),
             "new_v": (1, 1, HEADS, TP, HD), "new_rwkv": (1, 1, 2, HEADS, HD, HD), "new_s5_re": (1, 1, 2, 32, 64),
             "new_s5_im": (1, 1, 2, 32, 64)}


def kernel(**inputs):
    import numpy as np
    import concourse.bacc as bacc
    from concourse.bass_utils import run_bass_kernel_spmd

    nc = bacc.Bacc("TRN2", target_bir_lowering=False, num_devices=1)
    arrays, a = {}, {}
    for name, shape in _INS.items():
        arrays["in_" + name] = np.ascontiguousarray(inputs[name]).reshape(shape)
        a[name] = nc.dram_tensor("in_" + name, shape, F32, kind="ExternalInput").ap()
    for name, shape in _OUTS.items():
        a[name] = nc.dram_tensor("out_" + name, shape, F32, kind="ExternalOutput").ap()
    build(nc, a)
    r = run_bass_kernel_spmd(nc, [arrays], core_ids=[0])
    return tuple(np.asarray(r.results[0]["out_" + name]).reshape(_RETURNED[name]) for name in _OUTS)
```

```python
from contextlib import ExitStack

import concourse.bass as bass
from concourse import mybir
from concourse.alu_op_type import AluOpType as ALU

F32 = mybir.dt.float32
F32R = mybir.dt.float32r
I32 = mybir.dt.int32
U32 = mybir.dt.uint32
ACT = mybir.ActivationFunctionType
AX = mybir.AxisListType
ds = bass.ds

P = 128
D = 1024
KT = D // P
TS, TP = 512, 128
N = TS + TP
NT = N // P
MIX = 512
MT = MIX // P
HEADS, HD = 8, 64
ACOLS = 3 * MIX + 2 * 64 + 2 * 64 + 128
RT = ACOLS // P
QCOL, KCOL, VCOL, UCOL, GCOL = ACOLS, ACOLS + MIX, ACOLS + 2 * MIX, ACOLS + 3 * MIX, ACOLS + 4 * MIX
GRID_W, WIN_C, WIN_R = 64, 16, 8
GRID_H = TS // GRID_W
NDR, NDC = 2 * WIN_R - 1, 2 * WIN_C - 1
NEG = -1e30
ALPHA = 2.0 ** 0.25
LN_EPS, GN_EPS = 1e-5, 64e-5
E_N, E_F, TOPK = 64, 128, 8
EGROUPS, TOPG = 8, 4
ROUTED_SCALE = 2.5
ZS, ZP = 1, 515
ZW = 644
DECAY_C = 0.6065306597126334
PCOLS = {"c": (0, 8), "c_ctx": (8, 8), "rwkv_mu": (16, 15), "rwkv_w0": (31, 8), "rwkv_a0": (39, 8), "rwkv_kk": (47, 4),
         "rwkv_ka": (51, 4), "rwkv_rk": (55, 4), "s5_d": (59, 4), "s5_b_glu": (63, 4)}
NPCOL = 67
SHIFT1, SCALE1, GATE1, SHIFT2, SCALE2, GATE2 = range(6)


class Chain:

    def __init__(self, eng, sem, base=0):
        self.eng, self.sem, self.base, self.n = eng, sem, base, 0

    def __call__(self, ins):
        self.n += 1
        ins.then_inc(self.sem, 1)
        self.eng.wait_ge(self.sem, self.base + self.n)


class Mem:
    pass


def sems(nc, m, names):
    new = [nc.alloc_semaphore(name) for name in names.split()]
    m.phase_sems += new
    return new


def clear_sems(nc, m):
    nc.clear_and_free_semaphores(m.phase_sems)
    m.phase_sems = []
    nc.all_engine_barrier()


def ada_block(nc, m, slot, land, n):
    nc.tensor.wait_ge(land, n)
    for k in range(KT):
        last = nc.tensor.matmul(m.ps_mod[0:2, slot, :], m.c_silu[:, k, :], m.w_ada_sb[:, slot, k, :],
                                start=(k == 0), stop=(k == KT - 1))
    last.then_inc(m.s_mod_mm, 1)


def setup_phase(nc, m, a):
    with ExitStack() as ctx:
        x_sb = m.z[:].rearrange("p t c -> p (t c)")[:, 0:NT * D].rearrange("p (t d) -> p t d", t=NT)
        prow = ctx.enter_context(nc.sbuf_tensor("prow", [NPCOL, P], F32))
        ps_mod = ctx.enter_context(nc.psum_tensor("ps_mod0", [P, 2, 512], F32))
        ps_x = ctx.enter_context(nc.psum_tensor("ps_x", [P, 2, 512], F32))
        ps_xp = ctx.enter_context(nc.psum_tensor("ps_xp", [P, 2, 512], F32))
        ps_mt = ctx.enter_context(nc.psum_tensor("ps_mt", [P, 512], F32))
        m.ps_mod = ps_mod
        (m.s_x, m.s_c, m.s_b_ada, m.s_wa0, m.s_wa1, m.s_mod_mm, m.s_mod_sb, m.s_ident, m.s_silu, m.s_xt_mm,
         m.s_xt_sb, m.s_modt_mm, m.s_dve_a, m.s_h_spill, m.s_ht, m.s_pcol, m.s_pcol_mm) = sems(
            nc, m, "s_x s_c s_b_ada s_wa0 s_wa1 s_mod_mm s_mod_sb s_ident s_silu s_xt_mm s_xt_sb s_modt_mm s_dve_a s_h_spill "
            "s_ht s_pcol s_pcol_mm")
        w_ada = a["w_ada"].rearrange("(k p) n -> p k n", p=P)
        land = [m.s_wa0, m.s_wa1]
        with nc.Block() as block:

            @block.sync
            def _(sp):
                for j in range(4):
                    if j >= 2:
                        sp.wait_ge(m.s_mod_mm, j - 1)
                    sp.dma_start(m.w_ada_sb[:, j % 2], w_ada[:, :, ts512(j)]).then_inc(land[j % 2], 16)
                for t in range(2):
                    sp.dma_start(m.w_in_sb[:, t], a["w_in_t"][:, :, t * P:(t + 1) * P]).then_inc(m.s_win[t], 16)
                sp.wait_ge(m.s_ht, 8 * 2)
                sp.dma_start(m.h1_dram.rearrange("k p n -> p k n"), m.hT[:]).then_inc(m.s_h_spill, 16)
                sp.wait_ge(m.s_h_spill, 16)

            @block.scalar
            def _(act):
                for name, (c0, n) in PCOLS.items():
                    v = a[name]
                    v = v.rearrange("o n -> (o n)") if len(v.shape) == 2 else v
                    act.dma_start(prow[c0:c0 + n, :], v.rearrange("(k p) -> k p", p=P)).then_inc(m.s_c, 16)
                for t in range(NT - 1):
                    act.dma_start(x_sb[:, t], a["x_sample"][t * P:(t + 1) * P, :]).then_inc(m.s_x, 16)
                act.dma_start(x_sb[:, NT - 1], a["x_prompt"]).then_inc(m.s_x, 16)
                act.dma_start(m.mods[0:1], a["b_ada"].unsqueeze(0)).then_inc(m.s_b_ada, 16)
                act.dma_start(m.mods[1:2], a["b_ada"].unsqueeze(0)).then_inc(m.s_b_ada, 16)
                for t in range(2, 4):
                    act.dma_start(m.w_in_sb[:, t], a["w_in_t"][:, :, t * P:(t + 1) * P]).then_inc(m.s_win[t], 16)
                act.wait_ge(m.s_pcol, 1)
                nc.scalar.activation(m.c_silu[:], m.pcol[:, 0:2 * KT].rearrange("p (c k) -> p k c", c=2), ACT.Silu).then_inc(m.s_silu, 1)
                for k in range(KT):
                    act.wait_ge(m.s_xt_mm, k + 1)
                    nc.scalar.activation(m.hT[:, k, 0:TS], ps_x[:, k % 2, :], ACT.Identity)
                    nc.scalar.activation(m.hT[:, k, TS:N], ps_xp[:, k % 2, 0:TP],
                                         ACT.Identity).then_inc(m.s_xt_sb, 1)

            @block.gpsimd
            def _(pool):
                nc.gpsimd.memset(m.ident[:], 0.0).then_inc(m.s_ident, 1)
                pool.wait_ge(m.s_ident, 1)
                nc.gpsimd.affine_select(out=m.ident[:], in_=m.ident[:], compare_op=ALU.not_equal, fill=1.0, base=0,
                                        pattern=[[-1, P]], channel_multiplier=1).then_inc(m.s_ident, 1)

            @block.tensor
            def _(pe):
                pe.wait_ge(m.s_ident, 2)
                pe.wait_ge(m.s_c, 16 * len(PCOLS))
                nc.tensor.transpose(ps_mt[:, 128:128 + NPCOL], prow[:, :], m.ident[0:NPCOL, 0:NPCOL]).then_inc(m.s_pcol_mm, 1)
                pe.wait_ge(m.s_x, 16 * NT)
                for k in range(KT):
                    if k >= 2:
                        pe.wait_ge(m.s_xt_sb, k - 1)
                    for t in range(NT - 1):
                        nc.tensor.transpose(ps_x[:, k % 2, t * P:(t + 1) * P], x_sb[:, t, k * P:(k + 1) * P], m.ident[:])
                    nc.tensor.transpose(ps_xp[:, k % 2, 0:TP], x_sb[:, NT - 1, k * P:(k + 1) * P],
                                        m.ident[:]).then_inc(m.s_xt_mm, 1)
                pe.wait_ge(m.s_silu, 1)
                for j in range(4):
                    if j >= 2:
                        pe.wait_ge(m.s_mod_sb, j - 1)
                    ada_block(nc, m, j % 2, land[j % 2], 16 * (j // 2 + 1))
                pe.wait_ge(m.s_mod_sb, 4)
                for v in range(2):
                    for k in range(KT):
                        c0 = v * D + k * P
                        last = nc.tensor.transpose(ps_mt[:, (v * KT + k) * 2:(v * KT + k) * 2 + 2],
                                                   m.mods[0:2, c0:c0 + P], m.ident[0:2, 0:2])
                last.then_inc(m.s_modt_mm, 1)

            @block.vector
            def _(dve):
                dve.wait_ge(m.s_pcol_mm, 1)
                nc.vector.tensor_copy(m.pcol[:], ps_mt[:, 128:128 + NPCOL]).then_inc(m.s_pcol, 1)
                dve.wait_ge(m.s_b_ada, 32)
                for j in range(4):
                    dve.wait_ge(m.s_mod_mm, j + 1)
                    nc.vector.tensor_tensor(m.mods[0:2, ts512(j)], m.ps_mod[0:2, j % 2, :],
                                            m.mods[0:2, ts512(j)], ALU.add).then_inc(m.s_mod_sb, 1)
                link = Chain(dve, m.s_dve_a)
                dve.wait_ge(m.s_modt_mm, 1)
                pm = ps_mt[:, 0:4 * KT].rearrange("p (v k c) -> p v k c", v=2, c=2)
                nc.vector.tensor_copy(m.modT[:, 0], pm[:, 0])
                link(nc.vector.tensor_scalar_add(m.modT[:, 1], pm[:, 1], 1.0))
                for k in range(KT):
                    dve.wait_ge(m.s_xt_sb, k + 1)
                    for c, sl in ((0, slice(0, TS)), (1, slice(TS, N))):
                        nc.vector.tensor_scalar(m.hT[:, k, sl], m.hT[:, k, sl], m.modT[:, 1, k, c:c + 1],
                                                m.modT[:, 0, k, c:c + 1], ALU.mult, ALU.add).then_inc(m.s_ht, 1)


def ts512(j):
    return ds(j * 512, 512)


Z_TILES = RT + 3 * MT


def z_col(t):
    return t * P if t < RT + 2 * MT else t * P + MIX


def inproj_phase(nc, m, a):
    with ExitStack() as ctx:
        wv_sb = ctx.enter_context(nc.sbuf_tensor("wv_sb", [P, KT, MIX], F32))
        ps_s = ctx.enter_context(nc.psum_tensor("ps_s", [P, 2, 512], F32))
        ps_p = ctx.enter_context(nc.psum_tensor("ps_p", [P, 2, 512], F32))
        ps_v = ctx.enter_context(nc.psum_tensor("ps_v", [P, 1, 512], F32))
        ps_mod = ctx.enter_context(nc.psum_tensor("ps_mod1", [P, 2, 512], F32))
        kp_sb = m.yb[:, 0, 0:MIX]
        m.ps_mod = ps_mod
        (m.s_z_mm, m.s_z_act, m.s_z_dve, m.s_wv, m.s_v_mm, m.s_v_sb, m.s_wb0, m.s_wb1, m.s_mod_mm2, m.s_mod_sb2,
         m.s_kp_mm, m.s_kp_sb, m.s_out_kv, m.s_spill_mod) = sems(
            nc, m, "s_z_mm s_z_act s_z_dve s_wv s_v_mm s_v_sb s_wb0 s_wb1 s_mod_mm2 s_mod_sb2 s_kp_mm s_kp_sb s_out_kv "
            "s_spill_mod")
        w_ada = a["w_ada"].rearrange("(k p) n -> p k n", p=P)
        land = [m.s_wb0, m.s_wb1]
        m.s_mod_mm = m.s_mod_mm2

        def z_tile(t):
            return m.zr[:, t, :] if t < RT else m.z[:, t - RT, :]

        with nc.Block() as block:

            @block.sync
            def _(sp):
                for t in range(0, 23 - 4):
                    sp.wait_ge(m.s_z_mm, t + 1)
                    sp.dma_start(m.w_in_sb[:, t % 4], a["w_in_t"][:, :, (t + 4) * P:(t + 5) * P]).then_inc(m.s_win[t % 4], 16)
                for t in range(19, 23):
                    sp.wait_ge(m.s_z_mm, t + 1)
                    c0 = z_col(t + 4)
                    sp.dma_start(m.w_in_sb[:, t % 4], a["w_in_t"][:, :, c0:c0 + P]).then_inc(m.s_win[t % 4], 16)

            @block.gpsimd
            def _(pool):
                pool.dma_start(wv_sb[:], a["w_in_t"][:, :, VCOL:VCOL + MIX]).then_inc(m.s_wv, 16)
                for j in range(4, 12):
                    if j >= 6:
                        pool.wait_ge(m.s_mod_mm2, j - 5)
                    pool.dma_start(m.w_ada_sb[:, j % 2], w_ada[:, :, ts512(j)]).then_inc(land[j % 2], 16)
                pool.wait_ge(m.s_kp_sb, 1)
                pool.dma_start(a["new_k"].rearrange("h t d -> t h d"),
                               kp_sb.rearrange("p (h d) -> p h d", h=HEADS)).then_inc(m.s_out_kv, 16)
                pool.wait_ge(m.s_v_sb, NT)
                pool.dma_start(a["new_v"].rearrange("h t d -> t h d"),
                               m.zv[:, NT - 1].rearrange("p (h d) -> p h d", h=HEADS)).then_inc(m.s_out_kv, 16)
                pool.wait_ge(m.s_mod_sb2, 8)
                pool.dma_start(m.mods_dram, m.mods[0:2]).then_inc(m.s_spill_mod, 16)
                pool.wait_ge(m.s_out_kv, 32)
                pool.wait_ge(m.s_spill_mod, 16)

            @block.tensor
            def _(pe):
                def tile(t):
                    r, b = t % 4, t % 2
                    pe.wait_ge(m.s_win[r], 16 * (t // 4 + 1))
                    if t >= 2:
                        pe.wait_ge(m.s_z_act, t - 1)
                        pe.wait_ge(m.s_z_dve, t - 1)
                    for k in range(KT):
                        nc.tensor.matmul(ps_s[:, b, :], m.w_in_sb[:, r, k, :], m.hT[:, k, 0:TS],
                                         start=(k == 0), stop=(k == KT - 1))
                    for k in range(KT):
                        last = nc.tensor.matmul(ps_p[:, b, 0:TP], m.w_in_sb[:, r, k, :], m.hT[:, k, TS:N],
                                                start=(k == 0), stop=(k == KT - 1))
                    last.then_inc(m.s_z_mm, 1)

                for t in range(Z_TILES):
                    tile(t)
                pe.wait_ge(m.s_wv, 16)
                for t in range(NT):
                    if t >= 1:
                        pe.wait_ge(m.s_v_sb, t)
                    for k in range(KT):
                        last = nc.tensor.matmul(ps_v[:, 0, :], m.hT[:, k, t * P:(t + 1) * P], wv_sb[:, k, :],
                                                start=(k == 0), stop=(k == KT - 1))
                    last.then_inc(m.s_v_mm, 1)
                pe.wait_ge(m.s_z_dve, Z_TILES)
                for q in range(MT):
                    last = nc.tensor.transpose(ps_p[:, 0, q * P:(q + 1) * P], z_tile(RT + MT + q)[:, ZP:ZP + TP], m.ident[:])
                last.then_inc(m.s_kp_mm, 1)
                for j in range(4, 12):
                    if j >= 6:
                        pe.wait_ge(m.s_mod_sb2, j - 5)
                    ada_block(nc, m, j % 2, land[j % 2], 16 * (j // 2 - 1))

            @block.scalar
            def _(act):
                for t in range(Z_TILES):
                    act.wait_ge(m.s_z_mm, t + 1)
                    nc.scalar.activation(z_tile(t)[:, ZS:ZS + TS], ps_s[:, t % 2, :], ACT.Identity).then_inc(m.s_z_act, 1)
                for t in range(NT):
                    act.wait_ge(m.s_v_mm, t + 1)
                    nc.scalar.activation(m.zv[:, t], ps_v[:, 0, :], ACT.Identity).then_inc(m.s_v_sb, 1)
                act.wait_ge(m.s_kp_mm, 1)
                nc.scalar.activation(kp_sb, ps_p[:, 0, :], ACT.Identity).then_inc(m.s_kp_sb, 1)

            @block.vector
            def _(dve):
                for c0, c1 in ((0, ZS), (ZS + TS, ZP), (ZP + TP, ZW)):
                    nc.vector.memset(m.zr[:, 0:RT, c0:c1], 0.0)
                for t in range(Z_TILES):
                    dve.wait_ge(m.s_z_mm, t + 1)
                    nc.vector.tensor_copy(z_tile(t)[:, ZP:ZP + TP], ps_p[:, t % 2, 0:TP]).then_inc(m.s_z_dve, 1)
                for j in range(4, 12):
                    dve.wait_ge(m.s_mod_mm2, j - 3)
                    nc.vector.tensor_tensor(m.mods[0:2, ts512(j)], m.ps_mod[0:2, j % 2, :],
                                            m.mods[0:2, ts512(j)], ALU.add).then_inc(m.s_mod_sb2, 1)


def wait(eng, sem, v):
    if not isinstance(v, int) or v > 0:
        eng.wait_ge(sem, v)


ZQ, ZK, ZU = 0, MT, 2 * MT
NSLOT = NDR + 1


def attention_phase(nc, m, a):
    QT = TS // P
    SCALE = HD ** -0.5
    with ExitStack() as ctx:
        def sb(name, shape):
            return ctx.enter_context(nc.sbuf_tensor(name, shape, F32))

        def pb(name, shape):
            return ctx.enter_context(nc.psum_tensor(name, shape, F32))
        ck_sb = sb("ck_sb", [P, HEADS, HD])
        cv_sb = sb("cv_sb", [P, HEADS, HD])
        ckT = sb("ckT", [P, MT, P])
        rpb_in = sb("rpb_in", [HEADS * NDR, NDC])
        rpb_row = sb("rpb_row", [HEADS * NDR, 127])
        bias = sb("bias_tab", [P, HEADS, NSLOT, GRID_W])
        rev = sb("bias_rev", [GRID_W, HEADS, NDR, GRID_W])
        q_sb = sb("q_sb", [P, MT, P])
        s_sb = sb("s_sb", [P, 2, TS + P])
        p_sb = sb("p_sb", [P, 2, TS + P])
        pT_sb = sb("pT_sb", [P, 2, TS + P])
        nmax = sb("nmax", [P, 2])
        rsum = sb("rsum", [P, 2])
        rinv = sb("rinv", [P, 2])
        yb_sb = sb("yb_sb", [P, MIX])
        ps_s = pb("ps_as", [P, 2, TS])
        ps_c = pb("ps_ac", [P, 2, TS])[:, :, 0:P]
        ps_t5 = pb("ps_at5", [P, P])
        ps_t = pb("ps_at", [P, TS])
        ps_o = pb("ps_ao", [P, HD])
        ps_y = pb("ps_ay", [P, MT, P])
        rpb_dram = nc.dram_tensor("rpb_dram", [HEADS * NDR, 127], F32)
        (m.s_rpb, m.s_rpb0, m.s_rpbw, m.s_tab, m.s_tab_lo, m.s_tab_hi, m.s_ck, m.s_cv, m.s_ck_mm, m.s_ckT, m.s_q,
         m.s_sc, m.s_st, m.s_ex, m.s_tr, m.s_trA, m.s_trD, m.s_pv, m.s_o, m.s_rc, m.s_yt, m.s_yz, m.s_dve_b,
         m.s_pool_b) = sems(
            nc, m, "s_rpb s_rpb0 s_rpbw s_tab s_tab_lo s_tab_hi s_ck s_cv s_ck_mm s_ckT s_q s_sc s_st s_ex s_tr s_trA s_trD "
            "s_pv s_o s_rc s_yt s_yz s_dve_b s_pool_b")
        with nc.Block() as block:

            @block.sync
            def _(sp):
                sp.dma_start(ck_sb[:], a["cache_na_k"].rearrange("h t d -> t h d")).then_inc(m.s_ck, 16)
                sp.dma_start(rpb_in[:], a["na_rpb"]).then_inc(m.s_rpb, 16)
                sp.wait_ge(m.s_rpb0, 2)
                sp.dma_start(rpb_dram.ap(), rpb_row[:]).then_inc(m.s_rpbw, 16)
                sp.wait_ge(m.s_rpbw, 16)
                for h in range(HEADS):
                    src = bass.AP(rpb_dram, h * NDR * 127, [[1, GRID_W], [127, NDR], [1, GRID_W]])
                    sp.dma_start(rev[:, h], src).then_inc(m.s_tab, 16)
                sp.wait_ge(m.s_tab_lo, 1)
                sp.dma_start(bias[GRID_W:P, :, 1:NSLOT, :], bias[0:GRID_W, :, 0:NDR, :]).then_inc(m.s_tab_hi, 16)

            @block.gpsimd
            def _(pool):
                nc.gpsimd.memset(rpb_row[:], 0.0).then_inc(m.s_rpb0, 1)
                pool.wait_ge(m.s_rpb0, 1)
                pool.wait_ge(m.s_rpb, 16)
                nc.gpsimd.tensor_copy(rpb_row[:, 48:48 + NDC], rpb_in[:, ::-1]).then_inc(m.s_rpb0, 1)
                pool.dma_start(cv_sb[:], a["cache_na_v"].rearrange("h t d -> t h d")).then_inc(m.s_cv, 16)
                nc.gpsimd.tensor_copy(m.yc[:, :, 0:TS], m.z[:, ZU:ZU + MT, ZS:ZS + TS])
                nc.gpsimd.tensor_copy(m.yc[:, :, TS:N], m.z[:, ZU:ZU + MT, ZP:ZP + TP])
                pool.wait_ge(m.s_tab, 16 * HEADS)
                flat = rev[:].rearrange("p h r c -> p (h r) c")
                lo = flat[:, :, WIN_C:GRID_W]
                nc.gpsimd.affine_select(out=lo, in_=lo, compare_op=ALU.is_ge, fill=NEG, base=WIN_C // 2 + GRID_W - WIN_C - 1,
                                        pattern=[[0, HEADS * NDR], [-1, GRID_W - WIN_C]],
                                        channel_multiplier=-1).then_inc(m.s_pool_b, 1)
                pool.wait_ge(m.s_pool_b, 1)
                hi = flat[:, :, 0:GRID_W - WIN_C]
                nc.gpsimd.affine_select(out=hi, in_=hi, compare_op=ALU.is_ge, fill=NEG, base=WIN_C // 2 - GRID_W,
                                        pattern=[[0, HEADS * NDR], [1, GRID_W - WIN_C]],
                                        channel_multiplier=1).then_inc(m.s_pool_b, 1)

            def q_tile(i):
                return ZP if isinstance(i, int) and i == QT else ZS + i * P

            @block.tensor
            def _(pe):
                pe.wait_ge(m.s_ck, 16)
                for q in range(MT):
                    last = nc.tensor.transpose(ps_y[:, q, :], ck_sb[:, 2 * q:2 * q + 2, :].rearrange("p a d -> p (a d)"), m.ident[:])
                last.then_inc(m.s_ck_mm, 1)

                def scores(i, h):
                    n, b, hb, t = i * HEADS + h, h % 2, (h % 2) * HD, h // 2
                    wait(pe, m.s_st, n - 1)
                    q = q_sb[hb:hb + HD, t, :]
                    if not (isinstance(i, int) and i == QT):
                        nc.tensor.matmul(ps_s[:, b, :], q, m.z[hb:hb + HD, ZK + t, ZS:ZS + TS], start=True, stop=True)
                        nc.tensor.matmul(ps_c[:, b, :], q, ckT[hb:hb + HD, t, :], start=True, stop=True).then_inc(m.s_sc, 1)
                    else:
                        nc.tensor.matmul(ps_c[:, b, :], q, m.z[hb:hb + HD, ZK + t, ZP:ZP + TP],
                                         start=True, stop=True).then_inc(m.s_sc, 1)

                def turn(i, h):
                    n, b = i * HEADS + h, h % 2
                    pe.wait_ge(m.s_ex, n + 1)
                    wait(pe, m.s_trA, n)
                    wait(pe, m.s_trD, n)
                    if not (isinstance(i, int) and i == QT):
                        for k in range(4):
                            nc.tensor.transpose(ps_t[:, k * P:(k + 1) * P], p_sb[:, b, k * P:(k + 1) * P], m.ident[:])
                    nc.tensor.transpose(ps_t5[:], p_sb[:, b, TS:TS + P], m.ident[:]).then_inc(m.s_tr, 1)

                def pv(i, h):
                    n, b = i * HEADS + h, h % 2
                    pe.wait_ge(m.s_trA, n + 1)
                    pe.wait_ge(m.s_trD, n + 1)
                    wait(pe, m.s_o, n)
                    if not (isinstance(i, int) and i == QT):
                        for k in range(4):
                            nc.tensor.matmul(ps_o[:], pT_sb[:, b, k * P:(k + 1) * P], m.zv[:, k, h * HD:(h + 1) * HD],
                                             start=(k == 0), stop=False)
                        nc.tensor.matmul(ps_o[:], pT_sb[:, b, TS:TS + P], cv_sb[:, h, :],
                                         start=False, stop=True).then_inc(m.s_pv, 1)
                    else:
                        nc.tensor.matmul(ps_o[:], pT_sb[:, b, TS:TS + P], m.zv[:, QT, h * HD:(h + 1) * HD],
                                         start=True, stop=True).then_inc(m.s_pv, 1)

                def step(i):
                    pe.wait_ge(m.s_q, i + 1)
                    scores(i, 0)
                    scores(i, 1)
                    for h in range(HEADS):
                        turn(i, h)
                        if h + 2 < HEADS:
                            scores(i, h + 2)
                        if h:
                            pv(i, h - 1)
                    pv(i, HEADS - 1)
                    pe.wait_ge(m.s_o, HEADS * i + HEADS)
                    wait(pe, m.s_yz, i)
                    for t in range(MT):
                        last = nc.tensor.transpose(ps_y[:, t, :], yb_sb[:, t * P:(t + 1) * P], m.ident[:])
                    last.then_inc(m.s_yt, 1)
                pe.wait_ge(m.s_ckT, 1)
                pe.wait_ge(m.s_cv, 16)
                step(0)
                with pe.Fori(1, QT) as i:
                    step(i)
                step(QT)

            @block.vector
            def _(dve):
                link = Chain(dve, m.s_dve_b)
                dve.wait_ge(m.s_ck_mm, 1)
                nc.vector.tensor_copy(ckT[:], ps_y[:]).then_inc(m.s_ckT, 1)
                dve.wait_ge(m.s_pool_b, 2)
                nc.vector.tensor_copy(bias[0:GRID_W, :, 0:NDR, :], rev[:, :, :, ::-1]).then_inc(m.s_tab_lo, 1)

                def stage(i):
                    wait(dve, m.s_sc, HEADS * i)
                    nc.vector.tensor_scalar(q_sb[:], m.z[:, ZQ:ZQ + MT, ds(q_tile(i), P)], 1.0, None, ALU.mult).then_inc(m.s_q, 1)

                def soft(i, h, ctx_only):
                    n, b = i * HEADS + h, h % 2
                    dve.wait_ge(m.s_sc, n + 1)
                    wait(dve, m.s_ex, n - 1)
                    if not ctx_only:
                        tab = bias[:, h, ds(WIN_R - 1 - 2 * i, GRID_H), :]
                        nc.vector.scalar_tensor_tensor(s_sb[:, b, 0:TS], ps_s[:, b, :], SCALE,
                                                       tab.rearrange("p r c -> p (r c)"), ALU.mult, ALU.add)
                    link2(nc.vector.tensor_scalar(s_sb[:, b, TS:TS + P], ps_c[:, b, :], SCALE, None, ALU.mult), n)
                    src = s_sb[:, b, TS:TS + P] if ctx_only else s_sb[:, b, :]
                    nc.vector.tensor_reduce(nmax[:, b:b + 1], src, AX.X, ALU.max, negate=True).then_inc(m.s_st, 1)

                def link2(ins, n):
                    ins.then_inc(m.s_dve_b, 1)
                    dve.wait_ge(m.s_dve_b, n + 1)

                def rest(i, h):
                    n, b = i * HEADS + h, h % 2
                    dve.wait_ge(m.s_ex, n + 1)
                    wait(dve, m.s_o, n - 1)
                    nc.vector.reciprocal(rinv[:, b:b + 1], rsum[:, b:b + 1]).then_inc(m.s_rc, 1)
                    dve.wait_ge(m.s_tr, n + 1)
                    wait(dve, m.s_pv, n - 1)
                    nc.vector.tensor_copy(pT_sb[:, b, TS:TS + P], ps_t5[:]).then_inc(m.s_trD, 1)

                def step(i, ctx_only=False):
                    stage(i)
                    soft(i, 0, ctx_only)
                    for h in range(HEADS):
                        if h + 1 < HEADS:
                            soft(i, h + 1, ctx_only)
                        rest(i, h)
                    dve.wait_ge(m.s_yt, i + 1)
                    nc.vector.tensor_scalar(m.yb[:, :, ds(i * P, P)], ps_y[:], 1.0, None, ALU.mult).then_inc(m.s_yz, 1)
                dve.wait_ge(m.s_tab_hi, 16)
                step(0)
                with dve.Fori(1, QT) as i:
                    step(i)
                step(QT, True)

            @block.scalar
            def _(act):
                def soft(i, h, ctx_only):
                    n, b = i * HEADS + h, h % 2
                    act.wait_ge(m.s_st, n + 1)
                    wait(act, m.s_tr, n - 1)
                    wait(act, m.s_rc, n - 1)
                    sl = slice(TS, TS + P) if ctx_only else slice(0, TS + P)
                    nc.scalar.activation(p_sb[:, b, sl], s_sb[:, b, sl], ACT.Exp, bias=nmax[:, b:b + 1],
                                         accum_out=rsum[:, b:b + 1]).then_inc(m.s_ex, 1)

                def turned(i, h, ctx_only):
                    n, b = i * HEADS + h, h % 2
                    act.wait_ge(m.s_tr, n + 1)
                    wait(act, m.s_pv, n - 1)
                    if ctx_only:
                        act.sem_inc(m.s_trA, 1)
                    else:
                        nc.scalar.activation(pT_sb[:, b, 0:TS], ps_t[:], ACT.Identity).then_inc(m.s_trA, 1)

                def out(i, h):
                    n, b = i * HEADS + h, h % 2
                    act.wait_ge(m.s_pv, n + 1)
                    act.wait_ge(m.s_rc, n + 1)
                    if h == 0:
                        wait(act, m.s_yt, i)
                    nc.scalar.activation(yb_sb[:, h * HD:(h + 1) * HD], ps_o[:], ACT.Identity,
                                         scale=rinv[:, b:b + 1]).then_inc(m.s_o, 1)

                def step(i, ctx_only=False):
                    soft(i, 0, ctx_only)
                    for h in range(HEADS):
                        if h + 1 < HEADS:
                            soft(i, h + 1, ctx_only)
                        turned(i, h, ctx_only)
                        if h:
                            out(i, h - 1)
                    out(i, HEADS - 1)
                step(0)
                with act.Fori(1, QT) as i:
                    step(i)
                step(QT, True)


G_N, G_CH, G_ST = 32, 16, 64
GP = G_N // 2
CH = 8
NCS, NCP = TS // CH, TP // CH
NC = NCS + NCP
TWO_PI_HI, TWO_PI_LO = 6.28125, 0.0019353071795864769
ROUND = 12582912.0


def s5_phase(nc, m, a):
    with ExitStack() as whole, ExitStack() as ctx:
        def outer(name, shape):
            return whole.enter_context(nc.sbuf_tensor(name, shape, F32))

        def sb(name, shape):
            return ctx.enter_context(nc.sbuf_tensor(name, shape, F32))
        atT = outer("s5_atT", [P, 2, 2, GP, P])
        tt_sb = outer("s5_tt", [P, G_N, P])
        vt = outer("s5_vt", [P, 2, 2, GP, CH, G_CH])
        pc = outer("s5_pc", [P, 4, 2, GP])
        a8 = outer("s5_a8", [P, 2, 2, 2, GP])
        rows = sb("s5_rows", [P, P])
        crow = sb("s5_crow", [P, 2, 2, P])
        dt_row = sb("s5_dt_row", [P, 2, GP, 2])
        dt = sb("s5_dt", [P, 2, GP])
        w = sb("s5_w", [P, 16, 2, GP])
        pw = sb("s5_pw", [P, 2, CH, 2, 2, GP])
        pt = sb("s5_pt", [P, 2, 4, 2, 2, GP])
        b_sb = sb("s5_b", [P, 2, GP, G_CH])
        bb = sb("s5_bb", [P, 2, 2, GP, G_CH])
        c_sb = sb("s5_c", [P, 2, GP, G_CH])
        at = sb("s5_at", [P, 2, 2, GP, CH, G_CH])
        tmp = tt_sb[:].rearrange("p g q -> p (g q)").rearrange("p (n j t h) -> p n j t h", n=2, j=GP, t=CH)
        (m.s_p5, m.s_p5b, m.s_p5_mm, m.s_p5c, m.s_c5_mm, m.s_d5, m.s_sin5, m.s_w5, m.s_msk5, m.s_pool5,
         m.s_at_mm, m.s_at_sb, m.s_t_mm, m.s_t_sb, m.s_u_mm, m.s_u_sb, m.s_zz_mm, m.s_zz_sb, m.s_x5, m.s_y5_mm,
         m.s_y5_sb, m.s_f5_mm, m.s_f5_sb, m.s_ge5, m.s_glu_mm, m.s_glu_sb, m.s_glu_w, m.s_out5, m.s_fin_mm,
         m.s_fin_sb, m.s_dve5, m.s_tab5, m.s_du5, m.s_sp5, m.s_yc5, m.s_bb5, m.s_pl5, m.s_ut_mm, m.s_ut_sb, m.s_wt_mm, m.s_wt_sb) = sems(
            nc, m, "s_p5 s_p5b s_p5_mm s_p5c s_c5_mm s_d5 s_sin5 s_w5 s_msk5 s_pool5 s_at_mm s_at_sb s_t_mm s_t_sb "
            "s_u_mm s_u_sb s_zz_mm s_zz_sb s_x5 s_y5_mm s_y5_sb s_f5_mm s_f5_sb s_ge5 s_glu_mm s_glu_sb s_glu_w s_out5 "
            "s_fin_mm s_fin_sb s_dve5 s_tab5 s_du5 s_sp5 s_yc5 s_bb5 s_pl5 s_ut_mm s_ut_sb s_wt_mm s_wt_sb")
        ps_a = ctx.enter_context(nc.psum_tensor("ps_5a", [P, 2, 512], F32))
        with nc.Block() as block:

            @block.sync
            def _(sp):
                for n, name in enumerate(("s5_a_re", "s5_a_im", "state_s5_re", "state_s5_im")):
                    sp.dma_start(rows[32 * n:32 * n + 32, :],
                                 a[name].rearrange("d (j e) p -> (d j) (e p)", e=2)).then_inc(m.s_p5, 16)
                for c, name in enumerate(("s5_c_re", "s5_c_im")):
                    for j in range(GP):
                        sp.dma_start(crow[(j % 8) * G_CH:(j % 8 + 1) * G_CH, c, j // 8, :].rearrange("h (e p) -> h e p", e=2),
                                     a[name][2 * j:2 * j + 2].rearrange("e h p -> h e p")).then_inc(m.s_p5c, 16)

            @block.gpsimd
            def _(pool):
                pool.dma_start(dt_row[:], bass.AP(a["s5_log_dt"].tensor, 0, [[0, P], [1, 2 * G_N]])
                               .rearrange("p (d j e) -> p d j e", d=2, e=2)).then_inc(m.s_d5, 16)
                for c, name in enumerate(("s5_b_re", "s5_b_im")):
                    for e in range(2):
                        pool.dma_start(b_sb[e * G_ST:(e + 1) * G_ST, c],
                                       a[name].rearrange("(j e) p h -> e p j h", e=2)[e]).then_inc(m.s_p5b, 16)
                pool.wait_ge(m.s_bb5, 1)
                plink = Chain(pool, m.s_pl5)
                for d in range(2):
                    dn = s5_powers(pw, 1, d)
                    b = [bb[:, r, d].unsqueeze(2).to_broadcast([P, GP, CH, G_CH]) for r in range(2)]
                    s5_cmul(nc.gpsimd, plink, at[:, 0, d], at[:, 1, d], b[0], b[1], dn[0], dn[1], tmp[:, 1])

            @block.tensor
            def _(pe):
                pe.wait_ge(m.s_p5, 64)
                nc.tensor.transpose(ps_a[:, 0, 0:P], rows[:], m.ident[:]).then_inc(m.s_p5_mm, 1)
                pe.wait_ge(m.s_p5c, 16 * 32)
                for c in range(2):
                    for jt in range(2):
                        last = nc.tensor.transpose(ps_a[:, 1, (c * 2 + jt) * P:(c * 2 + jt + 1) * P], crow[:, c, jt, :], m.ident[:])
                last.then_inc(m.s_c5_mm, 1)

            @block.scalar
            def _(act):
                act.wait_ge(m.s_d5, 16)
                for e in range(2):
                    last = nc.scalar.activation(dt[e * G_ST:(e + 1) * G_ST], dt_row[e * G_ST:(e + 1) * G_ST, :, :, e], ACT.Exp)
                last.then_inc(m.s_w5, 1)
                act.wait_ge(m.s_sin5, 1)
                nc.scalar.activation(w[:, 4], w[:, 0], ACT.Exp)
                nc.scalar.activation(w[:, 5], w[:, 0], ACT.Exp, scale=-1.0)
                nc.scalar.activation(w[:, 6], w[:, 2], ACT.Sin)
                nc.scalar.activation(w[:, 7], w[:, 3], ACT.Sin).then_inc(m.s_w5, 1)

            @block.vector
            def _(dve):
                V = nc.vector
                link = Chain(dve, m.s_dve5)
                dve.wait_ge(m.s_p5_mm, 1)
                link(V.tensor_copy(pc[:], ps_a[:, 0, 0:P].rearrange("p (n d j) -> p n d j", n=4, d=2)))
                dve.wait_ge(m.s_w5, 1)
                V.tensor_tensor(w[:, 0], dt[:], pc[:, 0], ALU.mult)
                link(V.tensor_tensor(w[:, 1], dt[:], pc[:, 1], ALU.mult))
                link(V.tensor_scalar(w[:, 8], w[:, 1], 0.15915494309189535, ROUND, ALU.mult, ALU.add))
                link(V.tensor_scalar(w[:, 8], w[:, 8], ROUND, None, ALU.subtract))
                link(V.scalar_tensor_tensor(w[:, 2], w[:, 8], -TWO_PI_HI, w[:, 1], ALU.mult, ALU.add))
                link(V.scalar_tensor_tensor(w[:, 2], w[:, 8], -TWO_PI_LO, w[:, 2], ALU.mult, ALU.add))
                link(V.tensor_scalar(w[:, 2], w[:, 2], 3.1415925, -3.1415925, ALU.min, ALU.max))
                link(V.scalar_tensor_tensor(w[:, 3], w[:, 2], -1.0, w[:, 2], ALU.mult, ALU.max))
                V.tensor_scalar(w[:, 3], w[:, 3], -1.0, 1.5707963267948966, ALU.mult, ALU.add).then_inc(m.s_sin5, 1)
                dve.wait_ge(m.s_w5, 2)
                V.tensor_tensor(pw[:, 0, 0, 0], w[:, 4], w[:, 7], ALU.mult)
                V.tensor_tensor(pw[:, 1, 0, 0], w[:, 4], w[:, 6], ALU.mult)
                V.tensor_tensor(pw[:, 0, 0, 1], w[:, 5], w[:, 7], ALU.mult)
                link(V.scalar_tensor_tensor(pw[:, 1, 0, 1], w[:, 5], -1.0, w[:, 6], ALU.mult, ALU.mult))

                def power(lo, n, by):
                    for i in range(n):
                        fr, fi, xr, xi = pw[:, 0, by - 1], pw[:, 1, by - 1], pw[:, 0, i], pw[:, 1, i]
                        V.tensor_tensor(pt[:, 0, i], fi, xi, ALU.mult)
                        V.tensor_tensor(pt[:, 1, i], fi, xr, ALU.mult)
                        V.tensor_tensor(pw[:, 0, lo + i], fr, xr, ALU.mult)
                        last = V.tensor_tensor(pw[:, 1, lo + i], fr, xi, ALU.mult)
                    link(last)
                    V.tensor_tensor(pw[:, 0, lo:lo + n], pw[:, 0, lo:lo + n], pt[:, 0, 0:n], ALU.subtract)
                    link(V.tensor_tensor(pw[:, 1, lo:lo + n], pw[:, 1, lo:lo + n], pt[:, 1, 0:n], ALU.add))
                power(1, 1, 1)
                power(2, 2, 2)
                power(4, 4, 4)
                V.tensor_copy(a8[:, 0, :, 0], pw[:, 0, CH - 1, 0])
                V.tensor_copy(a8[:, 0, :, 1], pw[:, 0, CH - 1, 0])
                V.tensor_scalar(a8[:, 1, :, 0], pw[:, 1, CH - 1, 0], -1.0, None, ALU.mult)
                V.tensor_copy(a8[:, 1, :, 1], pw[:, 1, CH - 1, 0])
                V.tensor_scalar(w[:, 8], pw[:, 0, 0, 0], -1.0, None, ALU.add)
                V.tensor_tensor(w[:, 9], pc[:, 0], pc[:, 0], ALU.mult)
                link(V.tensor_tensor(w[:, 10], pc[:, 1], pc[:, 1], ALU.mult))
                link(V.tensor_tensor(w[:, 9], w[:, 9], w[:, 10], ALU.add))
                link(V.reciprocal(w[:, 9], w[:, 9]))
                V.tensor_tensor(w[:, 10], w[:, 8], pc[:, 0], ALU.mult)
                V.tensor_tensor(w[:, 11], pw[:, 1, 0, 0], pc[:, 1], ALU.mult)
                V.tensor_tensor(w[:, 12], pw[:, 1, 0, 0], pc[:, 0], ALU.mult)
                link(V.tensor_tensor(w[:, 13], w[:, 8], pc[:, 1], ALU.mult))
                V.tensor_tensor(w[:, 10], w[:, 10], w[:, 11], ALU.add)
                link(V.tensor_tensor(w[:, 12], w[:, 12], w[:, 13], ALU.subtract))
                V.tensor_tensor(w[:, 10], w[:, 10], w[:, 9], ALU.mult)
                link(V.tensor_tensor(w[:, 12], w[:, 12], w[:, 9], ALU.mult))
                dve.wait_ge(m.s_c5_mm, 1)
                link(V.tensor_copy(c_sb[:], ps_a[:, 1, :].rearrange("p (c j h) -> p c j h", c=2, h=G_CH)))
                dve.wait_ge(m.s_p5b, 64)

                for d in range(2):
                    g = [w[:, r, d].unsqueeze(2).to_broadcast([P, GP, G_CH]) for r in (10, 12)]
                    s5_cmul(V, link, bb[:, 0, d], bb[:, 1, d], b_sb[:, 0], b_sb[:, 1], g[0], g[1], tmp[:, 0, :, 0])
                V.memset(w[:, 15], 0.0).then_inc(m.s_bb5, 1)
                for d in range(2):
                    up = s5_powers(pw, 0, d)
                    c = [c_sb[:, r].unsqueeze(2).to_broadcast([P, GP, CH, G_CH]) for r in range(2)]
                    s5_cmul(V, link, vt[:, 0, d], vt[:, 1, d], c[0], c[1], up[0], up[1], tmp[:, 0], True)
        s5_local(nc, m, ctx, atT, tt_sb, vt, at)
        ctx.close()
        s5_scan(nc, m, a, pc, vt, atT, tt_sb, a8)


def s5_powers(pw, sign, d):
    step = 1 if d == 0 else -1
    return [pw[:, c, ::step, sign, d].rearrange("p e j -> p j e").unsqueeze(3).to_broadcast([P, GP, CH, G_CH]) for c in range(2)]


def s5_cmul(eng, link, out_re, out_im, xr, xi, yr, yi, t, negate_im=False):
    eng.tensor_tensor(out_re, xr, yr, ALU.mult)
    link(eng.tensor_tensor(t, xi, yi, ALU.mult))
    link(eng.tensor_tensor(out_re, out_re, t, ALU.subtract))
    eng.tensor_tensor(out_im, xr, yi, ALU.mult)
    link(eng.tensor_tensor(t, xi, yr, ALU.mult))
    if negate_im:
        link(eng.scalar_tensor_tensor(out_im, out_im, -1.0, t, ALU.mult, ALU.subtract))
    else:
        link(eng.tensor_tensor(out_im, out_im, t, ALU.add))


def s5_local(nc, m, ctx, atT, tt_sb, vt, at):
    ps_t = ctx.enter_context(nc.psum_tensor("ps_5t", [P, 4, 4, P], F32))
    msk = ctx.enter_context(nc.sbuf_tensor("s5_msk", [P, 2, CH, G_CH], F32))
    tm2 = ctx.enter_context(nc.sbuf_tensor("s5_tm2", [P, 4, P], F32))
    with nc.Block() as block:

        @block.gpsimd
        def _(pool):
            nc.gpsimd.memset(msk[:], 1.0).then_inc(m.s_pool5, 1)
            pool.wait_ge(m.s_pool5, 1)
            nc.gpsimd.affine_select(out=msk[:, 0], in_=msk[:, 0], compare_op=ALU.is_ge, fill=0.0, base=15,
                                    pattern=[[16, CH], [0, G_CH]], channel_multiplier=-1)
            nc.gpsimd.affine_select(out=msk[:, 1], in_=msk[:, 1], compare_op=ALU.is_ge, fill=0.0, base=0,
                                    pattern=[[-16, CH], [0, G_CH]], channel_multiplier=1).then_inc(m.s_msk5, 1)

        @block.tensor
        def _(pe):
            for n in range(16):
                c, d, j4 = n // 8, n // 4 % 2, n % 4
                if n >= 4:
                    pe.wait_ge(m.s_at_sb, n - 3)
                for j in range(4):
                    last = nc.tensor.transpose(ps_t[:, n % 4, j, :],
                                               at[:, c, d, 4 * j4 + j].rearrange("p t h -> p (t h)"), m.ident[:])
                last.then_inc(m.s_at_mm, 1)
            for j4 in range(4):
                pe.wait_ge(m.s_at_sb, 16)
                if j4:
                    pe.wait_ge(m.s_t_sb, 2 * j4)
                for d in range(2):
                    for e in range(2):
                        pr = slice(e * G_ST, (e + 1) * G_ST)
                        for j in range(4):
                            jj = 4 * j4 + j
                            for c in range(2):
                                last = nc.tensor.matmul(ps_t[:, 2 * d + e, j, :], at[pr, c, d, jj].rearrange("p t h -> p (t h)"),
                                                        vt[pr, c, d, jj].rearrange("p t h -> p (t h)"),
                                                        start=(c == 0), stop=(c == 1))
                last.then_inc(m.s_t_mm, 1)

        @block.scalar
        def _(act):
            for n in range(16):
                c, d, j4 = n // 8, n // 4 % 2, n % 4
                act.wait_ge(m.s_at_mm, n + 1)
                nc.scalar.activation(atT[:, c, d, 4 * j4:4 * j4 + 4], ps_t[:, n % 4], ACT.Identity).then_inc(m.s_at_sb, 1)

        @block.vector
        def _(dve):
            V = nc.vector
            dve.wait_ge(m.s_msk5, 1)
            mk = [msk[:, d].rearrange("p t h -> p (t h)").unsqueeze(1).to_broadcast([P, 4, P]) for d in range(2)]
            for j4 in range(4):
                dve.wait_ge(m.s_t_mm, j4 + 1)
                for e in range(2):
                    n = 2 * j4 + e
                    o = tt_sb[:, 8 * j4 + e:8 * j4 + 8:2, :]
                    if n:
                        dve.wait_ge(m.s_t_sb, n)
                    V.tensor_tensor(o, ps_t[:, e], mk[0], ALU.mult)
                    V.tensor_tensor(tm2[:], ps_t[:, 2 + e], mk[1], ALU.mult).then_inc(m.s_tab5, 1)
                    dve.wait_ge(m.s_tab5, n + 1)
                    V.tensor_tensor(o, o, tm2[:], ALU.add).then_inc(m.s_t_sb, 1)


def s5_scan(nc, m, a, pc, vt, atT, tt_sb, a8):
    NSL = 2 * NC
    with ExitStack() as ctx:
        def sb(name, shape):
            return ctx.enter_context(nc.sbuf_tensor(name, shape, F32))

        def pb(name, shape):
            return ctx.enter_context(nc.psum_tensor(name, shape, F32))
        ps_u = pb("ps_5u", [P, 2, 4, P])
        ps_z = pb("ps_5z", [P, 4, 4, P])
        u_sb = sb("s5_u", [P, G_N, NC])
        ut = sb("s5_ut", [P, MT, P * CH])
        zz = sb("s5_zz", [P, NSL, 2, GP])
        x = sb("s5_x", [P, NSL, 2, GP])
        xw = sb("s5_xw", [P, 3, 2, 2, GP])
        fin = sb("s5_fin", [P, 2, 2, GP])
        finT = sb("s5_finT", [G_ST, P])
        with nc.Block() as block:

            @block.tensor
            def _(pe):
                for n in range(8):
                    if n >= 2:
                        pe.wait_ge(m.s_ut_sb, n - 1)
                    for q in range(4):
                        last = nc.tensor.transpose(ps_u[0:NC, n % 2, q, :], m.yc[:, n // 2, 4 * (n % 2) + q:N:CH], m.ident[:])
                    last.then_inc(m.s_ut_mm, 1)
                pe.wait_ge(m.s_ut_sb, 8)
                for n in range(8):
                    if n >= 2:
                        pe.wait_ge(m.s_u_sb, n - 1)
                    for q in range(4):
                        g = 4 * n + q
                        last = nc.tensor.transpose(ps_u[:, n % 2, q, 0:NC], ut[0:NC, g // 8, (g % 8) * P:(g % 8 + 1) * P],
                                                   m.ident[0:NC, 0:NC])
                    last.then_inc(m.s_u_mm, 1)
                pe.wait_ge(m.s_u_sb, 8)
                for n in range(16):
                    c, d, j4 = n // 8, n // 4 % 2, n % 4
                    if n >= 4:
                        pe.wait_ge(m.s_zz_sb, n - 3)
                    for j in range(4):
                        for e in range(2):
                            last = nc.tensor.matmul(ps_z[e * G_ST:(e + 1) * G_ST, n % 4, j, 0:NC],
                                                    atT[:, c, d, 4 * j4 + j, e * G_ST:(e + 1) * G_ST],
                                                    u_sb[:, 2 * (4 * j4 + j) + e, :], start=True, stop=True)
                    last.then_inc(m.s_zz_mm, 1)

            @block.scalar
            def _(act):
                for n in range(8):
                    act.wait_ge(m.s_ut_mm, n + 1)
                    by_group = ut[0:NC, n // 2].rearrange("c (g s h) -> c s g h", g=8, s=CH)[:, 4 * (n % 2):4 * (n % 2) + 4]
                    nc.scalar.activation(by_group, ps_u[0:NC, n % 2].rearrange("c s (g h) -> c s g h", g=8),
                                         ACT.Identity).then_inc(m.s_ut_sb, 1)
                for n in range(8):
                    act.wait_ge(m.s_u_mm, n + 1)
                    nc.scalar.activation(u_sb[:, 4 * n:4 * n + 4, :], ps_u[:, n % 2, :, 0:NC], ACT.Identity).then_inc(m.s_u_sb, 1)
                for n in range(16):
                    c, d, j4 = n // 8, n // 4 % 2, n % 4
                    act.wait_ge(m.s_zz_mm, n + 1)
                    sl = slice(0, NC) if d == 0 else slice(NSL - 1, NC - 1, -1)
                    nc.scalar.activation(zz[:, sl, c, 4 * j4:4 * j4 + 4], ps_z[:, n % 4, :, 0:NC].rearrange("p j c -> p c j"),
                                         ACT.Identity).then_inc(m.s_zz_sb, 1)

            @block.vector
            def _(dve):
                V = nc.vector

                def two(buf, s0, s1):
                    return buf[:, s0:s1 + 1:s1 - s0]

                V.tensor_copy(two(x, 0, NC + NCP), pc[:, 2:4].rearrange("p c d j -> p d c j"))
                V.memset(x[:, NCS:NCS + 1], 0.0)
                V.memset(x[:, NC:NC + 1], 0.0).then_inc(m.s_x5, 1)
                dve.wait_ge(m.s_x5, 1)
                dve.wait_ge(m.s_zz_sb, 16)

                def step(n, s0, s1, o):
                    V.tensor_tensor(xw[:, 0], two(x, s0, s1), two(zz, s0, s1), ALU.add).then_inc(m.s_x5, 1)
                    dve.wait_ge(m.s_x5, n + 1)
                    V.tensor_tensor(xw[:, 1], xw[:, 0], a8[:, 0], ALU.mult)
                    V.tensor_tensor(xw[:, 2], xw[:, 0, :, ::-1], a8[:, 1], ALU.mult).then_inc(m.s_x5, 1)
                    dve.wait_ge(m.s_x5, n + 2)
                    V.tensor_tensor(o, xw[:, 1], xw[:, 2], ALU.add).then_inc(m.s_x5, 1)
                    dve.wait_ge(m.s_x5, n + 3)
                n = 1
                for k in range(NCP):
                    o = two(x, NCS + k + 1, NC + k + 1) if k + 1 < NCP else fin[:].rearrange("p c d j -> p d c j")
                    step(n, NCS + k, NC + k, o)
                    n += 3
                for k in range(NCS - 1):
                    step(n, k, NC + NCP + k, two(x, k + 1, NC + NCP + k + 1))
                    n += 3
        flat = atT[:].rearrange("p c d j q -> p (c d j q)")
        y_g = flat[:, 0:G_N * NC].rearrange("p (g c) -> p g c", g=G_N)
        y_f = flat[:, G_N * NC:G_N * NC + MT * N].rearrange("p (k n) -> p k n", k=MT)
        glu_w = flat[:, 5120:5120 + MT * MIX].rearrange("p (k n) -> p k n", k=MT)
        ps_y = ps_z[:, 0:2]
        ps_g = ps_z[:, 2:4].rearrange("p b j q -> p b (j q)")
        with nc.Block() as block:

            @block.sync
            def _(sp):
                sp.dma_start(glu_w, a["s5_w_glu"].rearrange("(k p) n -> p k n", p=P)).then_inc(m.s_glu_w, 16)
                sp.dma_start(m.y_dram[1], m.yb[:]).then_inc(m.s_sp5, 16)
                sp.wait_ge(m.s_yc5, MT)
                sp.dma_start(m.y_dram[2], m.yc[:]).then_inc(m.s_sp5, 16)
                sp.wait_ge(m.s_sp5, 32)

            @block.gpsimd
            def _(pool):
                pool.wait_ge(m.s_fin_sb, 1)
                pool.dma_start(a["new_s5_re"].rearrange("d (j e) p -> (d j) (e p)", e=2), finT[0:32, :]).then_inc(m.s_out5, 16)
                pool.dma_start(a["new_s5_im"].rearrange("d (j e) p -> (d j) (e p)", e=2), finT[32:64, :]).then_inc(m.s_out5, 16)
                pool.wait_ge(m.s_out5, 32)

            @block.tensor
            def _(pe):
                for j4 in range(4):
                    for e in range(2):
                        pr = slice(e * G_ST, (e + 1) * G_ST)
                        if j4:
                            pe.wait_ge(m.s_y5_sb, 2 * j4 - 1 + e)
                        for j in range(4):
                            jj = 4 * j4 + j
                            o = ps_y[:, e, j, 0:NC]
                            nc.tensor.matmul(o, tt_sb[:, 2 * jj + e, :], u_sb[:, 2 * jj + e, :], start=True, stop=False)
                            for d in range(2):
                                sl = slice(0, NC) if d == 0 else slice(NSL - 1, NC - 1, -1)
                                for c in range(2):
                                    last = nc.tensor.matmul(o, vt[pr, c, d, jj].rearrange("p t h -> p (t h)"), x[pr, sl, c, jj],
                                                            start=False, stop=(d == 1 and c == 1))
                        last.then_inc(m.s_y5_mm, 1)
                nc.tensor.transpose(ps_g[0:G_ST, 0, 0:P], fin[:].rearrange("p c d j -> p (c d j)"), m.ident[:]).then_inc(m.s_fin_mm, 1)
                pe.wait_ge(m.s_y5_sb, 8)
                for n in range(8):
                    if n >= 2:
                        pe.wait_ge(m.s_wt_sb, n - 1)
                    for q in range(4):
                        last = nc.tensor.transpose(ps_u[0:NC, n % 2, q, :], y_g[:, 4 * n + q, :], m.ident[:])
                    last.then_inc(m.s_wt_mm, 1)
                for f in range(MT):
                    pe.wait_ge(m.s_wt_sb, 2 * f + 2)
                    if f:
                        pe.wait_ge(m.s_f5_sb, 2 * f)
                    for t in range(CH):
                        last = nc.tensor.transpose(ps_y[:, t // 4, t % 4, 0:NC], ut[0:NC, f, t * P:(t + 1) * P],
                                                   m.ident[0:NC, 0:NC])
                    last.then_inc(m.s_f5_mm, 1)
                pe.wait_ge(m.s_glu_w, 16)
                pe.wait_ge(m.s_ge5, MT)
                pe.wait_ge(m.s_fin_sb, 1)
                for f in range(MT):
                    if f:
                        pe.wait_ge(m.s_glu_sb, f)
                    for b, sl in ((0, slice(0, TS)), (1, slice(TS, N))):
                        for k in range(MT):
                            last = nc.tensor.matmul(ps_g[:, b, 0:sl.stop - sl.start], glu_w[:, k, f * P:(f + 1) * P], y_f[:, k, sl],
                                                    start=(k == 0), stop=(k == MT - 1))
                    last.then_inc(m.s_glu_mm, 1)

            @block.vector
            def _(dve):
                V = nc.vector
                for n in range(8):
                    j4, e = n // 2, n % 2
                    dve.wait_ge(m.s_y5_mm, n + 1)
                    V.tensor_copy(y_g[:, 8 * j4 + e:8 * j4 + 8:2, :], ps_y[:, e, :, 0:NC]).then_inc(m.s_y5_sb, 1)
                dve.wait_ge(m.s_fin_mm, 1)
                V.tensor_copy(finT[:], ps_g[0:G_ST, 0, 0:P]).then_inc(m.s_fin_sb, 1)
                for f in range(MT):
                    dve.wait_ge(m.s_f5_mm, f + 1)
                    for b in range(2):
                        o = y_f[:, f].rearrange("p (c t) -> p t c", t=CH)[:, 4 * b:4 * b + 4]
                        u = m.yc[:, f].rearrange("p (c t) -> p t c", t=CH)[:, 4 * b:4 * b + 4]
                        d0 = PCOLS["s5_d"][0] + f
                        V.tensor_scalar(o, u, m.pcol[:, d0:d0 + 1], None, ALU.mult).then_inc(m.s_du5, 1)
                        dve.wait_ge(m.s_du5, 2 * f + b + 1)
                        V.tensor_tensor(o, o, ps_y[:, b, :, 0:NC], ALU.add).then_inc(m.s_f5_sb, 1)
                for f in range(MT):
                    dve.wait_ge(m.s_glu_sb, f + 1)
                    V.tensor_tensor(m.yc[:, f], m.yc[:, f], y_f[:, f], ALU.mult).then_inc(m.s_yc5, 1)

            @block.scalar
            def _(act):
                for n in range(8):
                    act.wait_ge(m.s_wt_mm, n + 1)
                    by_token = ut[0:NC, n // 2].rearrange("c (t g h) -> c g t h", t=CH, g=8)[:, 4 * (n % 2):4 * (n % 2) + 4]
                    nc.scalar.activation(by_token, ps_u[0:NC, n % 2].rearrange("c g (t h) -> c g t h", t=CH),
                                         ACT.Identity).then_inc(m.s_wt_sb, 1)
                for f in range(MT):
                    act.wait_ge(m.s_f5_sb, 2 * f + 2)
                    nc.scalar.activation(y_f[:, f], y_f[:, f], ACT.Gelu_apprx_tanh).then_inc(m.s_ge5, 1)
                b0 = PCOLS["s5_b_glu"][0]
                for f in range(MT):
                    act.wait_ge(m.s_glu_mm, f + 1)
                    nc.scalar.activation(m.yc[:, f, 0:TS], ps_g[:, 0, :], ACT.Sigmoid, bias=m.pcol[:, b0 + f:b0 + f + 1])
                    nc.scalar.activation(m.yc[:, f, TS:N], ps_g[:, 1, 0:TP], ACT.Sigmoid,
                                         bias=m.pcol[:, b0 + f:b0 + f + 1]).then_inc(m.s_glu_sb, 1)


R_T, K_T, V_T, LW_T, LA_T, LG_T = 0, MT, 2 * MT, 3 * MT, 3 * MT + 1, 3 * MT + 2
LEVELS = 7


def rwkv_phase(nc, m, a):
    with ExitStack() as ctx:
        def sb(name, shape):
            return ctx.enter_context(nc.sbuf_tensor(name, shape, F32))
        m.vt = sb("vt", [P, NT, MIX])
        m.sig, m.kd, m.bd = (sb(x, [P, 2, MT, N]) for x in ("sig", "kd", "bd"))
        m.lev = sb("lev", [P, 2, LEVELS, P])
        m.smask, m.imask = sb("smask", [P, 2, P]), sb("imask", [P, 2, P])
        m.st, m.rkh = sb("st", [P, 2, MT, HD]), sb("rkh", [P, MT, 2])
        m.bon, m.neghalf = sb("bon", [P, NT, HEADS]), sb("neghalf", [P, HEADS])
        m.kkn = m.zr[:, V_T:V_T + MT, 0:N]
        m.yo = m.zr[:, K_T:K_T + MT, :].rearrange("p t c -> p (t c)")[:, 0:NT * MIX].rearrange("p (t c) -> p t c", t=NT)
        rwkv_prepare(nc, m, a)
        rwkv_chunks(nc, m, a)
        rwkv_finish(nc, m, a)


def rwkv_prepare(nc, m, a):
    with ExitStack() as ctx:
        def sb(name, shape, dt=F32):
            return ctx.enter_context(nc.sbuf_tensor(name, shape, dt))
        w2 = sb("rw_w2", [P, MIX])
        a2 = sb("rw_a2", [P, MIX])
        s_in = sb("rw_sin", [HD, 2, HEADS, HD])
        mu2 = sb("rw_mu2", [P, 2, RT])
        ka1 = sb("rw_ka1", [P, MT])
        nb = sb("rw_nb", [P, 2, ZW - 2])
        zs = sb("rw_zs", [P, 2, ZW - 2])
        blk = sb("rw_blk", [P, P])
        tx = sb("rw_tx", [P, P], I32)
        ty = sb("rw_ty", [P, P], I32)
        kk = sb("rw_kk", [P, MT, N])
        sq = sb("rw_sq", [P, 2, N])
        rn = sb("rw_rn", [P, 2, N])
        ps_s = ctx.enter_context(nc.psum_tensor("ps_rs", [P, 2, 512], F32))
        ps_p = ctx.enter_context(nc.psum_tensor("ps_rp", [P, 2, 512], F32))
        ps_v = ctx.enter_context(nc.psum_tensor("ps_rv", [P, 2, 512], F32))
        ps_n = ctx.enter_context(nc.psum_tensor("ps_rn", [P, 2, 512], F32))
        (m.r_w, m.r_mu, m.r_nb, m.r_zs, m.r_sh, m.r_blk, m.r_pool, m.r_lora, m.r_sg, m.r_sg_mm, m.r_v_mm,
         m.r_v_sb, m.r_kk, m.r_sq, m.r_n_mm, m.r_rt, m.r_kkn, m.r_st, m.r_st_mm, m.r_dve, m.r_sm) = sems(
            nc, m, "r_w r_mu r_nb r_zs r_sh r_blk r_pool r_lora r_sg r_sg_mm r_v_mm r_v_sb r_kk r_sq r_n_mm r_rt r_kkn r_st "
            "r_st_mm r_dve r_sm")
        with nc.Block() as block:

            @block.sync
            def _(sp):
                sp.dma_start(w2[:], a["rwkv_w2"]).then_inc(m.r_w, 16)
                sp.dma_start(a2[:], a["rwkv_a2"]).then_inc(m.r_w, 16)
                sp.dma_start(s_in[:], a["state_rwkv"].rearrange("d h v k -> v d h k")).then_inc(m.r_st, 16)

            @block.gpsimd
            def _(pool):
                link = Chain(pool, m.r_pool)
                for t in range(RT):
                    if t >= 2:
                        pool.wait_ge(m.r_sh, t - 1)
                    nc.gpsimd.tensor_tensor(nb[:, t % 2], m.zr[:, t, 0:ZW - 2], m.zr[:, t, 2:ZW], ALU.add).then_inc(m.r_nb, 1)
                nc.gpsimd.iota(tx[:], pattern=[[0, P]], base=0, channel_multiplier=1)
                nc.gpsimd.iota(ty[:], pattern=[[1, P]], base=0, channel_multiplier=0)
                nc.gpsimd.memset(m.smask[:], 1.0)
                nc.gpsimd.memset(m.imask[:], 1.0)
                nc.gpsimd.memset(m.neghalf[:], -0.5)
                link(nc.gpsimd.memset(blk[:], 1.0))
                for buf, base in ((m.smask, -1), (m.imask, 0)):
                    nc.gpsimd.affine_select(out=buf[:, 0], in_=buf[:, 0], compare_op=ALU.is_ge, fill=0.0, base=base,
                                            pattern=[[-1, P]], channel_multiplier=1)
                    nc.gpsimd.affine_select(out=buf[:, 1], in_=buf[:, 1], compare_op=ALU.is_ge, fill=0.0, base=base,
                                            pattern=[[1, P]], channel_multiplier=-1)
                link(nc.gpsimd.affine_select(out=blk[:, 0:HD], in_=blk[:, 0:HD], compare_op=ALU.is_ge, fill=0.0, base=HD - 1,
                                             pattern=[[0, HD]], channel_multiplier=-1))
                nc.gpsimd.affine_select(out=blk[:, HD:P], in_=blk[:, HD:P], compare_op=ALU.is_ge, fill=0.0, base=-HD,
                                        pattern=[[0, HD]], channel_multiplier=1).then_inc(m.r_blk, 1)

            @block.vector
            def _(dve):
                V = nc.vector
                link = Chain(dve, m.r_dve)
                mu0 = PCOLS["rwkv_mu"][0]
                V.tensor_scalar(mu2[:, 0], m.pcol[:, mu0:mu0 + RT], -1.0, 1.0, ALU.mult, ALU.add)
                V.tensor_scalar(mu2[:, 1], m.pcol[:, mu0:mu0 + RT], 0.5, None, ALU.mult).then_inc(m.r_mu, 1)
                dve.wait_ge(m.r_mu, 1)
                ka0, kk0, rk0 = (PCOLS[x][0] for x in ("rwkv_ka", "rwkv_kk", "rwkv_rk"))
                V.tensor_scalar(ka1[:], m.pcol[:, ka0:ka0 + MT], -1.0, 1.0, ALU.mult, ALU.add)
                link(V.memset(m.rkh[:], 0.0))
                for e in range(2):
                    V.tensor_copy(m.rkh[e * HD:(e + 1) * HD, :, e], m.pcol[e * HD:(e + 1) * HD, rk0:rk0 + MT])
                for t in range(RT):
                    dve.wait_ge(m.r_nb, t + 1)
                    dve.wait_ge(m.r_zs, t + 1)
                    V.scalar_tensor_tensor(m.zr[:, t, 0:TS], nb[:, t % 2, 0:TS], mu2[:, 1, t:t + 1], zs[:, t % 2, 0:TS],
                                           ALU.mult, ALU.add)
                    V.scalar_tensor_tensor(m.zr[:, t, TS:N], nb[:, t % 2, ZP - 1:ZP - 1 + TP], mu2[:, 1, t:t + 1],
                                           zs[:, t % 2, ZP - 1:ZP - 1 + TP], ALU.mult, ALU.add).then_inc(m.r_sh, 1)
                dve.wait_ge(m.r_sh, RT)
                for f in range(MT):
                    V.tensor_scalar(kk[:, f], m.zr[:, K_T + f, 0:N], m.pcol[:, kk0 + f:kk0 + f + 1], None,
                                    ALU.mult).then_inc(m.r_kk, 1)
                dve.wait_ge(m.r_blk, 1)
                link(V.tensor_tensor(tx[:], tx[:], ty[:], ALU.bitwise_xor))
                for j in range(LEVELS):
                    link(V.tensor_single_scalar(ty[:], tx[:], j, ALU.logical_shift_right))
                    link(V.tensor_scalar(m.lev[:, 0, j], ty[:], 1.0, -1.0 if j == 0 else 1.0, ALU.is_equal, ALU.mult))
                    V.tensor_tensor(m.lev[:, 1, j], m.lev[:, 0, j], m.smask[:, 1], ALU.mult)
                    link(V.tensor_tensor(m.lev[:, 0, j], m.lev[:, 0, j], m.smask[:, 0], ALU.mult))
                dve.wait_ge(m.r_st_mm, 1)
                V.tensor_copy(m.st[:], ps_v[:, 0, :].rearrange("p (d q v) -> p d q v", d=2, q=MT)).then_inc(m.r_sm, 1)
                for f in range(MT):
                    dve.wait_ge(m.r_rt, f + 1)
                    link(V.tensor_scalar_max(rn[:, f % 2], rn[:, f % 2], 1e-12))
                    link(V.reciprocal(rn[:, f % 2], rn[:, f % 2]))
                    if f == 0:
                        dve.wait_ge(m.r_v_sb, NT)
                    V.tensor_tensor(m.kkn[:, f], kk[:, f], rn[:, f % 2], ALU.mult).then_inc(m.r_kkn, 1)
                dve.wait_ge(m.r_sg, 16)
                dve.wait_ge(m.r_kkn, MT)
                for d in range(2):
                    for f in range(MT):
                        V.tensor_tensor(m.bd[:, d, f], m.kkn[:, f], m.kd[:, d, f], ALU.mult)
                        link(V.tensor_scalar(m.kd[:, d, f], m.kd[:, d, f], m.pcol[:, ka0 + f:ka0 + f + 1], ka1[:, f:f + 1],
                                             ALU.mult, ALU.add))
                        last = V.tensor_tensor(m.kd[:, d, f], m.kd[:, d, f], m.zr[:, K_T + f, 0:N], ALU.mult)
                link(last)
                V.memset(m.bon[:], 0.0)
                link(V.memset(m.yo[:], 0.0))

            @block.scalar
            def _(act):
                A = nc.scalar.activation
                act.wait_ge(m.r_mu, 1)
                for t in range(RT):
                    if t >= 2:
                        act.wait_ge(m.r_sh, t - 1)
                    A(zs[:, t % 2], m.zr[:, t, 1:ZW - 1], ACT.Identity, scale=mu2[:, 0, t:t + 1]).then_inc(m.r_zs, 1)
                act.wait_ge(m.r_sh, RT)
                A(m.zr[:, LW_T, 0:N], m.zr[:, LW_T, 0:N], ACT.Tanh).then_inc(m.r_lora, 1)
                A(m.zr[:, LG_T, 0:N], m.zr[:, LG_T, 0:N], ACT.Sigmoid).then_inc(m.r_lora, 1)
                n = 0
                for kind, out, b0 in ((0, m.sig, PCOLS["rwkv_w0"][0]), (1, m.kd, PCOLS["rwkv_a0"][0])):
                    for f in range(MT):
                        for d in range(2):
                            act.wait_ge(m.r_sg_mm, n + 1)
                            b = m.pcol[:, b0 + d * MT + f:b0 + d * MT + f + 1]
                            A(out[:, d, f, 0:TS], ps_s[:, d, :], ACT.Sigmoid, bias=b)
                            A(out[:, d, f, TS:N], ps_p[:, d, 0:TP], ACT.Sigmoid, bias=b).then_inc(m.r_sg, 1)
                            n += 1
                act.wait_ge(m.r_sm, 1)
                for t in range(NT):
                    act.wait_ge(m.r_v_mm, t + 1)
                    A(m.vt[:, t], ps_v[:, t % 2, :], ACT.Identity).then_inc(m.r_v_sb, 1)
                for f in range(MT):
                    act.wait_ge(m.r_kk, f + 1)
                    if f >= 2:
                        act.wait_ge(m.r_n_mm, f - 1)
                    A(sq[:, f % 2], kk[:, f], ACT.Square).then_inc(m.r_sq, 1)
                    act.wait_ge(m.r_n_mm, f + 1)
                    if f >= 2:
                        act.wait_ge(m.r_kkn, f - 1)
                    A(rn[:, f % 2, 0:TS], ps_n[:, 0, :], ACT.Sqrt)
                    A(rn[:, f % 2, TS:N], ps_n[:, 1, 0:TP], ACT.Sqrt).then_inc(m.r_rt, 1)

            @block.tensor
            def _(pe):
                pe.wait_ge(m.r_st, 16)
                for d in range(2):
                    for q in range(MT):
                        last = nc.tensor.transpose(ps_v[:, 0, (d * MT + q) * HD:(d * MT + q + 1) * HD],
                                                   s_in[:, d, 2 * q:2 * q + 2].rearrange("v h k -> v (h k)"), m.ident[0:HD, 0:HD])
                last.then_inc(m.r_st_mm, 1)
                pe.wait_ge(m.r_w, 32)
                pe.wait_ge(m.r_lora, 2)
                n = 0
                for kind, w, tile in ((0, w2, LW_T), (1, a2, LA_T)):
                    for f in range(MT):
                        for d in range(2):
                            pr = slice(d * HD, (d + 1) * HD)
                            if n >= 2:
                                pe.wait_ge(m.r_sg, n - 1)
                            nc.tensor.matmul(ps_s[:, d, :], w[pr, f * P:(f + 1) * P], m.zr[pr, tile, 0:TS], start=True, stop=True)
                            nc.tensor.matmul(ps_p[:, d, 0:TP], w[pr, f * P:(f + 1) * P], m.zr[pr, tile, TS:N],
                                             start=True, stop=True).then_inc(m.r_sg_mm, 1)
                            n += 1
                pe.wait_ge(m.r_sm, 1)
                for t in range(NT):
                    if t >= 2:
                        pe.wait_ge(m.r_v_sb, t - 1)
                    for q in range(MT):
                        last = nc.tensor.transpose(ps_v[:, t % 2, q * P:(q + 1) * P], m.zr[:, V_T + q, t * P:(t + 1) * P], m.ident[:])
                    last.then_inc(m.r_v_mm, 1)
                pe.wait_ge(m.r_blk, 1)
                for f in range(MT):
                    pe.wait_ge(m.r_sq, f + 1)
                    if f:
                        pe.wait_ge(m.r_rt, f)
                    nc.tensor.matmul(ps_n[:, 0, :], blk[:], sq[:, f % 2, 0:TS], start=True, stop=True)
                    nc.tensor.matmul(ps_n[:, 1, 0:TP], blk[:], sq[:, f % 2, TS:N], start=True, stop=True).then_inc(m.r_n_mm, 1)


def rwkv_chunks(nc, m, a):
    STEPS = TS // P
    LJ = LEVELS - 1
    with ExitStack() as ctx:
        def sb(name, shape):
            return ctx.enter_context(nc.sbuf_tensor(name, shape, F32))
        rh, ah, kh, bh = (sb(x, [P, 2, MT, P]) for x in ("rc_r", "rc_a", "rc_k", "rc_b"))
        rkd = sb("rc_rkd", [P, MT, P])
        vs = sb("rc_v", [P, 2, MIX])
        cs, dm, dp = (sb(x, [P, MT, P]) for x in ("rc_cs", "rc_dm", "rc_dp"))
        ex = sb("rc_ex", [P, 3, MT, P])
        fs = sb("rc_fs", [P, 2, 2, MT])
        ones = sb("rc_ones", [P, P])
        lo, xi, yi, gg, lj, akt, rkt, rbt = (sb(x, [P, 2, MT, P]) for x in
                                             ("rc_l", "rc_x", "rc_y", "rc_g", "rc_lj", "rc_akt", "rc_rkt", "rc_rbt"))
        ktok, btok = sb("rc_ktok", [P, MIX]), sb("rc_btok", [P, MIX])
        sts = sb("rc_sts", [P, MT, HD])
        rhs, un = sb("rc_rhs", [P, 2, MT, HD]), sb("rc_un", [P, 2, MT, HD])
        ys = sb("rc_ys", [P, HEADS, HD])
        yq = sb("rc_yq", [P, HEADS, HD])
        mv = sb("rc_mv", [P, 4, HEADS])
        scr = sb("rc_scr", [P, 2])
        bank = [ctx.enter_context(nc.psum_tensor(f"ps_c{i}", [P, MT, P], F32)) for i in range(8)]
        (m.c_cs, m.c_d, m.c_ex, m.c_stage, m.c_gr, m.c_L, m.c_gd, m.c_y1, m.c_x1, m.c_lj, m.c_g, m.c_gsb, m.c_yg,
         m.c_xg, m.c_yup, m.c_xup, m.c_kb_mm, m.c_kb, m.c_bo_mm, m.c_bo, m.c_sts, m.c_rh_mm, m.c_rh, m.c_u_mm,
         m.c_un, m.c_y_mm, m.c_y, m.c_s_mm, m.c_s, m.c_mu, m.c_yc, m.c_sq, m.c_var, m.c_gn, m.c_one, m.c_dve,
         m.c_pl, m.c_stz, m.c_gp, m.c_scr) = sems(
            nc, m, "c_cs c_d c_ex c_stage c_gr c_L c_gd c_y1 c_x1 c_lj c_g c_gsb c_yg c_xg c_yup c_xup c_kb_mm c_kb c_bo_mm "
            "c_bo c_sts c_rh_mm c_rh c_u_mm c_un c_y_mm c_y c_s_mm c_s c_mu c_yc c_sq c_var c_gn c_one c_dve c_pl "
            "c_stz c_gp c_scr")

        def tok(i, d):
            if d == 0 or (isinstance(i, int) and i == STEPS):
                return i * P
            return (i * -P) + (STEPS - 1) * P

        def chunk(i, d):
            if d == 0 or (isinstance(i, int) and i == STEPS):
                return i
            return (i * -1) + (STEPS - 1)

        def unit(i, d):
            return i * 2 + d

        def bc4(x):
            return x.unsqueeze(1).to_broadcast([P, MT, P])

        def run(eng, body):
            body(0, 0, (0, 1))
            body(0, 1, (1, 0))
            with eng.Fori(1, STEPS) as i:
                body(i, 0, (i, 1))
                body(i, 1, (i + 1, 0))
            body(STEPS, 0, (STEPS, 1))
            body(STEPS, 1, None)

        with nc.Block() as block:

            @block.tensor
            def _(pe):
                mm = nc.tensor.matmul

                def body(i, d, nxt):
                    n = unit(i, d)
                    pe.wait_ge(m.c_stage, n + 1)
                    wait(pe, m.c_y, n * 2)
                    for e in range(2):
                        pr = slice(e * HD, (e + 1) * HD)
                        for k, (l, r) in enumerate(((ah, bh), (bh, ah), (kh, ah), (kh, rh), (bh, rh))):
                            if e:
                                if k == 0:
                                    pe.wait_ge(m.c_L, n * 2 + 1)
                                else:
                                    pe.wait_ge(m.c_gd, n * 8 + k)
                            for q in range(MT):
                                last = mm(bank[k][:, q, :], l[pr, d, q, :], r[pr, d, q, :], start=True, stop=True)
                            last.then_inc(m.c_gr, 1)
                    wait(pe, m.c_s, n)
                    for q in range(MT):
                        last = nc.tensor.transpose(bank[6][:, q, :], kh[:, d, q, :], m.ident[:])
                    last.then_inc(m.c_kb_mm, 1)
                    wait(pe, m.c_bo, n)
                    for q in range(MT):
                        last = nc.tensor.transpose(bank[7][:, q, :], bh[:, d, q, :], m.ident[:])
                    last.then_inc(m.c_kb_mm, 1)
                    pe.wait_ge(m.c_kb, n * 2 + 2)
                    for q in range(MT):
                        last = mm(bank[7][:, 0, 2 * q:2 * q + 2], rkd[:, q, :], m.rkh[:, q, :], start=True, stop=True)
                    last.then_inc(m.c_bo_mm, 1)
                    for j in range(LJ):
                        for g in range(2):
                            c = n * (2 * LJ) + 2 * j + g
                            pe.wait_ge(m.c_lj, c + 1)
                            if j == 0:
                                pe.wait_ge(m.c_y1, n * 2 + g + 1)
                                pe.wait_ge(m.c_x1, n * 2 + g + 1)
                                pe.wait_ge(m.c_gd, n * 8 + 8)
                            else:
                                pe.wait_ge(m.c_yup, c - 1)
                                pe.wait_ge(m.c_xup, n * (2 * LJ - 2) + 2 * j - 2 + g + 1)
                            for q in range(MT):
                                last = mm(bank[g][:, q, :], lj[:, g, q, :], yi[:, g, q, :], start=True, stop=True)
                            last.then_inc(m.c_g, 1)
                        for g in range(2):
                            c = n * (2 * LJ) + 2 * j + g
                            pe.wait_ge(m.c_gsb, c + 1)
                            for q in range(MT):
                                last = mm(bank[2 + g][:, q, :], xi[:, g, q, :], gg[:, g, q, :], start=True, stop=True)
                            last.then_inc(m.c_yg, 1)
                            if j < LJ - 1:
                                for q in range(MT):
                                    last = mm(bank[4 + g][:, q, :], gg[:, g, q, :], xi[:, g, q, :], start=True, stop=True)
                                last.then_inc(m.c_xg, 1)
                    pe.wait_ge(m.c_sts, n + 1)
                    for e in range(2):
                        pr = slice(e * HD, (e + 1) * HD)
                        for q in range(MT):
                            h, o = 2 * q + e, bank[e][:, q, 0:HD]
                            mm(o, ah[pr, d, q, :], sts[pr, q, :], start=True, stop=False)
                            last = mm(o, akt[:, e, q, :], vs[:, d, h * HD:(h + 1) * HD], start=False, stop=True)
                        last.then_inc(m.c_rh_mm, 1)
                    pe.wait_ge(m.c_yup, n * (2 * LJ) + 2 * LJ)
                    for e in range(2):
                        pe.wait_ge(m.c_rh, n * 2 + e + 1)
                        for q in range(MT):
                            last = mm(bank[2 + e][:, q, 0:HD], yi[:, e, q, :], rhs[:, e, q, :], start=True, stop=True)
                        last.then_inc(m.c_u_mm, 1)
                    for e in range(2):
                        pr = slice(e * HD, (e + 1) * HD)
                        pe.wait_ge(m.c_un, n * 2 + e + 1)
                        for q in range(MT):
                            h, o = 2 * q + e, bank[4 + e][:, q, 0:HD]
                            mm(o, rh[pr, d, q, :], sts[pr, q, :], start=True, stop=False)
                            mm(o, rkt[:, e, q, :], vs[:, d, h * HD:(h + 1) * HD], start=False, stop=False)
                            last = mm(o, rbt[:, e, q, :], un[:, e, q, :], start=False, stop=True)
                        last.then_inc(m.c_y_mm, 1)
                    for e in range(2):
                        pr = slice(e * HD, (e + 1) * HD)
                        for q in range(MT):
                            h = 2 * q + e
                            hc = slice(h * HD, (h + 1) * HD)
                            mm(bank[6][pr, q, 0:HD], ktok[:, hc], vs[:, d, hc], start=True, stop=False)
                            last = mm(bank[6][pr, q, 0:HD], btok[:, hc], un[:, e, q, :], start=False, stop=True)
                    last.then_inc(m.c_s_mm, 1)
                run(pe, body)

            @block.vector
            def _(dve):
                V = nc.vector

                def scans(i, d):
                    n = unit(i, d)
                    wait(dve, m.c_stage, n)
                    for q in range(MT):
                        last = V.tensor_tensor_scan(cs[:, q, :], ones[:], m.sig[:, d, q, ds(tok(i, d), P)], 0.0, ALU.mult, ALU.add)
                    last.then_inc(m.c_cs, 1)
                    dve.wait_ge(m.c_cs, n * 2 + 1)
                    V.tensor_tensor(dm[:], cs[:], cs[:, :, P // 2 - 1:P // 2].to_broadcast([P, MT, P]), ALU.subtract).then_inc(m.c_cs, 1)
                    dve.wait_ge(m.c_cs, n * 2 + 2)
                    V.tensor_tensor(dp[:], dm[:], m.sig[:, d, :, ds(tok(i, d), P)], ALU.subtract).then_inc(m.c_d, 1)

                def body(i, d, nxt):
                    n = unit(i, d)
                    if isinstance(i, int) and i == STEPS:
                        V.memset(m.st[:, d], 0.0).then_inc(m.c_stz, 1)
                        dve.wait_ge(m.c_stz, d + 1)
                    for e in range(2):
                        for k, out in ((1, yi), (2, akt), (3, rkt), (4, rbt)):
                            mk = m.lev[:, 1 - d, 0] if k == 1 else m.smask[:, 1 - d] if k == 2 else m.imask[:, 1 - d]
                            dve.wait_ge(m.c_gr, n * 10 + 5 * e + k + 1)
                            V.tensor_tensor(out[:, e], bank[k][:], bc4(mk), ALU.mult).then_inc(m.c_gd, 1)
                        dve.wait_ge(m.c_gd, n * 8 + 4 * e + 1)
                        V.tensor_tensor(yi[:, e], yi[:, e], bc4(m.ident[:]), ALU.add).then_inc(m.c_y1, 1)
                    dve.wait_ge(m.c_bo_mm, n + 1)
                    V.tensor_tensor(m.bon[:, ds(chunk(i, d), 1), :], m.bon[:, ds(chunk(i, d), 1), :],
                                    bank[7][:, 0:1, 0:HEADS], ALU.add).then_inc(m.c_bo, 1)
                    for j in range(LJ):
                        for g in range(2):
                            c = n * (2 * LJ) + 2 * j + g
                            dve.wait_ge(m.c_yg, c + 1)
                            V.tensor_tensor(yi[:, g], yi[:, g], bank[2 + g][:], ALU.subtract).then_inc(m.c_yup, 1)
                            if j < LJ - 1:
                                dve.wait_ge(m.c_xg, n * (2 * LJ - 2) + 2 * j + g + 1)
                                V.tensor_tensor(xi[:, g], xi[:, g], bank[4 + g][:], ALU.subtract).then_inc(m.c_xup, 1)
                        if j == 0 and nxt:
                            scans(*nxt)
                        if j == 1:
                            wait(dve, m.c_s_mm, n)
                            wait(dve, m.c_dve, n * 3)
                            dve.wait_ge(m.c_ex, n + 1)
                            V.tensor_tensor(sts[:], m.st[:, d], fs[:, d, 0].unsqueeze(2).to_broadcast([P, MT, HD]),
                                            ALU.mult).then_inc(m.c_sts, 1)
                    dve.wait_ge(m.c_s_mm, n + 1)
                    V.tensor_tensor(m.st[:, d], sts[:], bank[6][:, :, 0:HD], ALU.add).then_inc(m.c_s, 1)
                    dve.wait_ge(m.c_s, n + 1)
                    V.tensor_tensor(m.st[:, d], m.st[:, d], fs[:, d, 1].unsqueeze(2).to_broadcast([P, MT, HD]),
                                    ALU.mult).then_inc(m.c_dve, 1)
                    dve.wait_ge(m.c_y, n * 2 + 2)
                    V.tensor_reduce(mv[:, 0], ys[:], AX.X, ALU.add).then_inc(m.c_dve, 1)
                    dve.wait_ge(m.c_dve, n * 3 + 2)
                    V.tensor_scalar(mv[:, 1], mv[:, 0], 1.0 / HD, None, ALU.mult).then_inc(m.c_mu, 1)
                    dve.wait_ge(m.c_sq, n + 1)
                    V.tensor_reduce(mv[:, 2], yq[:], AX.X, ALU.add).then_inc(m.c_dve, 1)
                    dve.wait_ge(m.c_dve, n * 3 + 3)
                    V.tensor_scalar(mv[:, 3], mv[:, 2], 1.0 / HD, GN_EPS, ALU.mult, ALU.add).then_inc(m.c_var, 1)
                V.memset(ones[:], 1.0).then_inc(m.c_one, 1)
                dve.wait_ge(m.c_one, 1)
                scans(0, 0)
                run(dve, body)

            @block.scalar
            def _(act):
                A = nc.scalar.activation

                def exps(i, d):
                    n = unit(i, d)
                    act.wait_ge(m.c_d, n + 1)
                    c = DECAY_C
                    A(ex[:, 0], dm[:] if d == 0 else dp[:], ACT.Exp, scale=-c if d == 0 else c)
                    A(ex[:, 1], dm[:] if d == 0 else dp[:], ACT.Exp, scale=c if d == 0 else -c)
                    A(ex[:, 2], dp[:] if d == 0 else dm[:], ACT.Exp, scale=-c if d == 0 else c)
                    A(fs[:, d, d], cs[:, :, P // 2 - 1], ACT.Exp, scale=-c)
                    A(fs[:, d, 1 - d], dm[:, :, P - 1], ACT.Exp, scale=-c).then_inc(m.c_ex, 1)

                def body(i, d, nxt):
                    n = unit(i, d)
                    for e in range(2):
                        act.wait_ge(m.c_gr, n * 10 + 5 * e + 1)
                        A(lo[:, e], bank[0][:], ACT.Identity).then_inc(m.c_L, 1)
                    for k, out in ((6, ktok), (7, btok)):
                        act.wait_ge(m.c_kb_mm, n * 2 + k - 5)
                        A(out[:], bank[k][:].rearrange("p q c -> p (q c)"), ACT.Identity).then_inc(m.c_kb, 1)
                    for j in range(LJ):
                        for g in range(2):
                            c = n * (2 * LJ) + 2 * j + g
                            act.wait_ge(m.c_g, c + 1)
                            A(gg[:, g], bank[g][:], ACT.Identity).then_inc(m.c_gsb, 1)
                        if j == 2 and nxt:
                            exps(*nxt)
                    for e in range(2):
                        act.wait_ge(m.c_rh_mm, n * 2 + e + 1)
                        A(rhs[:, e], bank[e][:, :, 0:HD], ACT.Identity).then_inc(m.c_rh, 1)
                    for e in range(2):
                        act.wait_ge(m.c_u_mm, n * 2 + e + 1)
                        A(un[:, e], bank[2 + e][:, :, 0:HD], ACT.Identity, scale=-1.0).then_inc(m.c_un, 1)
                    wait(act, m.c_gn, n)
                    for e in range(2):
                        act.wait_ge(m.c_y_mm, n * 2 + e + 1)
                        A(ys[:, e:HEADS:2, :], bank[4 + e][:, :, 0:HD], ACT.Identity).then_inc(m.c_y, 1)
                    act.wait_ge(m.c_yc, n + 1)
                    A(yq[:], ys[:], ACT.Square).then_inc(m.c_sq, 1)
                exps(0, 0)
                run(act, body)

            @block.gpsimd
            def _(pool):
                G = nc.gpsimd

                def absorb():
                    G.tensor_tensor(scr[:, 0:1], scr[:, 1:2], scr[:, 1:2], ALU.add)

                def hats(i, d):
                    n = unit(i, d)
                    t = ds(tok(i, d), P)
                    pool.wait_ge(m.c_ex, n + 1)
                    wait(pool, m.c_s_mm, n - 1)
                    wait(pool, m.c_bo_mm, n)
                    absorb()
                    G.tensor_tensor(rkd[:], m.zr[:, R_T:R_T + MT, t], m.kd[:, d, :, t], ALU.mult)
                    G.tensor_tensor(rh[:, d], m.zr[:, R_T:R_T + MT, t], ex[:, 0], ALU.mult)
                    G.tensor_tensor(ah[:, d], m.kkn[:, :, t], ex[:, 2], ALU.mult)
                    G.tensor_tensor(kh[:, d], m.kd[:, d, :, t], ex[:, 1], ALU.mult)
                    G.tensor_copy(vs[:, d], m.vt[:, ds(chunk(i, d), 1), :].rearrange("p a c -> p (a c)"))
                    G.tensor_tensor(bh[:, d], m.bd[:, d, :, t], ex[:, 1], ALU.mult).then_inc(m.c_stage, 1)

                def body(i, d, nxt):
                    n = unit(i, d)
                    for e in range(2):
                        pool.wait_ge(m.c_L, n * 2 + e + 1)
                        G.tensor_tensor(xi[:, e], lo[:, e], bc4(m.lev[:, d, 0]), ALU.mult).then_inc(m.c_pl, 1)
                        pool.wait_ge(m.c_pl, n * 2 + e + 1)
                        G.tensor_tensor(xi[:, e], xi[:, e], bc4(m.ident[:]), ALU.add).then_inc(m.c_x1, 1)
                    for j in range(LJ):
                        for g in range(2):
                            c = n * (2 * LJ) + 2 * j + g
                            if j:
                                pool.wait_ge(m.c_g, c - 1)
                            G.tensor_tensor(lj[:, g], lo[:, g], bc4(m.lev[:, d, j + 1]), ALU.mult).then_inc(m.c_lj, 1)
                        if j == 4 and nxt:
                            hats(*nxt)
                    pool.wait_ge(m.c_mu, n + 1)
                    G.tensor_tensor(ys[:], ys[:], mv[:, 1].unsqueeze(2).to_broadcast([P, HEADS, HD]), ALU.subtract).then_inc(m.c_yc, 1)
                    pool.wait_ge(m.c_var, n + 1)
                    G.tensor_tensor(mv[:, 3], mv[:, 3], m.neghalf[:], ALU.pow).then_inc(m.c_gp, 1)
                    pool.wait_ge(m.c_gp, n * 2 + 1)
                    G.tensor_tensor(ys[:], ys[:], mv[:, 3].unsqueeze(2).to_broadcast([P, HEADS, HD]), ALU.mult).then_inc(m.c_gp, 1)
                    pool.wait_ge(m.c_gp, n * 2 + 2)
                    wait(pool, m.c_gn, n)
                    absorb()
                    yo = m.yo[:, ds(chunk(i, d), 1), :].rearrange("p a c -> p (a c)")
                    G.tensor_tensor(yo, yo, ys[:].rearrange("p h v -> p (h v)"), ALU.add).then_inc(m.c_gn, 1)
                G.memset(scr[:], 0.0).then_inc(m.c_scr, 1)
                pool.wait_ge(m.c_scr, 1)
                hats(0, 0)
                run(pool, body)


def rwkv_finish(nc, m, a):
    with ExitStack() as ctx:
        def sb(name, shape):
            return ctx.enter_context(nc.sbuf_tensor(name, shape, F32))
        ya = m.sig[:, 0]
        g2 = sb("rf_g2", [P, MIX])
        gg_ = sb("rf_gng", [P, MIX])
        gb = sb("rf_gnb", [P, MIX])
        bv = sb("rf_bv", [P, 2, HEADS, HD])
        so = sb("rf_so", [HD, 2, HEADS, HD])
        ps_g = ctx.enter_context(nc.psum_tensor("ps_fg", [P, 2, 512], F32))
        ps_t = ctx.enter_context(nc.psum_tensor("ps_ft", [P, 2, 512], F32))
        ps_s = ctx.enter_context(nc.psum_tensor("ps_fs", [P, 2, 512], F32))
        (m.f_w, m.f_gn, m.f_g_mm, m.f_bv, m.f_y, m.f_t_mm, m.f_t, m.f_s_mm, m.f_s, m.f_out, m.f_dve, m.f_ya) = sems(
            nc, m, "f_w f_gn f_g_mm f_bv f_y f_t_mm f_t f_s_mm f_s f_out f_dve f_ya")
        with nc.Block() as block:

            @block.sync
            def _(sp):
                sp.dma_start(g2[:], a["rwkv_g2"]).then_inc(m.f_w, 16)
                sp.dma_start(gg_[:], a["rwkv_gn_g"].partition_broadcast(P)).then_inc(m.f_gn, 16)
                sp.dma_start(gb[:], a["rwkv_gn_b"].partition_broadcast(P)).then_inc(m.f_gn, 16)
                sp.wait_ge(m.f_s, 2)
                sp.dma_start(a["new_rwkv"].rearrange("d h v k -> v d h k"), so[:]).then_inc(m.f_out, 16)
                sp.wait_ge(m.f_t, NT)
                sp.dma_start(m.y_dram[0], ya).then_inc(m.f_ya, 16)
                sp.wait_ge(m.f_ya, 16)
                sp.wait_ge(m.f_out, 16)

            @block.tensor
            def _(pe):
                for d in range(2):
                    for q in range(MT):
                        last = nc.tensor.transpose(ps_s[0:HD, d, q * P:(q + 1) * P], m.st[:, d, q, :], m.ident[:])
                    last.then_inc(m.f_s_mm, 1)
                pe.wait_ge(m.f_w, 16)
                for t in range(NT):
                    if t >= 2:
                        pe.wait_ge(m.f_y, t - 1)
                    nc.tensor.matmul(ps_g[:, t % 2, :], m.zr[:, LG_T, t * P:(t + 1) * P], g2[:], start=True, stop=True).then_inc(m.f_g_mm, 1)
                for t in range(NT):
                    pe.wait_ge(m.f_y, t + 1)
                    if t >= 2:
                        pe.wait_ge(m.f_t, t - 1)
                    for q in range(MT):
                        last = nc.tensor.transpose(ps_t[:, t % 2, q * P:(q + 1) * P], m.yo[:, t, q * P:(q + 1) * P], m.ident[:])
                    last.then_inc(m.f_t_mm, 1)

            @block.gpsimd
            def _(pool):
                for t in range(NT):
                    if t >= 2:
                        pool.wait_ge(m.f_y, t - 1)
                    nc.gpsimd.tensor_tensor(bv[:, t % 2], m.vt[:, t].rearrange("p (h v) -> p h v", h=HEADS),
                                            m.bon[:, t].unsqueeze(2).to_broadcast([P, HEADS, HD]), ALU.mult).then_inc(m.f_bv, 1)

            @block.vector
            def _(dve):
                V = nc.vector
                link = Chain(dve, m.f_dve)
                dve.wait_ge(m.f_gn, 32)
                for t in range(NT):
                    y = m.yo[:, t]
                    link(V.tensor_tensor(y, y, gg_[:], ALU.mult))
                    link(V.scalar_tensor_tensor(y, gb[:], 2.0, y, ALU.mult, ALU.add))
                    dve.wait_ge(m.f_bv, t + 1)
                    link(V.tensor_tensor(y, y, bv[:, t % 2].rearrange("p h v -> p (h v)"), ALU.add))
                    dve.wait_ge(m.f_g_mm, t + 1)
                    V.tensor_tensor(y, y, ps_g[:, t % 2, :], ALU.mult).then_inc(m.f_y, 1)

            @block.scalar
            def _(act):
                for d in range(2):
                    act.wait_ge(m.f_s_mm, d + 1)
                    nc.scalar.activation(so[:, d].rearrange("v h k -> v (h k)"), ps_s[0:HD, d, :], ACT.Identity).then_inc(m.f_s, 1)
                for t in range(NT):
                    act.wait_ge(m.f_t_mm, t + 1)
                    nc.scalar.activation(ya[:, :, t * P:(t + 1) * P], ps_t[:, t % 2, :].rearrange("p (q c) -> p q c", q=MT),
                                         ACT.Identity).then_inc(m.f_t, 1)


def mm3(nc, out, w_hi, w_lo, x_hi, x_lo, first, last):
    nc.tensor.matmul(out, w_hi, x_hi, start=first, stop=False)
    nc.tensor.matmul(out, w_hi, x_lo, start=False, stop=False)
    return nc.tensor.matmul(out, w_lo, x_hi, start=False, stop=last)


def merge_phase(nc, m, a):
    FT = D // P
    NH = N // 2
    mT = m.mT
    with ExitStack() as c2:
        def sb2(name, shape, dt=F32):
            return c2.enter_context(nc.sbuf_tensor(name, shape, dt))
        h_hi, h_lo = sb2("mg_hh", [P, KT, N], F32R), sb2("mg_hl", [P, KT, N], F32R)
        y_hi, y_lo = sb2("mg_yh", [P, 3, MT, N], F32R), sb2("mg_yl", [P, 3, MT, N], F32R)
        x1_flat = m.x1[:].rearrange("p t d -> p (t d)")
        y_in = [x1_flat[:, b * MT * N:(b + 1) * MT * N].rearrange("p (k n) -> p k n", k=MT) for b in range(2)]
        y_in.append(sb2("mg_yin", [P, MT, N])[:])
        w = sb2("mg_w", [P, 3, KT + MT, P])
        w_hi, w_lo = sb2("mg_wh", [P, 2, KT + MT, P], F32R), sb2("mg_wl", [P, 2, KT + MT, P], F32R)
        gs = sb2("mg_gs", [P, 2, N])
        pr = sb2("mg_pr", [P, 2, N])
        pg_0, pb_0 = (c2.enter_context(nc.psum_tensor(x, [P, 2, 512], F32)) for x in ("ps_g0", "ps_b0"))
        pg_1, pb_1 = (c2.enter_context(nc.psum_tensor(x, [P, 2, 512], F32)) for x in ("ps_g1", "ps_b1"))
        (m.g_h, m.g_y0, m.g_y1, m.g_y2, m.g_w0, m.g_w1, m.g_w2, m.g_hi, m.g_lo, m.g_yhi, m.g_ylo, m.g_whi,
         m.g_wlo, m.g_g_mm, m.g_b_mm, m.g_gs, m.g_pr, m.g_sum) = sems(
            nc, m, "g_h g_y0 g_y1 g_y2 g_w0 g_w1 g_w2 g_hi g_lo g_yhi g_ylo g_whi g_wlo g_g_mm g_b_mm g_gs g_pr g_sum")
        land, y_land = [m.g_w0, m.g_w1, m.g_w2], [m.g_y0, m.g_y1, m.g_y2]
        w_br = a["w_branch"].rearrange("n (k p) d -> n p k d", p=P)

        def run(eng, six):
            six(0)
            with eng.Fori(1, FT // 2 - 1) as i:
                six(i)
            six(FT // 2 - 1)

        with nc.Block() as block:

            @block.sync
            def _(sp):
                for k in range(KT):
                    sp.dma_start(mT[:, k], m.h1_dram[k]).then_inc(m.g_h, 16)

                def six(i):
                    for j in range(6):
                        r, n = j % 3, j % 3
                        wait(sp, m.g_wlo, i * 6 + j - 2)
                        c = (i * 2 + j // 3) * P
                        sp.dma_start(w[:, r, 0:KT], a["w_in_t"][:, :, ds(c + GCOL + n * D, P)]).then_inc(land[r], 16)
                        sp.dma_start(w[:, r, KT:], w_br[n, :, :, ds(c, P)]).then_inc(land[r], 16)
                        if isinstance(i, int) and j < 3:
                            sp.dma_start(y_in[j], m.y_dram[j]).then_inc(y_land[j], 16)
                run(sp, six)

            @block.gpsimd
            def _(pool):
                G = nc.gpsimd

                def six(i):
                    for j in range(6):
                        t, b, r = i * 6 + j, j % 2, j % 3
                        pool.wait_ge(m.g_whi, t + 1)
                        G.tensor_tensor(w_lo[:, b], w[:, r], w_hi[:, b].bitcast(F32), ALU.subtract).then_inc(m.g_wlo, 1)
                run(pool, six)

            @block.tensor
            def _(pe):
                def six(i):
                    for j in range(6):
                        b, n, t = j % 2, j % 3, i * 6 + j
                        pe.wait_ge(m.g_wlo, t + 1)
                        wait(pe, m.g_gs, t - 1)
                        if isinstance(t, int) and t == 0:
                            pe.wait_ge(m.g_lo, KT)
                        for o, sl in ((pg_0[:, b, 0:NH], slice(0, NH)), (pg_1[:, b, 0:NH], slice(NH, N))):
                            for k in range(KT):
                                last = mm3(nc, o, w_hi[:, b, k, :], w_lo[:, b, k, :], h_hi[:, k, sl], h_lo[:, k, sl],
                                           k == 0, k == KT - 1)
                        last.then_inc(m.g_g_mm, 1)
                        if isinstance(t, int) and t < 3:
                            pe.wait_ge(m.g_ylo, t + 1)
                        wait(pe, m.g_pr, t - 1)
                        for o, sl in ((pb_0[:, b, 0:NH], slice(0, NH)), (pb_1[:, b, 0:NH], slice(NH, N))):
                            for k in range(MT):
                                last = mm3(nc, o, w_hi[:, b, KT + k, :], w_lo[:, b, KT + k, :], y_hi[:, n, k, sl],
                                           y_lo[:, n, k, sl], k == 0, k == MT - 1)
                        last.then_inc(m.g_b_mm, 1)
                run(pe, six)

            @block.scalar
            def _(act):
                A = nc.scalar.activation

                def rounded(i, j):
                    act.wait_ge(land[j % 3], i * 64 + (j // 3) * 32 + 32)
                    wait(act, m.g_b_mm, i * 6 + j - 1)
                    A(w_hi[:, j % 2], w[:, j % 3], ACT.Identity).then_inc(m.g_whi, 1)

                def six(i):
                    for j in range(6):
                        t, b = i * 6 + j, j % 2
                        if j < 5:
                            rounded(i, j + 1)
                        elif not (isinstance(i, int) and i == FT // 2 - 1):
                            rounded(i + 1, 0)
                        if isinstance(t, int) and t < 3:
                            act.wait_ge(y_land[t], 16)
                            A(y_hi[:, t], y_in[t], ACT.Identity).then_inc(m.g_yhi, 1)
                        act.wait_ge(m.g_g_mm, t + 1)
                        wait(act, m.g_pr, t - 1)
                        A(gs[:, b, 0:NH], pg_0[:, b, 0:NH], ACT.Sigmoid)
                        A(gs[:, b, NH:N], pg_1[:, b, 0:NH], ACT.Sigmoid).then_inc(m.g_gs, 1)
                act.wait_ge(m.g_h, 16 * KT)
                for k in range(KT):
                    A(h_hi[:, k], mT[:, k], ACT.Identity).then_inc(m.g_hi, 1)
                rounded(0, 0)
                run(act, six)

            @block.vector
            def _(dve):
                V = nc.vector

                def six(i):
                    for j in range(6):
                        t, b, n = i * 6 + j, j % 2, j % 3
                        if isinstance(t, int) and t < 3:
                            dve.wait_ge(m.g_yhi, t + 1)
                            V.tensor_tensor(y_lo[:, t], y_in[t], y_hi[:, t].bitcast(F32), ALU.subtract).then_inc(m.g_ylo, 1)
                        dve.wait_ge(m.g_b_mm, t + 1)
                        dve.wait_ge(m.g_gs, t + 1)
                        wait(dve, m.g_sum, t)
                        V.tensor_tensor(pr[:, b, 0:NH], gs[:, b, 0:NH], pb_0[:, b, 0:NH], ALU.mult)
                        V.tensor_tensor(pr[:, b, NH:N], gs[:, b, NH:N], pb_1[:, b, 0:NH], ALU.mult).then_inc(m.g_pr, 1)
                        dve.wait_ge(m.g_pr, t + 1)
                        o = mT[:, ds(i * 2 + j // 3, 1), :].rearrange("p a c -> p (a c)")
                        if n == 0:
                            V.tensor_scalar(o, pr[:, b, :], 1.0, None, ALU.mult).then_inc(m.g_sum, 1)
                        else:
                            V.tensor_tensor(o, o, pr[:, b, :], ALU.add).then_inc(m.g_sum, 1)
                for k in range(KT):
                    dve.wait_ge(m.g_hi, k + 1)
                    V.tensor_tensor(h_lo[:, k], mT[:, k], h_hi[:, k].bitcast(F32), ALU.subtract).then_inc(m.g_lo, 1)
                run(dve, six)



def residual_phase(nc, m, a):
    FT = D // P
    mT = m.mT
    with ExitStack() as c2:
        def sb3(name, shape):
            return c2.enter_context(nc.sbuf_tensor(name, shape, F32))
        wo = sb3("mg_wo", [P, FT, D])
        g1 = sb3("mg_g1", [P, 2, D])
        s2, b2 = sb3("mg_s2", [P, 2, D]), sb3("mg_b2", [P, 2, D])
        h2 = sb3("mg_h2", [P, 2, D])
        lng, lnb = sb3("mg_lng", [P, D]), sb3("mg_lnb", [P, D])
        tp = sb3("mg_tp", [P, 2, D])
        st = sb3("mg_st", [P, NT, 2, 6])
        mv = sb3("mg_mv", [P, NT, 4])
        ps_o = c2.enter_context(nc.psum_tensor("ps_mo", [P, 2, D], F32))
        ps_t = c2.enter_context(nc.psum_tensor("ps_mtr", [P, 2, D], F32))
        (m.o_h2, m.o_hw0, m.o_hw1, m.o_w, m.o_x, m.o_g, m.o_mm, m.o_dve, m.o_sq, m.o_nrm, m.o_ln, m.o_t_mm,
         m.o_ht, m.o_tp, m.o_pl, m.o_sqv) = sems(
            nc, m, "o_h2 o_hw0 o_hw1 o_w o_x o_g o_mm o_dve o_sq o_nrm o_ln o_t_mm o_ht o_tp o_pl o_sqv")
        m.o_hw = [m.o_hw0, m.o_hw1]
        with nc.Block() as block:

            @block.sync
            def _(sp):
                sp.dma_start(wo[:], a["w_out"].rearrange("(k p) d -> p k d", p=P)).then_inc(m.o_w, 16)
                sp.dma_start(m.x1[:, 0:NT - 1], a["x_sample"].rearrange("(t p) d -> p t d", p=P)).then_inc(m.o_x, 16)
                sp.dma_start(m.x1[:, NT - 1], a["x_prompt"]).then_inc(m.o_x, 16)
                for t in range(NT):
                    sp.wait_ge(m.o_h2, t + 1)
                    sp.dma_start(m.h2_dram[t * P:(t + 1) * P, :], h2[:, t % 2]).then_inc(m.o_hw[t % 2], 16)
                sp.wait_ge(m.o_hw[0], 16 * ((NT + 1) // 2))
                sp.wait_ge(m.o_hw[1], 16 * (NT // 2))

            @block.scalar
            def _(act):
                for c in range(2):
                    for row, which in ((g1, GATE1), (s2, SCALE2), (b2, SHIFT2)):
                        act.dma_start(row[:, c], m.mods_dram[c, which * D:(which + 1) * D].partition_broadcast(P)).then_inc(m.o_g, 16)
                act.dma_start(lng[:], a["ln1_g"].partition_broadcast(P)).then_inc(m.o_g, 16)
                act.dma_start(lnb[:], a["ln1_b"].partition_broadcast(P)).then_inc(m.o_g, 16)

                def turned(t):
                    act.wait_ge(m.o_t_mm, t + 1)
                    nc.scalar.activation(m.h2T[:, :, t * P:(t + 1) * P], ps_t[:, t % 2].rearrange("p (k c) -> p k c", k=KT),
                                         ACT.Identity).then_inc(m.o_ht, 1)
                for t in range(NT):
                    act.wait_ge(m.o_sqv, t + 1)
                    nc.scalar.activation(mv[:, t, 3:4], mv[:, t, 2:3], ACT.Sqrt).then_inc(m.o_sq, 1)
                    if t:
                        turned(t - 1)
                turned(NT - 1)

            @block.tensor
            def _(pe):
                pe.wait_ge(m.o_w, 16)

                def turn(t):
                    pe.wait_ge(m.o_h2, t + 1)
                    if t >= 2:
                        pe.wait_ge(m.o_ht, t - 1)
                    for k in range(KT):
                        last = nc.tensor.transpose(ps_t[:, t % 2, k * P:(k + 1) * P], h2[:, t % 2, k * P:(k + 1) * P], m.ident[:])
                    last.then_inc(m.o_t_mm, 1)
                for t in range(NT):
                    if t >= 2:
                        pe.wait_ge(m.o_tp, t - 1)
                    for h in range(2):
                        for k in range(FT):
                            last = nc.tensor.matmul(ps_o[:, t % 2, ts512(h)], mT[:, k, t * P:(t + 1) * P], wo[:, k, ts512(h)],
                                                    start=(k == 0), stop=(k == FT - 1))
                    last.then_inc(m.o_mm, 1)
                    if t:
                        turn(t - 1)
                turn(NT - 1)

            @block.vector
            def _(dve):
                V = nc.vector
                link = Chain(dve, m.o_dve)
                dve.wait_ge(m.o_x, 32)
                dve.wait_ge(m.o_g, 128)
                link(V.tensor_scalar_add(s2[:], s2[:], 1.0))

                def modulate(t):
                    c = t // (NT - 1)
                    dve.wait_ge(m.o_ln, t + 1)
                    if t >= 2:
                        dve.wait_ge(m.o_t_mm, t - 1)
                        dve.wait_ge(m.o_hw[t % 2], 16 * (t // 2))
                    link(V.tensor_tensor(h2[:, t % 2], m.x1[:, t], s2[:, c], ALU.mult))
                    V.tensor_tensor(h2[:, t % 2], h2[:, t % 2], b2[:, c], ALU.add).then_inc(m.o_h2, 1)
                for t in range(NT):
                    x, c = m.x1[:, t], t // (NT - 1)
                    dve.wait_ge(m.o_mm, t + 1)
                    V.tensor_tensor(tp[:, t % 2], ps_o[:, t % 2], g1[:, c], ALU.mult).then_inc(m.o_tp, 1)
                    dve.wait_ge(m.o_tp, t + 1)
                    link(V.scalar_tensor_tensor(x, x, ALPHA, tp[:, t % 2], ALU.mult, ALU.add))
                    norm_stats(V, dve, link, m, x, st[:, t], mv[:, t], m.o_sqv, m.o_sq, t)
                    V.tensor_scalar(x, x, mv[:, t, 0:1], mv[:, t, 3:4], ALU.subtract, ALU.mult).then_inc(m.o_nrm, 1)
                    if t:
                        modulate(t - 1)
                modulate(NT - 1)

            @block.gpsimd
            def _(pool):
                for t in range(NT):
                    x = m.x1[:, t]
                    pool.wait_ge(m.o_nrm, t + 1)
                    nc.gpsimd.tensor_tensor(x, x, lng[:], ALU.mult).then_inc(m.o_pl, 1)
                    pool.wait_ge(m.o_pl, t + 1)
                    nc.gpsimd.tensor_tensor(x, x, lnb[:], ALU.add).then_inc(m.o_ln, 1)


def norm_stats(V, dve, link, m, x, st, mv, sqv, sq, t):
    V.bn_stats(st[:, 0], x[:, 0:512])
    link(V.bn_stats(st[:, 1], x[:, 512:1024]))
    link(V.bn_aggr(mv[:, 0:2], st.rearrange("p s c -> p (s c)")))
    V.tensor_scalar_add(mv[:, 2:3], mv[:, 1:2], LN_EPS).then_inc(sqv, 1)
    dve.wait_ge(sq, t + 1)
    link(V.reciprocal(mv[:, 3:4], mv[:, 3:4]))




SLOTS = P
JOBS = (N * TOPK + E_N * (SLOTS - 1)) // SLOTS + 1
PAIRS = (JOBS + 1) // 2
JCOLS = 2 * PAIRS + 2


def router_phase(nc, m, a):
    GE = E_N // EGROUPS
    with ExitStack() as ctx:
        def sb(name, shape, dt=F32):
            return ctx.enter_context(nc.sbuf_tensor(name, shape, dt))
        rw = sb("ro_w", [P, KT, E_N])
        rb = sb("ro_b", [P, E_N])
        sc, sel, rep = sb("ro_sc", [P, NT, E_N]), sb("ro_sel", [P, NT, E_N]), sb("ro_rep", [P, NT, E_N])
        chosen, gates, slot = sb("ro_ch", [P, NT, E_N]), sb("ro_gates", [P, NT, E_N]), sb("ro_slot", [P, NT, E_N])
        m8 = sb("ro_m8", [P, NT, EGROUPS, 8])
        top = sb("ro_top", [P, NT, 8])
        grp, rank = sb("ro_grp", [P, NT, EGROUPS]), sb("ro_rank", [P, NT, EGROUPS])
        gt, eq = sb("ro_gt", [P, NT, EGROUPS, EGROUPS]), sb("ro_eq", [P, NT, EGROUPS, EGROUPS])
        low = sb("ro_low", [P, EGROUPS, EGROUPS])
        sm = sb("ro_sum", [P, NT])
        before, ones = sb("ro_before", [P, P]), sb("ro_ones", [P, P])
        col_i, tok_i = sb("ro_coli", [P, P], I32), sb("ro_toki", [P, NT * TOPK + 1], I32)
        col, tok = sb("ro_col", [P, P]), sb("ro_tok", [P, NT * TOPK + 1])
        cnt, nb, end, start = (sb(x, [P, E_N]) for x in ("ro_cnt", "ro_nb", "ro_end", "ro_start"))
        pick = sb("ro_pick", [P, NT, TOPK, E_N])
        pl, job, place = (sb(x, [P, NT, TOPK]) for x in ("ro_pl", "ro_job", "ro_place"))
        hot_p, hot_j = sb("ro_hotp", [P, NT * TOPK, P]), sb("ro_hotj", [P, NT * TOPK, JCOLS])
        je = sb("ro_je", [P, 2])
        wg, wu = sb("sh_wg", [P, KT, E_F]), sb("sh_wu", [P, KT, E_F])
        wd = sb("sh_wd", [P, D])
        sg, hu, hh = sb("sh_sg", [P, N]), sb("sh_hu", [P, N]), sb("sh_hh", [P, N])
        ps = ctx.enter_context(nc.psum_tensor("ps_ro", [P, NT, E_N], F32))
        ps_c = ctx.enter_context(nc.psum_tensor("ps_rc", [P, NT + 1, E_N], F32))
        ps_j = ctx.enter_context(nc.psum_tensor("ps_rj", [P, 512], F32))
        pg = ctx.enter_context(nc.psum_tensor("ps_sg", [P, 2, 512], F32))
        pd = ctx.enter_context(nc.psum_tensor("ps_sd", [P, 2, 512], F32))
        (m.t_w, m.t_b, m.t_mm, m.t_sc, m.t_const, m.t_iota, m.t_dve, m.t_ch, m.t_cnt, m.t_hot, m.t_tid, m.t_je,
         m.t_row, m.u_w, m.u_wd, m.u_g, m.u_sg, m.u_u, m.u_hu, m.u_hh, m.u_dn, m.u_acc) = sems(
            nc, m, "t_w t_b t_mm t_sc t_const t_iota t_dve t_ch t_cnt t_hot t_tid t_je t_row u_w u_wd u_g u_sg u_u u_hu u_hh "
            "u_dn u_acc")
        with nc.Block() as block:

            @block.sync
            def _(sp):
                sp.dma_start(rw[:], a["router_w"].rearrange("(k p) e -> p k e", p=P)).then_inc(m.t_w, 16)
                sp.dma_start(rb[:], a["router_bias"].partition_broadcast(P)).then_inc(m.t_b, 16)
                sp.dma_start(wg[:], a["sh_w_gate"].rearrange("(k p) f -> p k f", p=P)).then_inc(m.u_w, 16)
                sp.dma_start(wu[:], a["sh_w_up"].rearrange("(k p) f -> p k f", p=P)).then_inc(m.u_w, 16)
                sp.dma_start(wd[:], a["sh_w_down"]).then_inc(m.u_wd, 16)

            @block.gpsimd
            def _(pool):
                G = nc.gpsimd
                G.memset(low[:], 1.0)
                G.memset(before[:], 1.0)
                G.memset(ones[:], 1.0)
                G.iota(col_i[:], pattern=[[1, P]], base=0, channel_multiplier=0)
                G.iota(tok_i[:, 0:NT * TOPK].rearrange("p (t j) -> p t j", t=NT), pattern=[[TOPK * P, NT], [1, TOPK]], base=1,
                       channel_multiplier=TOPK)
                G.iota(tok_i[:, NT * TOPK:], pattern=[[0, 1]], base=0, channel_multiplier=1).then_inc(m.t_iota, 1)
                pool.wait_ge(m.t_iota, 1)
                G.affine_select(out=low[:], in_=low[:], compare_op=ALU.is_ge, fill=0.0, base=-1,
                                pattern=[[1, EGROUPS], [-1, EGROUPS]], channel_multiplier=0)
                G.affine_select(out=before[:], in_=before[:], compare_op=ALU.is_ge, fill=0.0, base=-1,
                                pattern=[[1, P]], channel_multiplier=-1)
                G.tensor_copy(col[:], col_i[:])
                G.tensor_copy(tok[:], tok_i[:]).then_inc(m.t_const, 1)
                pool.wait_ge(m.u_sg, 1)
                pool.wait_ge(m.u_hu, 1)
                G.tensor_tensor(hh[:], sg[:], hu[:], ALU.mult).then_inc(m.u_hh, 1)

            @block.tensor
            def _(pe):
                mm = nc.tensor.matmul
                pe.wait_ge(m.t_w, 16)
                for t in range(NT):
                    for k in range(KT):
                        last = mm(ps[:, t, :], m.h2T[:, k, t * P:(t + 1) * P], rw[:, k, :], start=(k == 0), stop=(k == KT - 1))
                last.then_inc(m.t_mm, 1)
                pe.wait_ge(m.u_w, 32)
                for w, done in ((wg, m.u_g), (wu, m.u_u)):
                    if w is wu:
                        pe.wait_ge(m.u_sg, 1)
                    for o, sl in ((pg[:, 0, :], slice(0, TS)), (pg[:, 1, 0:TP], slice(TS, N))):
                        for k in range(KT):
                            last = mm(o, w[:, k, :], m.h2T[:, k, sl], start=(k == 0), stop=(k == KT - 1))
                    last.then_inc(done, 1)
                pe.wait_ge(m.u_wd, 16)
                pe.wait_ge(m.u_hh, 1)
                for t in range(NT):
                    for h in range(2):
                        n = 2 * t + h
                        if n >= 2:
                            pe.wait_ge(m.u_acc, n - 1)
                        mm(pd[:, h, :], hh[:, t * P:(t + 1) * P], wd[:, ts512(h)], start=True, stop=True).then_inc(m.u_dn, 1)
                pe.wait_ge(m.t_ch, 1)
                for t in range(NT):
                    for u in range(t):
                        mm(ps_c[:, t, :], ones[:], chosen[:, u, :], start=(u == 0), stop=False)
                    mm(ps_c[:, t, :], before[:], chosen[:, t, :], start=(t == 0), stop=True)
                for u in range(NT):
                    last = mm(ps_c[:, NT, :], ones[:], chosen[:, u, :], start=(u == 0), stop=(u == NT - 1))
                last.then_inc(m.t_cnt, 1)
                pe.wait_ge(m.t_hot, 1)
                for q in range(NT * TOPK):
                    last = mm(ps_j[:, 0:JCOLS], hot_p[:, q, :], hot_j[:, q, :], start=(q == 0), stop=(q == NT * TOPK - 1))
                last.then_inc(m.t_tid, 1)
                pe.wait_ge(m.t_je, 1)
                nc.tensor.transpose(ps_j[0:2, P:2 * P], je[:], m.ident[:]).then_inc(m.t_row, 1)

            @block.scalar
            def _(act):
                A = nc.scalar.activation
                act.wait_ge(m.t_mm, 1)
                A(sc[:], ps[:], ACT.Sigmoid).then_inc(m.t_sc, 1)
                act.wait_ge(m.u_g, 1)
                A(sg[:, 0:TS], pg[:, 0, :], ACT.Silu)
                A(sg[:, TS:N], pg[:, 1, 0:TP], ACT.Silu).then_inc(m.u_sg, 1)
                act.wait_ge(m.u_u, 1)
                A(hu[:, 0:TS], pg[:, 0, :], ACT.Identity)
                A(hu[:, TS:N], pg[:, 1, 0:TP], ACT.Identity).then_inc(m.u_hu, 1)
                for n in range(2 * NT):
                    act.wait_ge(m.u_dn, n + 1)
                    A(m.acc[:, n // 2, ts512(n % 2)], pd[:, n % 2, :], ACT.Identity).then_inc(m.u_acc, 1)

            @block.vector
            def _(dve):
                V = nc.vector
                link = Chain(dve, m.t_dve)
                dve.wait_ge(m.t_sc, 1)
                dve.wait_ge(m.t_b, 16)
                link(V.tensor_tensor(sel[:], sc[:], rb[:].unsqueeze(1).to_broadcast([P, NT, E_N]), ALU.add))
                for t in range(NT):
                    for g in range(EGROUPS):
                        last = V.max(m8[:, t, g], sel[:, t, g * GE:(g + 1) * GE])
                link(last)
                link(V.tensor_tensor(grp[:], m8[:, :, :, 0], m8[:, :, :, 1], ALU.add))
                dve.wait_ge(m.t_const, 1)
                for t in range(NT):
                    gj = grp[:, t].unsqueeze(1).to_broadcast([P, EGROUPS, EGROUPS])
                    gi = grp[:, t].unsqueeze(2).to_broadcast([P, EGROUPS, EGROUPS])
                    V.tensor_tensor(gt[:, t], gj, gi, ALU.is_gt)
                    last = V.tensor_tensor(eq[:, t], gj, gi, ALU.is_equal)
                link(last)
                link(V.tensor_tensor(eq[:], eq[:], low[:].unsqueeze(1).to_broadcast([P, NT, EGROUPS, EGROUPS]), ALU.mult))
                link(V.tensor_tensor(gt[:], gt[:], eq[:], ALU.add))
                link(V.tensor_reduce(rank[:], gt[:], AX.X, ALU.add))
                link(V.tensor_scalar(rank[:], rank[:], TOPG - 0.5, None, ALU.is_lt))
                rk = rank[:].unsqueeze(3).to_broadcast([P, NT, EGROUPS, GE])
                s4 = sel[:].rearrange("p t (g e) -> p t g e", g=EGROUPS)
                link(V.tensor_tensor(s4, s4, rk, ALU.mult))
                link(V.tensor_scalar(rank[:], rank[:], -1.0, -NEG, ALU.add, ALU.mult))
                link(V.tensor_tensor(s4, s4, rk, ALU.add))
                for t in range(NT):
                    last = V.max(top[:, t], sel[:, t])
                link(last)
                for t in range(NT):
                    last = V.match_replace(rep[:, t], top[:, t], sel[:, t], 3.0 * NEG)
                link(last)
                V.tensor_scalar(chosen[:], rep[:], 2.0 * NEG, None, ALU.is_lt).then_inc(m.t_ch, 1)
                dve.wait_ge(m.t_ch, 1)
                link(V.tensor_tensor(gates[:], chosen[:], sc[:], ALU.mult))
                link(V.tensor_reduce(sm[:], gates[:], AX.X, ALU.add))
                link(V.reciprocal(sm[:], sm[:]))
                link(V.tensor_scalar(sm[:], sm[:], ROUTED_SCALE, None, ALU.mult))
                V.tensor_tensor(gates[:], gates[:], sm[:].unsqueeze(2).to_broadcast([P, NT, E_N]), ALU.mult)
                dve.wait_ge(m.t_cnt, 1)
                link(V.tensor_scalar(cnt[:], ps_c[:, NT, :], SLOTS / 2 - 0.5, 1.0 / SLOTS, ALU.add, ALU.mult))
                link(V.tensor_scalar(nb[:], cnt[:], ROUND, None, ALU.add))
                link(V.tensor_scalar(nb[:], nb[:], -ROUND, None, ALU.add))
                link(V.tensor_tensor_scan(end[:], ones[:, 0:E_N], nb[:], 0.0, ALU.mult, ALU.add))
                link(V.tensor_tensor(start[:], end[:], nb[:], ALU.subtract))
                link(V.tensor_scalar(start[:], start[:], float(SLOTS), 1.0, ALU.mult, ALU.add))
                link(V.tensor_tensor(slot[:], ps_c[:, 0:NT, :], start[:].unsqueeze(1).to_broadcast([P, NT, E_N]), ALU.add))
                link(V.tensor_tensor(slot[:], slot[:], chosen[:], ALU.mult))
                for t in range(NT):
                    last = V.max(top[:, t], slot[:, t])
                link(last)
                for t in range(NT):
                    last = V.tensor_tensor(pick[:, t], slot[:, t].unsqueeze(1).to_broadcast([P, TOPK, E_N]),
                                           top[:, t].unsqueeze(2).to_broadcast([P, TOPK, E_N]), ALU.is_equal)
                link(V.tensor_scalar(pl[:], top[:], -SLOTS / 2 - 0.5, 1.0 / SLOTS, ALU.add, ALU.mult))
                for t in range(NT):
                    last = V.tensor_tensor(pick[:, t], pick[:, t], gates[:, t].unsqueeze(1).to_broadcast([P, TOPK, E_N]), ALU.mult)
                link(V.tensor_scalar(job[:], pl[:], ROUND, None, ALU.add))
                link(V.tensor_scalar(job[:], job[:], -ROUND, None, ALU.add))
                V.tensor_reduce(m.gj[:], pick[:], AX.X, ALU.add)
                link(V.scalar_tensor_tensor(place[:], job[:], -float(SLOTS), top[:], ALU.mult, ALU.add))
                link(V.tensor_scalar(place[:], place[:], -1.0, None, ALU.add))
                for q in range(NT * TOPK):
                    t, j = q // TOPK, q % TOPK
                    V.tensor_scalar(hot_p[:, q, :], col[:], place[:, t, j:j + 1], None, ALU.is_equal)
                    last = V.tensor_scalar(hot_j[:, q, :], col[:, 0:JCOLS], job[:, t, j:j + 1], tok[:, q:q + 1],
                                           ALU.is_equal, ALU.mult)
                last.then_inc(m.t_hot, 1)
                link(V.tensor_scalar(cnt[:], end[:], tok[:, NT * TOPK:], None, ALU.is_le))
                link(V.tensor_reduce(je[:, 0:1], cnt[:], AX.X, ALU.add))
                link(V.tensor_scalar(je[:, 0:1], je[:, 0:1], E_N - 1.0, None, ALU.min))
                link(V.tensor_scalar(je[:, 1:2], end[:, E_N - 1:E_N], 0.5 - 2.0, 0.5, ALU.add, ALU.mult))
                link(V.tensor_scalar(je[:, 1:2], je[:, 1:2], ROUND, None, ALU.add))
                V.tensor_scalar(je[:, 1:2], je[:, 1:2], -ROUND, None, ALU.add).then_inc(m.t_je, 1)
                dve.wait_ge(m.t_je, 1)
                V.tensor_copy(m.last_pair[:], je[0:1, 1:2])
                dve.wait_ge(m.t_tid, 1)
                dve.wait_ge(m.t_row, 1)
                link(V.tensor_scalar(m.row[:], ps_j[:, 0:JCOLS], -1.0, None, ALU.add))
                V.tensor_single_scalar(m.tid[:], m.row[:], 3, ALU.arith_shift_right)
                V.tensor_copy(m.jobs[:], ps_j[0:1, P:2 * P])


def moe_phase(nc, m, a):
    with ExitStack() as ctx:
        def sb(name, shape, dt=F32):
            return ctx.enter_context(nc.sbuf_tensor(name, shape, dt))
        wg, wu = sb("me_wg", [P, 2, KT, E_F]), sb("me_wu", [P, 2, KT, E_F])
        wd = sb("me_wd", [P, 2, D])
        ids, outs = sb("me_ids", [P, 2], I32), sb("me_outs", [P, 2], I32)
        xg = sb("me_xg", [P, 2, D])
        xT = sb("me_xT", [P, 2, KT, P])
        sg, hh = sb("me_sg", [P, P]), sb("me_hh", [P, P])
        yb = sb("me_yb", [P, 2, D])
        scr = sb("me_scr", [P, 3])
        ps_x = ctx.enter_context(nc.psum_tensor("ps_jx", [P, 2, D], F32))
        ps_g, ps_u = (ctx.enter_context(nc.psum_tensor(x, [P, 512], F32)) for x in ("ps_jg", "ps_ju"))
        ps_d = ctx.enter_context(nc.psum_tensor("ps_jd", [P, D], F32))
        (m.j_w0, m.j_w1, m.j_d0, m.j_d1, m.j_x0, m.j_x1, m.j_ids, m.j_outs, m.j_scr, m.j_turn, m.j_xt, m.j_up, m.j_sg, m.j_hh,
         m.j_dn, m.j_y, m.j_yw0, m.j_yw1) = sems(
            nc, m, "j_w0 j_w1 j_d0 j_d1 j_x0 j_x1 j_ids j_outs j_scr j_turn j_xt j_up j_sg j_hh j_dn j_y j_yw0 j_yw1")
        w_land, d_land, x_land, y_out = [m.j_w0, m.j_w1], [m.j_d0, m.j_d1], [m.j_x0, m.j_x1], [m.j_yw0, m.j_yw1]
        gate_w = a["exp_w_gate"].rearrange("e (p k) f -> e p k f", p=P)
        up_w = a["exp_w_up"].rearrange("e (p k) f -> e p k f", p=P)

        def run(eng, pair, more=0):
            end = eng.value_load(m.last_pair[0:1, 0:1], min_val=0, max_val=PAIRS - 1)
            for i in range(1 + more):
                pair(i)
            with eng.Fori(1 + more, PAIRS + more) as i:
                with eng.If(i < end + (1 + more)):
                    pair(i)
            return end

        with nc.Block() as block:

            @block.sync
            def _(sp):
                def pair(i):
                    for s in range(2):
                        n = i * 2 + s
                        e = sp.value_load(m.jobs[0:1, ds(n, 1)], min_val=0, max_val=E_N - 1)
                        wait(sp, m.j_up, n - 1)
                        sp.dma_start(wg[:, s], gate_w[ds(e, 1)].rearrange("e p k f -> p (e k) f")).then_inc(w_land[s], 16)
                        sp.dma_start(wu[:, s], up_w[ds(e, 1)].rearrange("e p k f -> p (e k) f")).then_inc(w_land[s], 16)
                        wait(sp, m.j_dn, n - 1)
                        sp.dma_start(wd[:, s], a["exp_w_down"][ds(e, 1)].rearrange("e f d -> f (e d)")).then_inc(d_land[s], 16)
                run(sp, pair)

            @block.gpsimd
            def _(pool):
                G = nc.gpsimd

                def absorb(c):
                    G.tensor_tensor(scr[:, c:c + 1], scr[:, 2:3], scr[:, 2:3], ALU.add)

                def gather(s, n):
                    wait(pool, m.j_turn, n - 1)
                    absorb(0)
                    G.tensor_copy(ids[:, s:s + 1], m.tid[:, ds(n, 1)]).then_inc(m.j_ids, 1)
                    pool.wait_ge(m.j_ids, n + 1)
                    absorb(1)
                    G.indirect_dma_start(xg[:, s], None, m.h2_dram, bass.IndirectOffsetOnAxis(ids[:, s:s + 1], axis=0),
                                         bounds_check=N - 1, oob_is_err=False).then_inc(x_land[s], 16)

                def scatter(i, s, n):
                    pool.wait_ge(m.j_y, n + 1)
                    wait(pool, y_out[s], i * 16)
                    absorb(0)
                    G.tensor_copy(outs[:, s:s + 1], m.row[:, ds(n, 1)]).then_inc(m.j_outs, 1)
                    pool.wait_ge(m.j_outs, n + 1)
                    absorb(1)
                    G.indirect_dma_start(m.yj_dram, bass.IndirectOffsetOnAxis(outs[:, s:s + 1], axis=0), yb[:, s], None,
                                         bounds_check=N * TOPK - 1, oob_is_err=False).then_inc(y_out[s], 16)

                def pair(i):
                    gather(0, i * 2)
                    if not (isinstance(i, int) and i < 2):
                        scatter(i - 2, 0, i * 2 - 4)
                    gather(1, i * 2 + 1)
                    if not (isinstance(i, int) and i < 2):
                        scatter(i - 2, 1, i * 2 - 3)
                G.memset(xg[:], 0.0)
                G.memset(scr[:], 0.0).then_inc(m.j_scr, 1)
                pool.wait_ge(m.j_scr, 1)
                end = run(pool, pair, 1)
                for s in range(2):
                    scatter(end, s, end * 2 + s)
                for s in range(2):
                    pool.wait_ge(x_land[s], end * 16 + 32)
                    pool.wait_ge(y_out[s], end * 16 + 16)

            @block.tensor
            def _(pe):
                mm = nc.tensor.matmul

                def turn(i, s, n):
                    pe.wait_ge(x_land[s], i * 16 + 16)
                    wait(pe, m.j_xt, n - 1)
                    for k in range(KT):
                        last = nc.tensor.transpose(ps_x[:, s, k * P:(k + 1) * P], xg[:, s, k:D:KT], m.ident[:])
                    last.then_inc(m.j_turn, 1)

                def up(i, s, n):
                    pe.wait_ge(w_land[s], i * 32 + 32)
                    pe.wait_ge(m.j_xt, n + 1)
                    wait(pe, m.j_hh, n)
                    for o, w in ((ps_g, wg), (ps_u, wu)):
                        for k in range(KT):
                            last = mm(o[:, 0:P], w[:, s, k, :], xT[:, s, k, :], start=(k == 0), stop=(k == KT - 1))
                    last.then_inc(m.j_up, 1)

                def down(i, s, n):
                    pe.wait_ge(d_land[s], i * 16 + 16)
                    pe.wait_ge(m.j_hh, n + 1)
                    wait(pe, m.j_y, n)
                    for h in range(2):
                        last = mm(ps_d[:, ts512(h)], hh[:], wd[:, s, ts512(h)], start=True, stop=True)
                    last.then_inc(m.j_dn, 1)

                def pair(i):
                    n = i * 2
                    turn(i, 1, n + 1)
                    up(i, 0, n)
                    if not (isinstance(i, int) and i == 0):
                        down(i - 1, 1, n - 1)
                    turn(i + 1, 0, n + 2)
                    up(i, 1, n + 1)
                    down(i, 0, n)
                turn(0, 0, 0)
                end = run(pe, pair)
                down(end, 1, end * 2 + 1)

            @block.scalar
            def _(act):
                def turned(s, n):
                    act.wait_ge(m.j_turn, n + 1)
                    wait(act, m.j_up, n - 1)
                    nc.scalar.activation(xT[:, s], ps_x[:, s].rearrange("p (k c) -> p k c", k=KT), ACT.Identity).then_inc(m.j_xt, 1)

                def silu(n):
                    act.wait_ge(m.j_up, n + 1)
                    wait(act, m.j_hh, n)
                    nc.scalar.activation(sg[:], ps_g[:, 0:P], ACT.Silu).then_inc(m.j_sg, 1)

                def pair(i):
                    n = i * 2
                    turned(1, n + 1)
                    silu(n)
                    turned(0, n + 2)
                    silu(n + 1)
                turned(0, 0)
                run(act, pair)

            @block.vector
            def _(dve):
                V = nc.vector

                def mul(n):
                    dve.wait_ge(m.j_sg, n + 1)
                    wait(dve, m.j_dn, n)
                    V.tensor_tensor(hh[:], sg[:], ps_u[:, 0:P], ALU.mult).then_inc(m.j_hh, 1)

                def rows(i, s, n):
                    dve.wait_ge(m.j_dn, n + 1)
                    wait(dve, y_out[s], i * 16)
                    V.tensor_copy(yb[:, s], ps_d[:]).then_inc(m.j_y, 1)

                def pair(i):
                    n = i * 2
                    mul(n)
                    if not (isinstance(i, int) and i == 0):
                        rows(i - 1, 1, n - 1)
                    mul(n + 1)
                    rows(i, 0, n)
                end = run(dve, pair)
                rows(end, 1, end * 2 + 1)


def combine_phase(nc, m, a):
    with ExitStack() as ctx:
        def sb(name, shape, dt=F32):
            return ctx.enter_context(nc.sbuf_tensor(name, shape, dt))
        NR, HALF = 4, TOPK // 2
        rows = sb("cb_rows", [P, NR, HALF, D])
        g2 = sb("cb_g2", [P, 2, D])
        lng, lnb = sb("cb_lng", [P, D]), sb("cb_lnb", [P, D])
        st = sb("cb_st", [P, NT, 2, 6])
        mv = sb("cb_mv", [P, NT, 4])
        m.e_land = sems(nc, m, " ".join(f"e_land{r}" for r in range(NR)))
        (m.e_used, m.e_g, m.e_dve, m.e_sqv, m.e_sq, m.e_nrm, m.e_pl, m.e_ln, m.e_out) = sems(
            nc, m, "e_used e_g e_dve e_sqv e_sq e_nrm e_pl e_ln e_out")
        with nc.Block() as block:

            @block.sync
            def _(sp):
                y_tok = m.yj_dram.rearrange("(t p j) d -> t p j d", p=P, j=TOPK)
                for q in range(2 * NT):
                    if q >= NR:
                        sp.wait_ge(m.e_used, (q - NR + 1) * HALF)
                    sp.dma_start(rows[:, q % NR], y_tok[q // 2, :, (q % 2) * HALF:(q % 2 + 1) * HALF, :]).then_inc(m.e_land[q % NR], 16)

            @block.gpsimd
            def _(pool):
                for t in range(NT):
                    x = m.acc[:, t]
                    pool.wait_ge(m.e_nrm, t + 1)
                    nc.gpsimd.tensor_tensor(x, x, lng[:], ALU.mult).then_inc(m.e_pl, 1)
                    pool.wait_ge(m.e_pl, t + 1)
                    nc.gpsimd.tensor_tensor(x, x, lnb[:], ALU.add).then_inc(m.e_ln, 1)
                    pool.wait_ge(m.e_ln, t + 1)
                    o = a["y_prompt"] if t == NT - 1 else a["y_sample"][t * P:(t + 1) * P, :]
                    pool.dma_start(o, m.acc[:, t]).then_inc(m.e_out, 16)
                pool.wait_ge(m.e_out, 16 * NT)

            @block.scalar
            def _(act):
                for c in range(2):
                    act.dma_start(g2[:, c], m.mods_dram[c, GATE2 * D:(GATE2 + 1) * D].partition_broadcast(P)).then_inc(m.e_g, 16)
                act.dma_start(lng[:], a["ln2_g"].partition_broadcast(P)).then_inc(m.e_g, 16)
                act.dma_start(lnb[:], a["ln2_b"].partition_broadcast(P)).then_inc(m.e_g, 16)
                for t in range(NT):
                    act.wait_ge(m.e_sqv, t + 1)
                    nc.scalar.activation(mv[:, t, 3:4], mv[:, t, 2:3], ACT.Sqrt).then_inc(m.e_sq, 1)

            @block.vector
            def _(dve):
                V = nc.vector
                link = Chain(dve, m.e_dve)
                for t in range(NT):
                    x, c = m.acc[:, t], t // (NT - 1)
                    for j in range(TOPK):
                        q = t * TOPK + j
                        b = q // HALF
                        dve.wait_ge(m.e_land[b % NR], 16 * (b // NR + 1))
                        if j:
                            dve.wait_ge(m.e_used, q)
                        V.scalar_tensor_tensor(x, rows[:, b % NR, j % HALF], m.gj[:, t, j:j + 1], x, ALU.mult, ALU.add).then_inc(m.e_used, 1)
                    dve.wait_ge(m.e_used, (t + 1) * TOPK)
                    if t == 0:
                        dve.wait_ge(m.e_g, 64)
                    link(V.tensor_tensor(x, x, g2[:, c], ALU.mult))
                    link(V.scalar_tensor_tensor(x, m.x1[:, t], ALPHA, x, ALU.mult, ALU.add))
                    norm_stats(V, dve, link, m, x, st[:, t], mv[:, t], m.e_sqv, m.e_sq, t)
                    V.tensor_scalar(x, x, mv[:, t, 0:1], mv[:, t, 3:4], ALU.subtract, ALU.mult).then_inc(m.e_nrm, 1)


STOP_AFTER = None


def build(nc, a):
    m = Mem()
    a["w_in_t"] = a["w_in"].rearrange("(k p) n -> p k n", p=P)
    m.mods_dram = nc.dram_tensor("mods_dram", [2, 6 * D], F32).ap()
    m.h1_dram = nc.dram_tensor("h1_dram", [KT, P, N], F32).ap()
    m.h2_dram = nc.dram_tensor("h2_dram", [N, D], F32).ap()
    m.yj_dram = nc.dram_tensor("yj_dram", [N * TOPK, D], F32).ap()
    m.y_dram = nc.dram_tensor("y_dram", [3, P, MT, N], F32).ap()
    with ExitStack() as ctx:
        m.phase_sems = []
        def sb(stack, name, shape):
            return stack.enter_context(nc.sbuf_tensor(name, shape, F32))

        m.ident = sb(ctx, "ident", [P, P])
        m.pcol = sb(ctx, "pcol", [P, NPCOL])
        m.modT = sb(ctx, "modT", [P, 2, KT, 2])
        m.c_silu = sb(ctx, "c_silu", [P, KT, 2])
        m.s_win = [ctx.enter_context(nc.semaphore(f"s_win{r}")) for r in range(4)]
        with ExitStack() as mixer:
            m.zr = sb(mixer, "zr", [P, RT, ZW])
            with ExitStack() as branches:
                m.yb = sb(branches, "yb", [P, MT, N])
                m.yc = sb(branches, "yc", [P, MT, N])
                with ExitStack() as mid:
                    m.z = sb(mid, "z", [P, 3 * MT, ZW])
                    m.zv = sb(mid, "zv", [P, NT, MIX])
                    with ExitStack() as front:
                        m.hT = sb(front, "hT", [P, KT, N])
                        m.w_ada_sb = sb(front, "w_ada_sb", [P, 2, KT, 512])
                        m.w_in_sb = sb(front, "w_in_sb", [P, 4, KT, P])
                        m.mods = sb(front, "mods", [2, 6 * D])
                        setup_phase(nc, m, a)
                        inproj_phase(nc, m, a)
                    if STOP_AFTER == "inproj":
                        return
                    clear_sems(nc, m)
                    attention_phase(nc, m, a)
                    if STOP_AFTER == "attention":
                        return
                clear_sems(nc, m)
                s5_phase(nc, m, a)
                if STOP_AFTER == "s5":
                    return
            clear_sems(nc, m)
            rwkv_phase(nc, m, a)
            if STOP_AFTER == "rwkv":
                return
        with ExitStack() as tail:
            m.x1 = sb(tail, "x1", [P, NT, D])
            m.mT = sb(tail, "mT", [P, D // P, N])
            clear_sems(nc, m)
            merge_phase(nc, m, a)
            m.h2T = sb(tail, "h2T", [P, KT, N])
            m.acc = sb(tail, "acc", [P, NT, D])
            m.gj = sb(tail, "gj", [P, NT, TOPK])
            m.row, m.tid = (tail.enter_context(nc.sbuf_tensor(x, [P, JCOLS], I32)) for x in ("row", "tid"))
            m.jobs, m.last_pair = (tail.enter_context(nc.sbuf_tensor(x, [1, w], I32)) for x, w in (("jobs", P), ("last_pair", 1)))
            clear_sems(nc, m)
            residual_phase(nc, m, a)
            if STOP_AFTER == "merge":
                return
            clear_sems(nc, m)
            router_phase(nc, m, a)
            if STOP_AFTER == "router":
                return
            clear_sems(nc, m)
            moe_phase(nc, m, a)
            if STOP_AFTER == "moe":
                return
            clear_sems(nc, m)
            combine_phase(nc, m, a)


_INS = {
    "x_prompt": (TP, D), "x_sample": (TS, D), "c": (1, D), "cache_na_k": (HEADS, 128, HD),
    "cache_na_v": (HEADS, 128, HD), "state_rwkv": (2, HEADS, HD, HD), "state_s5_re": (2, 32, 64),
    "state_s5_im": (2, 32, 64), "c_ctx": (D,), "w_ada": (D, 6 * D), "b_ada": (6 * D,), "w_in": (D, GCOL + 3 * D),
    "rwkv_mu": (ACOLS,), "rwkv_w0": (2, MIX), "rwkv_w2": (128, MIX), "rwkv_a0": (2, MIX), "rwkv_a2": (128, MIX),
    "rwkv_g2": (128, MIX), "rwkv_kk": (MIX,), "rwkv_ka": (MIX,), "rwkv_rk": (MIX,), "rwkv_gn_g": (MIX,),
    "rwkv_gn_b": (MIX,), "na_rpb": (HEADS * NDR, NDC), "s5_a_re": (2, 32, 64), "s5_a_im": (2, 32, 64),
    "s5_log_dt": (2, 32), "s5_b_re": (32, 64, 16), "s5_b_im": (32, 64, 16), "s5_c_re": (32, 16, 64),
    "s5_c_im": (32, 16, 64), "s5_d": (MIX,), "s5_w_glu": (MIX, MIX), "s5_b_glu": (MIX,), "w_branch": (3, MIX, D),
    "w_out": (D, D), "ln1_g": (D,), "ln1_b": (D,), "router_w": (D, E_N), "router_bias": (E_N,),
    "exp_w_gate": (E_N, D, E_F), "exp_w_up": (E_N, D, E_F), "exp_w_down": (E_N, E_F, D), "sh_w_gate": (D, E_F),
    "sh_w_up": (D, E_F), "sh_w_down": (E_F, D), "ln2_g": (D,), "ln2_b": (D,),
}
_OUTS = {"y_prompt": (TP, D), "y_sample": (TS, D), "new_k": (HEADS, TP, HD), "new_v": (HEADS, TP, HD),
         "new_rwkv": (2, HEADS, HD, HD), "new_s5_re": (2, 32, 64), "new_s5_im": (2, 32, 64)}
_RETURNED = {"y_prompt": (1, TP, D), "y_sample": (1, TS, D), "new_k": (1, 1, HEADS, TP, HD),
             "new_v": (1, 1, HEADS, TP, HD), "new_rwkv": (1, 1, 2, HEADS, HD, HD), "new_s5_re": (1, 1, 2, 32, 64),
             "new_s5_im": (1, 1, 2, 32, 64)}


def kernel(**inputs):
    import numpy as np
    import concourse.bacc as bacc
    from concourse.bass_utils import run_bass_kernel_spmd

    nc = bacc.Bacc("TRN2", target_bir_lowering=False, num_devices=1)
    arrays, a = {}, {}
    for name, shape in _INS.items():
        arrays["in_" + name] = np.ascontiguousarray(inputs[name]).reshape(shape)
        a[name] = nc.dram_tensor("in_" + name, shape, F32, kind="ExternalInput").ap()
    for name, shape in _OUTS.items():
        a[name] = nc.dram_tensor("out_" + name, shape, F32, kind="ExternalOutput").ap()
    build(nc, a)
    r = run_bass_kernel_spmd(nc, [arrays], core_ids=[0])
    return tuple(np.asarray(r.results[0]["out_" + name]).reshape(_RETURNED[name]) for name in _OUTS)
```
